# Optimizing a Trainium2 kernel written in Bass

```python
import jax
import jax.numpy as jnp
from jax import lax
import numpy as np

D_MODEL = 1024
BATCH = 1
SEQ = 256
DEPTH = 2
DEC_BATCH = 1
DEC_SEQ = 64
PAST_LEN = 512

CHUNK = 64
SUB_CHUNK = 16
N_SUB = CHUNK // SUB_CHUNK
N_EVEN = (DEPTH + 1) // 2
N_ODD = DEPTH // 2

RWKV_HEADS = 8
RWKV_HEAD_DIM = 64
RWKV_DIM = RWKV_HEADS * RWKV_HEAD_DIM
DECAY_LORA = 64
AAA_LORA = 64
GATE_LORA = 128
RWKV_PROJ = 3 * RWKV_DIM + DECAY_LORA + AAA_LORA + GATE_LORA
RWKV_SPLITS = (RWKV_DIM, 2 * RWKV_DIM, 3 * RWKV_DIM, 3 * RWKV_DIM + DECAY_LORA, 3 * RWKV_DIM + DECAY_LORA + AAA_LORA)
RWKV_GN_EPS = RWKV_HEAD_DIM * 1e-5
DECAY_SCALE = 0.6065306597126334

GLA_HEADS = 4
GLA_DK = 64
GLA_DV = 128
GLA_KDIM = GLA_HEADS * GLA_DK
GLA_VDIM = GLA_HEADS * GLA_DV
GLA_GATE_RANK = 16
GLA_TAU = 16.0
GLA_PROJ = 2 * GLA_KDIM + GLA_VDIM + GLA_GATE_RANK + GLA_VDIM
GLA_SPLITS = (GLA_KDIM, 2 * GLA_KDIM, 2 * GLA_KDIM + GLA_VDIM, 2 * GLA_KDIM + GLA_VDIM + GLA_GATE_RANK)

P_AB = RWKV_PROJ + GLA_PROJ
MIX_AB = RWKV_DIM + GLA_VDIM

HGRN_HEADS = 8
HGRN_HEAD_DIM = 128
HGRN_DIM = HGRN_HEADS * HGRN_HEAD_DIM
P_C = 4 * HGRN_DIM

D_FF = 2816
N_EXPERTS = 8
TOP_K = 2
EXPERT_D_FF = 2816
MOE_BLOCK = 128

ALPHA = (2 * DEPTH) ** 0.25
BETA = (8 * DEPTH) ** -0.25
NORM_EPS = 1e-5

kernel_name = 'hybrid_rwkv7_gla_hgrn2_moe_stream_step'

def layer_norm(x, g, b):
    x32 = x.astype(jnp.float32)
    xc = x32 - jnp.mean(x32, -1, keepdims=True)
    var = jnp.mean(xc * xc, -1, keepdims=True)
    return (xc * lax.rsqrt(var + NORM_EPS) * g + b).astype(x.dtype)

def rms_norm(x, w):
    x = x.astype(jnp.float32)
    return x * lax.rsqrt(jnp.mean(x * x, -1, keepdims=True) + NORM_EPS) * w

def swiglu(h, w1, w3, w2):
    return (jax.nn.silu(h @ w1) * (h @ w3)) @ w2

def chunk_gated_linear_attention(q, k, v, log_a, s0):
    bsz, t_len, n_h, dk = q.shape
    dv = v.shape[-1]
    n_chunks = -(-t_len // CHUNK)
    pad = n_chunks * CHUNK - t_len

    def to_chunks(a):
        a = jnp.pad(a.astype(jnp.float32), ((0, 0), (0, pad), (0, 0), (0, 0)))
        return a.reshape(bsz, n_chunks, CHUNK, n_h, a.shape[-1]).transpose(1, 0, 3, 2, 4)

    cross_mask = jnp.asarray((np.arange(CHUNK)[None, :] // SUB_CHUNK) < np.arange(N_SUB)[:, None])
    sub_causal = jnp.asarray(np.tril(np.ones((SUB_CHUNK, SUB_CHUNK), dtype=bool)))

    def body(s, blk):
        qc, kc, vc, gc = blk
        b = jnp.cumsum(gc, axis=2)
        o = jnp.einsum('bhld,bhdv->bhlv', qc * jnp.exp(b), s)
        qs = qc.reshape(bsz, n_h, N_SUB, SUB_CHUNK, dk)
        ks = kc.reshape(bsz, n_h, N_SUB, SUB_CHUNK, dk)
        vs = vc.reshape(bsz, n_h, N_SUB, SUB_CHUNK, dv)
        bs = b.reshape(bsz, n_h, N_SUB, SUB_CHUNK, dk)
        e = jnp.concatenate([jnp.zeros_like(bs[:, :, :1, 0]), bs[:, :, :-1, -1]], axis=2)
        qg = qs * jnp.exp(bs - e[:, :, :, None])
        kg = kc[:, :, None] * jnp.exp(jnp.minimum(e[:, :, :, None] - b[:, :, None], 0.0))
        sc = jnp.where(cross_mask[:, None, :], jnp.einsum('bhixd,bhisd->bhixs', qg, kg), 0.0)
        o_cross = jnp.einsum('bhixs,bhsv->bhixv', sc, vc)
        dec = jnp.where(sub_causal[:, :, None],
                        jnp.exp(jnp.minimum(bs[..., :, None, :] - bs[..., None, :, :], 0.0)), 0.0)
        sw = jnp.sum(qs[..., :, None, :] * ks[..., None, :, :] * dec, axis=-1)
        o_in = jnp.einsum('bhits,bhisv->bhitv', sw, vs)
        o = o + (o_cross + o_in).reshape(bsz, n_h, CHUNK, dv)
        b_last = b[:, :, -1]
        s = s * jnp.exp(b_last)[..., None] + jnp.einsum('bhld,bhlv->bhdv', kc * jnp.exp(b_last[:, :, None] - b), vc)
        return s, o

    s, o = lax.scan(body, s0.astype(jnp.float32), (to_chunks(q), to_chunks(k), to_chunks(v), to_chunks(log_a)))
    o = o.transpose(1, 0, 3, 2, 4).reshape(bsz, n_chunks * CHUNK, n_h, dv)[:, :t_len]
    return o, s

def rwkv7_recurrence(r, w, k, v, kk, a, s0):
    def step(s, inp):
        r_t, w_t, k_t, v_t, kk_t, a_t = inp
        sa = jnp.einsum('bhvk,bhk->bhv', s, kk_t)
        s = (s * w_t[:, :, None, :] - sa[..., None] * (kk_t * a_t)[:, :, None, :]
             + v_t[..., None] * k_t[:, :, None, :])
        return s, jnp.einsum('bhvk,bhk->bhv', s, r_t)
    seq = tuple(jnp.moveaxis(t, 1, 0) for t in (r, w, k, v, kk, a))
    s, o = lax.scan(step, s0.astype(jnp.float32), seq)
    return jnp.moveaxis(o, 0, 1), s

def mix_rwkv_gla(h, j, p, shift_prev, s_rwkv, s_gla):
    f32 = jnp.float32
    bsz, t_len, _ = h.shape
    proj = h @ p['w_in_ab'][j]
    pr, pg = proj[..., :RWKV_PROJ], proj[..., RWKV_PROJ:]
    prev = jnp.concatenate([shift_prev[:, None].astype(pr.dtype), pr[:, :-1]], axis=1)
    xs = (pr + (prev - pr) * p['rwkv_mu'][j]).astype(f32)
    r, k, v, wd, ad, gd = jnp.split(xs, list(RWKV_SPLITS), axis=-1)
    hd = (bsz, t_len, RWKV_HEADS, RWKV_HEAD_DIM)
    w = jnp.exp(-DECAY_SCALE * jax.nn.sigmoid(p['rwkv_w0'][j] + jnp.tanh(wd) @ p['rwkv_w_up'][j])).reshape(hd)
    a = jax.nn.sigmoid(p['rwkv_a0'][j] + ad @ p['rwkv_a_up'][j]).reshape(hd)
    g = jax.nn.sigmoid(gd) @ p['rwkv_g_up'][j]
    r, k, v = r.reshape(hd), k.reshape(hd), v.reshape(hd)
    kk = k * p['rwkv_k_k'][j].reshape(RWKV_HEADS, RWKV_HEAD_DIM)
    kk = kk / jnp.maximum(jnp.sqrt(jnp.sum(kk * kk, -1, keepdims=True)), 1e-12)
    k = k * (1.0 + (a - 1.0) * p['rwkv_k_a'][j].reshape(RWKV_HEADS, RWKV_HEAD_DIM))
    o, s_rwkv = rwkv7_recurrence(r, w, k, v, kk, a, s_rwkv)
    mu_o = jnp.mean(o, -1, keepdims=True)
    var_o = jnp.mean(jnp.square(o - mu_o), -1, keepdims=True)
    o = ((o - mu_o) * lax.rsqrt(var_o + RWKV_GN_EPS)).reshape(bsz, t_len, RWKV_DIM) * p['rwkv_gn_w'][j] + p['rwkv_gn_b'][j]
    bonus = jnp.sum(r * k * p['rwkv_r_k'][j], -1, keepdims=True) * v
    o_rwkv = (o + bonus.reshape(bsz, t_len, RWKV_DIM)) * g
    q, kg, vg, gz, og = jnp.split(pg.astype(f32), list(GLA_SPLITS), axis=-1)
    log_a = jax.nn.log_sigmoid(gz @ p['gla_gate_up'][j] + p['gla_gate_b'][j]) / GLA_TAU
    kd = (bsz, t_len, GLA_HEADS, GLA_DK)
    o_g, s_gla = chunk_gated_linear_attention(q.reshape(kd) * GLA_DK ** -0.5, kg.reshape(kd),
                                              vg.reshape(bsz, t_len, GLA_HEADS, GLA_DV), log_a.reshape(kd), s_gla)
    o_g = rms_norm(o_g, p['gla_norm_w'][j]).reshape(bsz, t_len, GLA_VDIM) * jax.nn.silu(og)
    out = jnp.concatenate([o_rwkv, o_g], axis=-1).astype(h.dtype) @ p['w_out_ab'][j]
    return out, pr[:, -1], s_rwkv, s_gla

def mix_hgrn2(h, j, lb, p, s0):
    f32 = jnp.float32
    bsz, t_len, _ = h.shape
    proj = (h @ p['w_in_c'][j]).astype(f32)
    q, f, i, g = jnp.split(proj, 4, axis=-1)
    lb = lb.astype(f32)
    log_f = jnp.logaddexp(jnp.log(lb), jnp.log1p(-lb) + jax.nn.log_sigmoid(f))
    k = (1.0 - lb) * jax.nn.sigmoid(-f)
    hd = (bsz, t_len, HGRN_HEADS, HGRN_HEAD_DIM)
    o, s = chunk_gated_linear_attention(jax.nn.silu(q).reshape(hd), k.reshape(hd), i.reshape(hd), log_f.reshape(hd), s0)
    o = rms_norm(o, p['hgrn_norm_w'][j]).reshape(bsz, t_len, HGRN_DIM) * jax.nn.silu(g)
    return o.astype(h.dtype) @ p['w_out_c'][j], s

def moe_swiglu(h, router, w1, w3, w2):
    f32 = jnp.float32
    bsz, t_len, d = h.shape
    x = h.reshape(-1, d)
    n_tok = x.shape[0]
    probs = jax.nn.softmax((x @ router).astype(f32), axis=-1)
    top_p, top_e = lax.top_k(probs, TOP_K)
    top_p = top_p / jnp.sum(top_p, -1, keepdims=True)
    n_slots = n_tok * TOP_K
    flat_e = top_e.reshape(-1)
    order = jnp.argsort(flat_e)
    sorted_e = flat_e[order]
    counts = jnp.bincount(flat_e, length=N_EXPERTS)
    padded = (counts + MOE_BLOCK - 1) // MOE_BLOCK * MOE_BLOCK
    group_start = jnp.cumsum(counts) - counts
    padded_end = jnp.cumsum(padded)
    padded_start = padded_end - padded
    dest = padded_start[sorted_e] + jnp.arange(n_slots) - group_start[sorted_e]
    n_blocks = -(-n_slots // MOE_BLOCK) + N_EXPERTS
    slot_token = order // TOP_K
    row_token = jnp.zeros((n_blocks * MOE_BLOCK,), jnp.int32).at[dest].set(slot_token.astype(jnp.int32))
    block_expert = jnp.minimum(jnp.searchsorted(padded_end, jnp.arange(n_blocks) * MOE_BLOCK, side='right'),
                               N_EXPERTS - 1)

    def expert_block(args):
        xb, e = args
        return (jax.nn.silu(xb @ w1[e]) * (xb @ w3[e])) @ w2[e]

    y_rows = lax.map(expert_block, (x[row_token].reshape(n_blocks, MOE_BLOCK, d), block_expert))
    y_slots = y_rows.reshape(-1, d)[dest].astype(f32) * top_p.reshape(-1)[order][:, None]
    y = jnp.zeros((n_tok, d), f32).at[slot_token].add(y_slots)
    return y.astype(h.dtype).reshape(bsz, t_len, d)

def run_trunk(x, s_rwkv, s_shift, s_gla, s_hgrn, lower_bounds, p):
    new_rwkv, new_shift, new_gla, new_hgrn = [], [], [], []
    for layer in range(DEPTH):
        j = layer // 2
        if layer % 2 == 0:
            out, sh, sr, sg = mix_rwkv_gla(x, j, p, s_shift[j], s_rwkv[j], s_gla[j])
            x = layer_norm(ALPHA * x + out, p['ln_ab_g'][j], p['ln_ab_b'][j])
            ffn = swiglu(x, p['ffn_w1'][j], p['ffn_w3'][j], p['ffn_w2'][j])
            x = layer_norm(ALPHA * x + ffn, p['ln_ffn_g'][j], p['ln_ffn_b'][j])
            new_rwkv.append(sr)
            new_shift.append(sh)
            new_gla.append(sg)
        else:
            out, sc = mix_hgrn2(x, j, lower_bounds[layer], p, s_hgrn[j])
            x = layer_norm(ALPHA * x + out, p['ln_c_g'][j], p['ln_c_b'][j])
            moe = moe_swiglu(x, p['moe_router'][j], p['moe_w1'][j], p['moe_w3'][j], p['moe_w2'][j])
            x = layer_norm(ALPHA * x + moe, p['ln_moe_g'][j], p['ln_moe_b'][j])
            new_hgrn.append(sc)
    return x, jnp.stack(new_rwkv), jnp.stack(new_shift), jnp.stack(new_gla), jnp.stack(new_hgrn)

def setup_inputs(seed: int = 0) -> dict:
    key = jax.random.key(seed)
    ks = iter(jax.random.split(key, 64))

    def nrm(shape, scale):
        return jax.random.normal(next(ks), shape, jnp.float32) * scale

    def gain(shape):
        return 1.0 + nrm(shape, 0.05)

    ne, no, ex = N_EVEN, N_ODD, N_EXPERTS
    return {
        'x_prompt': nrm((BATCH, SEQ, D_MODEL), 1.0),
        'x_sample': nrm((DEC_BATCH, DEC_SEQ, D_MODEL), 1.0),
        'state_rwkv': nrm((ne, DEC_BATCH, RWKV_HEADS, RWKV_HEAD_DIM, RWKV_HEAD_DIM), 0.3),
        'cache_rwkv_shift': nrm((ne, DEC_BATCH, RWKV_PROJ), 1.0),
        'state_gla': nrm((ne, DEC_BATCH, GLA_HEADS, GLA_DK, GLA_DV), 0.3),
        'state_hgrn': nrm((no, DEC_BATCH, HGRN_HEADS, HGRN_HEAD_DIM, HGRN_HEAD_DIM), 0.3),
        'w_in_ab': nrm((ne, D_MODEL, P_AB), D_MODEL ** -0.5),
        'rwkv_mu': jax.random.uniform(next(ks), (ne, RWKV_PROJ), jnp.float32),
        'rwkv_w0': nrm((ne, RWKV_DIM), 0.5),
        'rwkv_w_up': nrm((ne, DECAY_LORA, RWKV_DIM), 0.5 * DECAY_LORA ** -0.5),
        'rwkv_a0': nrm((ne, RWKV_DIM), 0.5),
        'rwkv_a_up': nrm((ne, AAA_LORA, RWKV_DIM), AAA_LORA ** -0.5),
        'rwkv_g_up': nrm((ne, GATE_LORA, RWKV_DIM), GATE_LORA ** -0.5),
        'rwkv_k_k': 0.85 + nrm((ne, RWKV_DIM), 0.05),
        'rwkv_k_a': gain((ne, RWKV_DIM)),
        'rwkv_r_k': nrm((ne, RWKV_HEADS, RWKV_HEAD_DIM), 0.1),
        'rwkv_gn_w': gain((ne, RWKV_DIM)),
        'rwkv_gn_b': nrm((ne, RWKV_DIM), 0.02),
        'gla_gate_up': nrm((ne, GLA_GATE_RANK, GLA_KDIM), GLA_GATE_RANK ** -0.5),
        'gla_gate_b': nrm((ne, GLA_KDIM), 0.1),
        'gla_norm_w': gain((ne, GLA_DV)),
        'w_out_ab': nrm((ne, MIX_AB, D_MODEL), BETA * MIX_AB ** -0.5),
        'ln_ab_g': gain((ne, D_MODEL)),
        'ln_ab_b': nrm((ne, D_MODEL), 0.02),
        'ffn_w1': nrm((ne, D_MODEL, D_FF), D_MODEL ** -0.5),
        'ffn_w3': nrm((ne, D_MODEL, D_FF), D_MODEL ** -0.5),
        'ffn_w2': nrm((ne, D_FF, D_MODEL), BETA * D_FF ** -0.5),
        'ln_ffn_g': gain((ne, D_MODEL)),
        'ln_ffn_b': nrm((ne, D_MODEL), 0.02),
        'w_in_c': nrm((no, D_MODEL, P_C), D_MODEL ** -0.5),
        'hgrn_lb': nrm((DEPTH, HGRN_DIM), 0.5),
        'hgrn_norm_w': gain((no, HGRN_HEAD_DIM)),
        'w_out_c': nrm((no, HGRN_DIM, D_MODEL), BETA * HGRN_DIM ** -0.5),
        'ln_c_g': gain((no, D_MODEL)),
        'ln_c_b': nrm((no, D_MODEL), 0.02),
        'moe_router': nrm((no, D_MODEL, ex), D_MODEL ** -0.5),
        'moe_w1': nrm((no, ex, D_MODEL, EXPERT_D_FF), D_MODEL ** -0.5),
        'moe_w3': nrm((no, ex, D_MODEL, EXPERT_D_FF), D_MODEL ** -0.5),
        'moe_w2': nrm((no, ex, EXPERT_D_FF, D_MODEL), BETA * EXPERT_D_FF ** -0.5),
        'ln_moe_g': gain((no, D_MODEL)),
        'ln_moe_b': nrm((no, D_MODEL), 0.02),
    }

def reference(x_prompt, x_sample, state_rwkv, cache_rwkv_shift, state_gla, state_hgrn,
              w_in_ab, rwkv_mu, rwkv_w0, rwkv_w_up, rwkv_a0, rwkv_a_up, rwkv_g_up, rwkv_k_k, rwkv_k_a,
              rwkv_r_k, rwkv_gn_w, rwkv_gn_b, gla_gate_up, gla_gate_b, gla_norm_w, w_out_ab, ln_ab_g, ln_ab_b,
              ffn_w1, ffn_w3, ffn_w2, ln_ffn_g, ln_ffn_b,
              w_in_c, hgrn_lb, hgrn_norm_w, w_out_c, ln_c_g, ln_c_b,
              moe_router, moe_w1, moe_w3, moe_w2, ln_moe_g, ln_moe_b):
    p = {
        'w_in_ab': w_in_ab, 'rwkv_mu': rwkv_mu, 'rwkv_w0': rwkv_w0, 'rwkv_w_up': rwkv_w_up,
        'rwkv_a0': rwkv_a0, 'rwkv_a_up': rwkv_a_up, 'rwkv_g_up': rwkv_g_up, 'rwkv_k_k': rwkv_k_k,
        'rwkv_k_a': rwkv_k_a, 'rwkv_r_k': rwkv_r_k, 'rwkv_gn_w': rwkv_gn_w, 'rwkv_gn_b': rwkv_gn_b,
        'gla_gate_up': gla_gate_up, 'gla_gate_b': gla_gate_b, 'gla_norm_w': gla_norm_w, 'w_out_ab': w_out_ab,
        'ln_ab_g': ln_ab_g, 'ln_ab_b': ln_ab_b, 'ffn_w1': ffn_w1, 'ffn_w3': ffn_w3, 'ffn_w2': ffn_w2,
        'ln_ffn_g': ln_ffn_g, 'ln_ffn_b': ln_ffn_b, 'w_in_c': w_in_c, 'hgrn_norm_w': hgrn_norm_w,
        'w_out_c': w_out_c, 'ln_c_g': ln_c_g, 'ln_c_b': ln_c_b, 'moe_router': moe_router,
        'moe_w1': moe_w1, 'moe_w3': moe_w3, 'moe_w2': moe_w2, 'ln_moe_g': ln_moe_g, 'ln_moe_b': ln_moe_b,
    }
    s = jax.nn.softmax(hgrn_lb.astype(jnp.float32), axis=0)
    lower_bounds = jnp.cumsum(s, axis=0) - s[0]
    nb = x_prompt.shape[0]
    f32 = jnp.float32
    y_prompt, p_rwkv, p_shift, p_gla, p_hgrn = run_trunk(
        x_prompt,
        jnp.zeros((N_EVEN, nb, RWKV_HEADS, RWKV_HEAD_DIM, RWKV_HEAD_DIM), f32),
        jnp.zeros((N_EVEN, nb, RWKV_PROJ), x_prompt.dtype),
        jnp.zeros((N_EVEN, nb, GLA_HEADS, GLA_DK, GLA_DV), f32),
        jnp.zeros((N_ODD, nb, HGRN_HEADS, HGRN_HEAD_DIM, HGRN_HEAD_DIM), f32),
        lower_bounds, p)
    y_sample, d_rwkv, d_shift, d_gla, d_hgrn = run_trunk(
        x_sample, state_rwkv, cache_rwkv_shift, state_gla, state_hgrn, lower_bounds, p)
    return (y_prompt, y_sample, p_rwkv, p_shift, p_gla, p_hgrn, d_rwkv, d_shift, d_gla, d_hgrn)


_drawn_inputs = setup_inputs


def setup_inputs(seed=0):
    import zlib

    import numpy as np

    out = dict(_drawn_inputs(seed))
    spreads = {}
    factors = {'state_rwkv': 2.688,
     'state_gla': 3.637,
     'state_hgrn': 5.059,
     'rwkv_k_k': 3.762,
     'rwkv_gn_w': 2.861,
     'rwkv_gn_b': 8.0,
     'gla_norm_w': 4.608,
     'hgrn_norm_w': 2.759}
    for name, (base, spread) in spreads.items():
        noise = np.random.default_rng([zlib.crc32(name.encode()), seed]).standard_normal(out[name].shape)
        drawn = base * np.exp(spread * noise) if base else spread * noise
        out[name] = jnp.asarray(drawn.astype(out[name].dtype))
    for name, factor in factors.items():
        out[name] = (out[name] * factor).astype(out[name].dtype)
    return out
```

```python
import numpy as np
from contextlib import ExitStack

import concourse.bass as bass
from concourse import mybir

F32 = mybir.dt.float32
F32R = mybir.dt.float32r
I32 = mybir.dt.int32
ALU = mybir.AluOpType
ACT = mybir.ActivationFunctionType
AX = mybir.AxisListType

P = 128
D = 1024
KC = D // P
T_PROMPT, T_SAMPLE = 256, 64
T = T_PROMPT + T_SAMPLE
C = 64
NCH = T // C
N_PROMPT_CH = T_PROMPT // C
LEVELS = 6
TILES = [(0, 128), (128, 128), (256, 64)]

RH, RN = 8, 64
RDIM = RH * RN
RF = RDIM // P
RPROJ = 3 * RDIM + 64 + 64 + 128
RPC = RPROJ // P
DECAY_SCALE = 0.6065306597126334
GN_EPS = RN * 1e-5

GH, GDK, GDV = 4, 64, 128
GK, GV, GR = GH * GDK, GH * GDV, 16
G0 = RPROJ
GZ0 = G0 + 2 * GK + GV
GO0 = GZ0 + GR
P_AB = GO0 + GV
GLA_TAU = 16.0

HH, HD = 8, 128
FF = 2816
FC = FF // P
NE = 8
ALPHA = 4.0 ** 0.25
NORM_EPS = 1e-5

SC = 256
TILE = KC * SC
DENSE_RING = 4
HALF = TILE // 2
BLK = 128
STRIPS = FF // SC
HALVES = 6 * STRIPS
MOE_RING = 11
UNITS = 6
assert HALVES % MOE_RING == 0 and HALVES % UNITS == 0
MAX_BLOCKS = -(-T // BLK)
NX = NE * (MAX_BLOCKS - 1)


def mixed_trunk(nc, ins, outs):
    ctx = ExitStack()
    with ctx:
        def sem(name):
            return ctx.enter_context(nc.semaphore(name))

        def sb(name, shape, dt=F32):
            return ctx.enter_context(nc.sbuf_tensor(name, shape, dt))

        bank = [ctx.enter_context(nc.psum_tensor(f"bank{i}", [P, 512], F32)) for i in range(8)]

        ident = sb("ident", [P, P])
        ones = sb("ones", [P, P])
        bdones = sb("bdones", [P, P])
        utri = sb("utri", [P, P])
        mask_pr = sb("mask_pr", [C, 2, C])
        lower = sb("lower", [C, LEVELS, C])
        upper = sb("upper", [C, LEVELS, C])
        reset = sb("reset", [P, T])
        slots = sb("slots", [P, BLK])
        vec = sb("vec", [P, 160])
        gate_up = sb("gate_up", [GR, GK])
        gz_w = sb("gz_w", [P, KC, GR])
        router = sb("router", [P, KC, NE])
        xT = sb("xT", [P, KC, T])
        arena_words = 45760
        with nc.sbuf_tensor("arena", [P, arena_words], F32) as arena:
            pass
        split_words = (2 * UNITS * HALF) + 2 * KC * BLK + 2 * 2 * BLK
        split_at = arena_words - MOE_RING * HALF - split_words
        sb("arena_low", [P, split_at])
        w_hi = sb("w_hi", [P, UNITS, HALF], F32R)
        w_lo = sb("w_lo", [P, UNITS, HALF], F32R)
        xe_hi = sb("xe_hi", [P, KC, BLK], F32R)
        xe_lo = sb("xe_lo", [P, KC, BLK], F32R)
        gt_hi = sb("gt_hi", [P, 2, BLK], F32R)
        gt_lo = sb("gt_lo", [P, 2, BLK], F32R)
        moe_ring = sb("moe_ring", [P, MOE_RING, HALF])

        def slot(i):
            o = arena_words - (i + 1) * TILE
            return arena[:, o:o + TILE]

        class Region:
            def __init__(self, start, end):
                self.at, self.end = start, end

            def take(self, n):
                o = self.at
                self.at += n
                assert self.at <= self.end, (self.at, self.end)
                return arena[:, o:o + n]

        def tok(ap, k):
            return ap.rearrange("p (k t) -> p k t", k=k)

        dense_top = arena_words - DENSE_RING * TILE

        r = Region(0, dense_top)
        pr_all = r.take(RPC * (T + 2))
        PR = pr_all.rearrange("p (f t) -> p f t", f=RPC)
        XS = tok(r.take(RPC * T), RPC)
        aT = tok(r.take(RF * T), RF)
        bT = tok(r.take(RF * T), RF)
        kkT = tok(r.take(RF * T), RF)
        PRC = r.take(RF * 2 * T).rearrange("p (f a t) -> p f a t", f=RF, a=2)
        QT = tok(r.take(RF * T), RF)
        KT = tok(r.take(RF * T), RF)
        GT = tok(r.take(RF * T), RF)
        gq = tok(r.take(2 * T), 2)
        gk = tok(r.take(2 * T), 2)
        gv = tok(r.take(4 * T), 4)
        gog = tok(r.take(4 * T), 4)
        gla_b = tok(r.take(2 * T), 2)
        oT = tok(r.take(8 * T), 8)
        mix0 = r.at
        s1 = tok(pr_all[:, 0:RF * T], RF)
        s2 = tok(pr_all[:, RF * T:2 * RF * T], RF)
        lw = tok(pr_all[:, 2 * RF * T:3 * RF * T], RF)
        BV = kkT
        a0 = RPC * (T + 2) + RPC * T
        xst = arena[:, mix0:mix0 + 3 * D].rearrange("p (i n) -> p i n", i=3)
        m = Region(mix0, dense_top)
        TV = m.take(2 * RDIM).rearrange("p (b n) -> p b n", b=2)
        TQ = m.take(2 * RDIM).rearrange("p (b n) -> p b n", b=2)
        TK = m.take(2 * RDIM).rearrange("p (b n) -> p b n", b=2)
        G1 = m.take(2 * 2 * RDIM).rearrange("p (b h n) -> p b h n", b=2, h=RH)
        G2 = m.take(2 * 2 * RDIM).rearrange("p (b h n) -> p b h n", b=2, h=RH)
        Tm = m.take(2 * RDIM).rearrange("p (b h n) -> p b h n", b=2, h=RH)
        Tt = m.take(2 * RDIM).rearrange("p (b h n) -> p b h n", b=2, h=RH)
        Xm = m.take(2 * RDIM).rearrange("p (b h n) -> p b h n", b=2, h=RH)
        g1_all = G1.rearrange("p b h n -> p (b h n)")
        wup = g1_all[:, 0:RDIM]
        aup = g1_all[:, RDIM:2 * RDIM]
        gup = g1_all[:, 2 * RDIM:3 * RDIM]
        vrow = G2.rearrange("p b h n -> p (b h n)")[:, 0:2 * P].rearrange("p (a n) -> p a n", a=2)
        W1s = m.take(RDIM)
        Un = m.take(RDIM)
        state_nat = Xm[:, 0, :, :].rearrange("p h n -> p (h n)").rearrange("p (f n) -> p f n", f=RF)
        m2 = Region(0, RPC * (T + 2))
        H = m2.take(2 * RDIM).rearrange("p (g f n) -> p g f n", g=2, f=RF)
        Hout = m2.take(2 * RDIM).rearrange("p (g f n) -> p g f n", g=2, f=RF)
        Osb = arena[:, RPC * (T + 2):RPC * (T + 2) + NCH * RDIM].rearrange("p (c h n) -> p c h n", c=NCH, h=RH)
        Osq = arena[:, a0:a0 + NCH * RDIM].rearrange("p (c h n) -> p c h n", c=NCH, h=RH)

        def attention_buffers(reg, F, heads, width):
            b = {}
            b["Z"] = tok(reg.take(F * T), F)
            b["KD"] = tok(reg.take(F * T), F)
            b["E"] = tok(reg.take(F * T), F)
            b["Sc"] = reg.take(NCH * heads * C).rearrange("p (c h t) -> p c h t", c=NCH, h=heads)
            b["TV"] = reg.take(heads * P)
            b["TK"] = reg.take(F * P)
            b["S"] = reg.take(2 * F * width).rearrange("p (g f n) -> p g f n", g=2, f=F)
            return b

        gla = attention_buffers(Region(mix0, dense_top), 2, GH, 2 * GDV)
        gla.update(F=2, heads=GH, q=gq, k=gk, v=gv, b=gla_b, O=oT[:, 4:8, :], sq=lw, gate=gog,
                   name="gla", vdim=GDV)
        f_ = Region(0, dense_top - 2 * KC * T)
        ff_g = tok(f_.take(FC * T), FC)
        ff_s = tok(f_.take(4 * T), 4)
        res = tok(arena[:, dense_top - 2 * KC * T:dense_top - KC * T], KC)
        sq = tok(arena[:, dense_top - KC * T:dense_top], KC)
        h_ = Region(0, dense_top - 2 * KC * T)
        hq = tok(h_.take(HH * T), HH)
        hf = tok(h_.take(HH * T), HH)
        hi = tok(h_.take(HH * T), HH)
        hg = tok(h_.take(HH * T), HH)
        hb = tok(h_.take(HH * T), HH)
        hgrn = attention_buffers(h_, HH, HH, HD)
        hgrn.update(F=HH, heads=HH, q=hq, k=hf, v=hi, b=hb, O=hq, sq=hgrn["E"], gate=hg,
                    name="hgrn", vdim=HD)
        e_ = Region(0, split_at)
        xtok = e_.take(3 * D).rearrange("p (i n) -> p i n", i=3)
        acc = tok(e_.take(KC * T), KC)
        sq2 = tok(e_.take(KC * T), KC)
        pick = e_.take(3 * BLK).rearrange("p (i n) -> p i n", i=3)
        pickw = e_.take(3 * BLK).rearrange("p (i n) -> p i n", i=3)
        pickT = e_.take(T)
        eh = e_.take(2 * SC).rearrange("p (b n) -> p b n", b=2)
        eg = e_.take(SC)
        ey = e_.take(D)
        pair = e_.take(2 * 3 * NE * NE).rearrange("p (a i n) -> p a i n", a=2, i=3)
        compact = e_.take(NX * NX).rearrange("p (j c) -> p j c", j=NX)

        dC = sb("dC", [P, RF, NCH])
        ends = sb("ends", [P, HH, NCH])
        last = sb("last", [P, 2, RPC])
        lrow = sb("lrow", [RPC, 2, P])
        gz_s = sb("gz_s", [GR, T])
        stat = sb("stat", [C, 2, NCH * RH])
        mean = sb("mean", [P, T])
        lbw = sb("lbw", [P, 8, HH])
        eps_gn = sb("eps_gn", [P, 1])
        eps_norm = sb("eps_norm", [P, 1])
        lg = sb("lg", [P, 3, NE])
        rt = sb("rt", [P, 12, 3, NE])
        cur = sb("cur", [P, 3])
        wcur = sb("wcur", [P, 3])
        jlt = sb("jlt", [P, NE, NE])
        pos = sb("pos", [P, NE, 3])
        wts = sb("wts", [P, NE, 3])
        cnt = sb("cnt", [P, NE])
        cand = sb("cand", [P, 8, NX])
        extra_i = sb("extra_i", [P, 2, NX], I32)
        bases = sb("bases", [P, NX])
        n_extra = sb("n_extra", [P, 4], I32)

        V, vloads, at = {}, [], [0, 0]

        def vector(name, ap, table):
            rows = ap.shape[0]
            V[name] = (0 if table == 0 else 91) + at[table]
            vloads.append((table, at[table], rows, ap))
            at[table] += rows

        def rows_of(ap, w=P):
            return ap.rearrange("a (r w) -> (a r) w", w=w)

        vector("mu", rows_of(ins["rwkv_mu"]), 0)
        vector("shift", rows_of(ins["cache_rwkv_shift"].rearrange("a b n -> (a b) n")), 0)
        for n in ("rwkv_w0", "rwkv_a0", "rwkv_k_k", "rwkv_k_a"):
            vector(n, rows_of(ins[n]), 0)
        vector("rwkv_r_k", rows_of(ins["rwkv_r_k"].rearrange("a h n -> a (h n)")), 0)
        for n in ("rwkv_gn_w", "rwkv_gn_b", "gla_gate_b", "gla_norm_w",
                  "ln_ab_g", "ln_ab_b", "ln_ffn_g", "ln_ffn_b"):
            vector(n, rows_of(ins[n]), 0)
        assert at[0] == 91
        for n in ("hgrn_lb", "hgrn_norm_w", "ln_c_g", "ln_c_b", "ln_moe_g", "ln_moe_b"):
            vector(n, rows_of(ins[n]), 1)

        def vcol(name, j=0):
            return vec[:, V[name] + j:V[name] + j + 1]

        names = {}

        shared = {}
        for stage, of_gla in (("z", LEVELS + 1), ("sc", (LEVELS + 1) * NCH * 2), ("sc_full", (LEVELS + 1) * NCH * 2),
                              ("qk", 1), ("tm", 2 * NCH), ("tm_full", 2 * NCH), ("s", NCH), ("o", NCH), ("o_full", NCH),
                              ("ds_full", NCH), ("osq", 1), ("rms", GH), ("rms_full", GH), ("min", 1), ("softplus", 1),
                              ("dist", LEVELS + 1), ("e", LEVELS + 2), ("s_zero", 2), ("b", 2), ("out", 1),
                              ("state_in", 32), ("stored", 64)):
            shared["gla_" + stage] = ("attention_" + stage, 0)
            shared["hgrn_" + stage] = ("attention_" + stage, of_gla)
        for stage, each in (("res", KC), ("ln_full", 2), ("centered", 1), ("sq", 1), ("std", 1), ("ln", 1)):
            for i, n_ in enumerate(("ab", "ffn", "c", "moe")):
                shared[n_ + "_" + stage] = ("norm_" + stage, i * each)

        def S(name):
            name = shared.get(name, (name, 0))[0]
            if name not in names:
                names[name] = sem(name)
            return names[name]

        def at_count(name, value=1):
            return S(name), shared.get(name, (name, 0))[1] + value

        tiles = []

        def strip(w, row0, rows, col):
            return w[row0 * P:(row0 + rows) * P, col:col + SC].rearrange("(k p) n -> p k n", p=P)

        w_in = ins["w_in_ab"][0]
        AB_COLS = [i * SC for i in range(RPROJ // SC)] + [G0, G0 + GK, G0 + 2 * GK, G0 + 2 * GK + SC, GO0, GO0 + SC]
        for i, col in enumerate(AB_COLS):
            tiles.append((strip(w_in, 0, KC, col), KC, "ab_full", 2 * i + 2))
        for i in range(D // SC):
            tiles.append((strip(ins["w_out_ab"][0], 0, KC, i * SC), KC, "out_ab_full", 2 * i + 2))
        for i in range(STRIPS):
            tiles.append((strip(ins["ffn_w1"][0], 0, KC, i * SC), KC, "h1_full", 2 * i + 2))
            tiles.append((strip(ins["ffn_w3"][0], 0, KC, i * SC), KC, "h3_full", 2 * i + 2))
        W2_GROUPS = [(0, 8), (8, 8), (16, 6)]
        for i in range(D // SC):
            for gi, (r0, n) in enumerate(W2_GROUPS):
                tiles.append((strip(ins["ffn_w2"][0], r0, n, i * SC), n) +
                             (("w2_full", 2 * i + 2) if gi == 2 else ("w2_part_used", 2 * i + gi + 1)))
        for i in range(4 * D // SC):
            tiles.append((strip(ins["w_in_c"][0], 0, KC, i * SC), KC, "in_c_full", 2 * i + 2))
        for i in range(D // SC):
            tiles.append((strip(ins["w_out_c"][0], 0, KC, i * SC), KC, "out_c_full", 2 * i + 2))
        ND = len(tiles)
        AB_T, OUT_T = 0, len(AB_COLS)
        FFN_T = OUT_T + D // SC
        W2_T = FFN_T + 2 * STRIPS
        INC_T = W2_T + 3 * (D // SC)
        OUTC_T = INC_T + 4 * D // SC

        def tile_of(i):
            return slot(i % DENSE_RING).rearrange("p (k n) -> p k n", k=KC)

        def bc(ap, axis, n):
            shape = list(ap.shape)
            return ap.unsqueeze(axis).to_broadcast(shape[:axis] + [n] + shape[axis:])

        def chunk(c):
            return slice(c * C, (c + 1) * C)

        BATCHES = [[0, 1], [2, 3], [4]]
        E_H1, E_H3, E_Y, E_SCR = bank[0:2], bank[2:4], bank[4:6], bank[6:8]

        UP1 = [0] + [3 * s - 1 for s in range(1, STRIPS)]
        UP3 = [1] + [3 * s for s in range(1, STRIPS)]
        DOWN = [3 * s + 4 for s in range(STRIPS - 1)] + [3 * STRIPS - 1]

        def res_of(n_):
            return acc if n_ == "moe" else res

        def sq_of(n_):
            return sq2 if n_ == "moe" else sq

        def expert_loops(eng, body, rest):
            body(0, 0, None)
            with eng.Fori(1, NE) as e:
                body(e, e, None)
            eng.wait_ge(S("extras_known"), 1)
            nx = eng.value_load(n_extra[0:1, 0:1], min_val=0, max_val=NX)
            with eng.If(nx > 0):
                with eng.Fori(0, nx) as j:
                    body(j + NE, eng.value_load(extra_i[0:1, 0, bass.ds(j, 1)], min_val=0, max_val=NE - 1), j)
            rest(nx + NE)

        block = ctx.enter_context(nc.Block())
        where = {}

        @block.tensor
        def _(pe):
            turn = [0]
            owner = [None] * 8

            def take(name, taken, value):
                k = turn[0] % 8
                turn[0] += 1
                if owner[k]:
                    pe.wait_ge(*at_count(owner[k][0], owner[k][1]))
                owner[k] = (taken, value)
                where[name] = bank[k]
                return bank[k]

            def weights(i):
                pe.wait_ge(*at_count(f"tile_in{i % DENSE_RING}", 16 * (i // DENSE_RING + 1)))
                return tile_of(i)

            def dense_pair(i, rhs, name, j0, full, taken, k0=0):
                w = weights(i)
                for j in range(2):
                    b = take((name, j0 + j), taken, j0 + j + 1)
                    for k in range(KC):
                        mm = pe.matmul(b[:, 0:T], w[:, k, j * P:(j + 1) * P], rhs[:, k, :],
                                       start=(k == 0), stop=(k == KC - 1))
                    mm.then_inc(S(full), 1)

            pe.wait_ge(*at_count("masks", 1))
            pe.wait_ge(*at_count("vectors_in", 16 * len(vloads)))
            for t in range(2):
                n = at[t]
                b = take(("vec", t), "vec_done", t + 1)
                pe.transpose(b[:, 0:n], vrow[0:n, t, :], ident[0:n, 0:n]).then_inc(S("vec_full"), 1)
            pe.wait_ge(*at_count("x_in", 48))
            for k in range(KC):
                b = take(("x", k), "x_done", k + 1)
                for i, (t0, n) in enumerate(TILES):
                    mm = pe.transpose(b[:, t0:t0 + n], xst[0:n, i, k * P:(k + 1) * P], ident[0:n, 0:n])
                mm.then_inc(S("x_full"), 1)

            pe.wait_ge(*at_count("x_done", KC))
            for i in range(len(AB_COLS)):
                dense_pair(AB_T + i, xT, "ab", 2 * i, "ab_full", "ab_done")
            pe.wait_ge(*at_count("small_in", 16 * 6))
            b = take(("ab", 2 * len(AB_COLS)), "ab_done", 2 * len(AB_COLS) + 1)
            for k in range(KC):
                mm = pe.matmul(b[0:GR, 0:T], gz_w[:, k, :], xT[:, k, :], start=(k == 0), stop=(k == KC - 1))
            mm.then_inc(S("ab_full"), 1)

            pe.wait_ge(*at_count("last_copied", 2))
            pe.wait_ge(*at_count("lora_in", 2))
            for n in range(3 * RF):
                f = n % RF
                w = (wup, aup, gup)[n // RF]
                b = take(("lora", n), "lora_done", n + 1)
                pe.matmul(b[:, 0:T], w[:, f * P:(f + 1) * P], XS[:, 13 if n >= 2 * RF else 12, :],
                          start=True, stop=True).then_inc(S("lora_full"), 1)
            pe.wait_ge(*at_count("ab_done", 2 * len(AB_COLS) + 1))
            for f in range(2):
                n = 3 * RF + f
                b = take(("lora", n), "lora_done", n + 1)
                pe.matmul(b[:, 0:T], gate_up[:, f * P:(f + 1) * P], gz_s[:, :], start=True, stop=True)\
                  .then_inc(S("lora_full"), 1)
            for g in range(2):
                b = take(("last", g), "last_rows", g + 1)
                pe.transpose(b[0:RPC, 0:P], last[:, g, :], ident[:, :]).then_inc(S("last_full"), 1)

            pe.wait_ge(*at_count("kk_squares", 1))
            for f in range(RF):
                b = take(("kk", f), "kk_norm", f + 1)
                pe.matmul(b[:, 0:T], bdones[:, :], KT[:, f, :], start=True, stop=True).then_inc(S("kk_full"), 1)
            pe.wait_ge(*at_count("bonus_in", 1))
            for f in range(RF):
                b = take(("bonus", f), "bonus_done", f + 1)
                pe.matmul(b[:, 0:T], bdones[:, :], oT[:, f, :], start=True, stop=True).then_inc(S("bonus_full"), 1)
            pe.wait_ge(*at_count("rwkv_state_in", 32))
            b = take(("h0", 0), "h_init", 1)
            for f in range(RF):
                mm = pe.transpose(b[:, f * P:(f + 1) * P], state_nat[:, f, :], ident[:, :])
            mm.then_inc(S("h0_full"), 1)

            pe.wait_ge(*at_count("rwkv_ready", 1))
            for batch in BATCHES:
                for bi, c in enumerate(batch):
                    for n, src in enumerate((XS[:, 8:12, :], QT, KT)):
                        b = take(("tm", 3 * c + n), "tm_done", 3 * c + n + 1)
                        for f in range(RF):
                            mm = pe.transpose(b[0:C, f * P:(f + 1) * P], src[:, f, chunk(c)], ident[:, :])
                        mm.then_inc(S("tm_full"), 1)
                    for n, left in enumerate((KT, QT)):
                        for par in range(2):
                            rows = slice(64 * par, 64 * par + 64)
                            b = take(("gram", 6 * c + 2 * n + par), "gram_done", 6 * c + 2 * n + par + 1)
                            for f in range(RF):
                                mm = pe.matmul(b[0:C, f * P:(f + 1) * P], left[rows, f, chunk(c)],
                                               PRC[rows, f, :, chunk(c)], start=(f == 0), stop=(f == RF - 1),
                                               skip_group_check=True)
                            mm.then_inc(S("gram_full"), 1)
                    for par in range(2):
                        rows = slice(64 * par, 64 * par + 64)
                        b = take(("gram", 6 * c + 4 + par), "gram_done", 6 * c + 4 + par + 1)
                        for f in range(RF):
                            mm = pe.matmul(b[0:C, f * C:(f + 1) * C], PRC[rows, f, 0, chunk(c)], QT[rows, f, chunk(c)],
                                           start=(f == 0), stop=(f == RF - 1), skip_group_check=True)
                        mm.then_inc(S("gram_full"), 1)
                first, nb = batch[0], len(batch)
                for lv in range(1, LEVELS):
                    for bi, c in enumerate(batch):
                        pe.wait_ge(*at_count("inv_ready", LEVELS * first + (lv - 1) * nb + bi + 1))
                        n = 5 * first + (lv - 1) * nb + bi + 1
                        b = take(("X", lv, c), "inv_x", n)
                        for hh in range(RH):
                            mm = pe.matmul(b[0:C, hh * C:(hh + 1) * C], G2[0:C, bi, hh, 0:C], Tm[0:C, bi, hh, :],
                                           start=(hh == 0), stop=(hh == RH - 1), skip_group_check=True)
                        mm.then_inc(S("inv_full"), 1)
                    for bi, c in enumerate(batch):
                        pe.wait_ge(*at_count("inv_x", 5 * first + (lv - 1) * nb + bi + 1))
                        if lv < LEVELS - 1:
                            b = take(("Y", lv, c), "inv_y", 4 * first + (lv - 1) * nb + bi + 1)
                            for hh in range(RH):
                                mm = pe.matmul(b[0:C, hh * C:(hh + 1) * C], Tt[0:C, bi, hh, :], Xm[0:C, bi, hh, :],
                                               start=(hh == 0), stop=(hh == RH - 1), skip_group_check=True)
                            mm.then_inc(S("inv_full"), 1)
                        b = take(("Yt", lv, c), "inv_ready", LEVELS * first + lv * nb + bi + 1)
                        for hh in range(RH):
                            mm = pe.matmul(b[0:C, hh * C:(hh + 1) * C], Xm[0:C, bi, hh, :], Tt[0:C, bi, hh, :],
                                           start=(hh == 0), stop=(hh == RH - 1), skip_group_check=True)
                        mm.then_inc(S("inv_full"), 1)
                for bi, c in enumerate(batch):
                    g = 0 if c < N_PROMPT_CH else 1

                    def heads(b, left, right, last_one=False):
                        for hh in range(RH):
                            st = (hh % 2) * RF + hh // 2
                            mm = pe.matmul(b[0:C, hh * C:(hh + 1) * C], left(st), right[:, hh * C:(hh + 1) * C],
                                           start=False, stop=(last_one and hh == RH - 1), skip_group_check=True)
                        return mm

                    pe.wait_ge(*at_count("h_init", 1))
                    if c:
                        pe.wait_ge(*at_count("h_done", c))
                    pe.wait_ge(*at_count("tm_done", 3 * c + 3))
                    b = take(("w1", c), "w1_done", c + 1)
                    for f in range(RF):
                        pe.matmul(b[0:C, f * P:(f + 1) * P], PRC[:, f, 0, chunk(c)], H[:, g, f, :],
                                  start=(f == 0), stop=False, skip_group_check=True)
                    heads(b, lambda st: G1[0:C, bi, st, 0:C], TV[0:C, bi, :], True).then_inc(S("seq_full"), 1)
                    bo = take(("o", c), "o_done", c + 1)
                    for f in range(RF):
                        pe.matmul(bo[0:C, f * P:(f + 1) * P], PRC[:, f, 1, chunk(c)], H[:, g, f, :],
                                  start=(f == 0), stop=False, skip_group_check=True)
                    heads(bo, lambda st: G1[0:C, bi, st, C:2 * C], TV[0:C, bi, :])
                    pe.wait_ge(*at_count("inv_ready", LEVELS * first + (LEVELS - 1) * nb + bi + 1))
                    pe.wait_ge(*at_count("w1_done", c + 1))
                    b = take(("u", c), "u_done", c + 1)
                    for hh in range(RH):
                        st = (hh % 2) * RF + hh // 2
                        mm = pe.matmul(b[0:C, hh * C:(hh + 1) * C], Tt[0:C, bi, st, :], W1s[0:C, hh * C:(hh + 1) * C],
                                       start=(hh == 0), stop=(hh == RH - 1), skip_group_check=True)
                    mm.then_inc(S("seq_full"), 1)
                    pe.wait_ge(*at_count("u_done", c + 1))
                    heads(bo, lambda st: G2[0:C, bi, st, C:2 * C], Un[0:C, :], True).then_inc(S("seq_full"), 1)
                    b = take(("dh", c), "h_done", c + 1)
                    for f in range(RF):
                        cols = slice(f * P, (f + 1) * P)
                        pe.matmul(b[:, cols], TK[0:C, bi, cols], TV[0:C, bi, cols],
                                  start=(f == 0), stop=False, skip_group_check=True)
                        mm = pe.matmul(b[:, cols], TQ[0:C, bi, cols], Un[0:C, cols],
                                       start=False, stop=(f == RF - 1), skip_group_check=True)
                    mm.then_inc(S("seq_full"), 1)
            pe.wait_ge(*at_count("h_done", NCH))
            for g in range(2):
                b = take(("hout", g), "hout_done", g + 1)
                for f in range(RF):
                    mm = pe.transpose(b[:, f * P:(f + 1) * P], H[:, g, f, :], ident[:, :])
                mm.then_inc(S("hout_full"), 1)
            pe.wait_ge(*at_count("gn_done", 1))
            for c in range(NCH):
                b = take(("ot", c), "ot_done", c + 1)
                for f in range(RF):
                    mm = pe.transpose(b[:, f * C:(f + 1) * C],
                                      Osb[0:C, c, 2 * f:2 * f + 2, :].rearrange("p h n -> p (h n)"), ident[0:C, 0:C])
                mm.then_inc(S("ot_full"), 1)

            def attention(a):
                n_, F, NH = a["name"], a["F"], a["heads"]
                pars = NH // F
                W = P // pars
                banks = max(1, pars)
                for lv in range(LEVELS + 1):
                    pe.wait_ge(*at_count(n_ + "_z", lv + 1))
                    zb = (a["Z"], a["KD"])[lv % 2]
                    for c in range(NCH):
                        for par in range(pars):
                            rows = slice(W * par, W * par + W)
                            i = lv * NCH * pars + c * pars + par
                            b = take((n_, "sc", i), n_ + "_sc", i + 1)
                            for f in range(F):
                                left, right = (a["k"], a["q"]) if lv == 0 else (zb, zb)
                                mm = pe.matmul(b[0:C, f * C:(f + 1) * C], left[rows, f, chunk(c)],
                                               right[rows, f, chunk(c)], start=(f == 0), stop=(f == F - 1),
                                               skip_group_check=True)
                            mm.then_inc(S(n_ + "_sc_full"), 1)
                pe.wait_ge(*at_count(n_ + "_qk", 1))
                pe.wait_ge(*at_count(n_ + "_sc", (LEVELS + 1) * NCH * pars))
                pe.wait_ge(*at_count(n_ + "_state_in", 16 * pars))
                tv = 0
                for c in range(NCH):
                    g = 0 if c < N_PROMPT_CH else 1
                    for src, dst_n, per in ((a["v"], NH, 4), (a["KD"], F, 4)):
                        for k0 in range(0, dst_n, per):
                            m_ = min(per, dst_n - k0)
                            b = take((n_, "tm", tv), n_ + "_tm", tv + 1)
                            tv += 1
                            for k in range(m_):
                                mm = pe.transpose(b[0:C, k * P:(k + 1) * P], src[:, k0 + k, chunk(c)], ident[:, :])
                            mm.then_inc(S(n_ + "_tm_full"), 1)
                    if c:
                        pe.wait_ge(*at_count(n_ + "_s", c))
                    b = take((n_, "o", c), n_ + "_o", c + 1)
                    for hh in range(NH):
                        f, par = hh // pars, hh % pars
                        pe.matmul(b[:, hh * C:(hh + 1) * C], a["S"][:, g, f, par * P:(par + 1) * P],
                                  a["Z"][:, f, chunk(c)], start=(hh == 0), stop=False, skip_group_check=True)
                    pe.wait_ge(*at_count(n_ + "_tm", tv))
                    for hh in range(NH):
                        f, par = hh // pars, hh % pars
                        mm = pe.matmul(b[:, hh * C:(hh + 1) * C], a["TV"][0:C, hh * P:(hh + 1) * P],
                                       a["Sc"][0:C, c, par * F + f, :], start=False, stop=(hh == NH - 1),
                                       skip_group_check=True)
                    mm.then_inc(S(n_ + "_o_full"), 1)
                    per = 4 // pars
                    for k0 in range(0, F, per):
                        i = c * (F // min(per, F)) + k0 // per
                        b = take((n_, "ds", i), n_ + "_s", c + 1)
                        for k in range(min(per, F)):
                            f = k0 + k
                            mm = pe.matmul(b[:, k * P * pars:(k + 1) * P * pars], a["TK"][0:C, f * P:(f + 1) * P],
                                           a["TV"][0:C, f * P * pars:(f + 1) * P * pars],
                                           start=(k == 0), stop=(k == min(per, F) - 1), skip_group_check=True)
                        mm.then_inc(S(n_ + "_ds_full"), 1)
                pe.wait_ge(*at_count(n_ + "_osq", 1))
                for hh in range(NH):
                    b = take((n_, "rms", hh), n_ + "_rms", hh + 1)
                    pe.matmul(b[:, 0:T], ones[:, :], a["sq"][:, hh, :], start=True, stop=True)\
                      .then_inc(S(n_ + "_rms_full"), 1)

            def layer_norm(n_):
                for part, ready, src, taken in (("sum", "_res", res_of(n_), "_centered"), ("sqs", "_sq", sq_of(n_), "_std")):
                    if n_ + ready != "moe_res":
                        pe.wait_ge(*at_count(n_ + ready, 1 if ready == "_sq" else KC))
                    b = take((n_, part), n_ + taken, 1)
                    for k in range(KC):
                        mm = pe.matmul(b[:, 0:T], ones[:, :], src[:, k, :], start=(k == 0), stop=(k == KC - 1))
                    mm.then_inc(S(n_ + "_ln_full"), 1)

            attention(gla)
            pe.wait_ge(*at_count("rwkv_out", 1))
            pe.wait_ge(*at_count("gla_out", 1))
            for i in range(D // SC):
                dense_pair(OUT_T + i, oT, "out_ab", 2 * i, "out_ab_full", "ab_res")
            layer_norm("ab")
            pe.wait_ge(*at_count("ab_ln", 1))
            for i in range(STRIPS):
                dense_pair(FFN_T + 2 * i, xT, "h1", 2 * i, "h1_full", "h1_done")
                dense_pair(FFN_T + 2 * i + 1, xT, "h3", 2 * i, "h3_full", "ffn_g")
            pe.wait_ge(*at_count("ffn_g", FC))
            for i in range(D // SC):
                two = [take(("w2", 2 * i + j), "ffn_res", 2 * i + j + 1) for j in range(2)]
                for gi, (r0, n) in enumerate(W2_GROUPS):
                    w = weights(W2_T + 3 * i + gi)
                    for j in range(2):
                        for k in range(n):
                            mm = pe.matmul(two[j][:, 0:T], w[:, k, j * P:(j + 1) * P], ff_g[:, r0 + k, :],
                                           start=(r0 + k == 0), stop=(r0 + k == FC - 1))
                        if gi == len(W2_GROUPS) - 1:
                            mm.then_inc(S("w2_full"), 1)
                    if gi < len(W2_GROUPS) - 1:
                        mm.then_inc(S("w2_part_used"), 1)
            layer_norm("ffn")
            pe.wait_ge(*at_count("ffn_ln", 1))
            for i in range(4 * D // SC):
                dense_pair(INC_T + i, xT, "in_c", 2 * i, "in_c_full", "in_c_done")
            attention(hgrn)
            pe.wait_ge(*at_count("hgrn_out", 1))
            for i in range(D // SC):
                dense_pair(OUTC_T + i, hq, "out_c", 2 * i, "out_c_full", "c_res")
            layer_norm("c")

            pe.wait_ge(*at_count("c_ln", 1))
            for i, (t0, n) in enumerate(TILES):
                for k0 in (0, 4):
                    j = 2 * i + k0 // 4
                    b = take(("xtok", j), "xtok_done", j + 1)
                    for k in range(4):
                        mm = pe.transpose(b[0:n, k * P:(k + 1) * P], xT[:, k0 + k, t0:t0 + n], ident[:, :])
                    mm.then_inc(S("xtok_full"), 1)
            for i, (t0, n) in enumerate(TILES):
                b = take(("logit", i), "logits_done", i + 1)
                for k in range(KC):
                    mm = pe.matmul(b[0:n, 0:NE], xT[:, k, t0:t0 + n], router[:, k, :],
                                   start=(k == 0), stop=(k == KC - 1))
                mm.then_inc(S("logit_full"), 1)
            pe.wait_ge(*at_count("chosen", 1))
            for i in range(3):
                b = take(("pos", i), "pos_done", i + 1)
                for j in range(i):
                    pe.matmul(b[:, 0:NE], ones[:, :], rt[:, 0, j, :], start=(j == 0), stop=False)
                pe.matmul(b[:, 0:NE], utri[:, :], rt[:, 0, i, :], start=(i == 0), stop=True).then_inc(S("pos_full"), 1)
            b = take(("count", 0), "pos_done", 4)
            for j in range(3):
                mm = pe.matmul(b[:, 0:NE], ones[:, :], rt[:, 0, j, :], start=(j == 0), stop=(j == 2))
            mm.then_inc(S("pos_full"), 1)
            pe.wait_ge(*at_count("xtok_done", 6))
            pe.wait_ge(*at_count("pos_done", 4))
            pe.wait_ge(*at_count("logits_done", 3))
            pe.wait_ge(*at_count("c_std", 1))
            pe.wait_ge(*at_count("hgrn_rms", HH))
            pe.wait_ge(*at_count("c_res", KC))

            def half_tile(n, q, h):
                pe.wait_ge(S("e_lo"), HALVES * n + 2 * q + h + 1)
                u = (2 * q + h) % UNITS
                return w_hi[:, u, :], w_lo[:, u, :]

            def scatter(n, k, b):
                if k == 0:
                    pe.wait_ge(S("e_y"), 2 * n)
                    pe.wait_ge(S("e_pickt"), n)
                pe.matmul(b[:, 0:T], ey[:, k * P:(k + 1) * P], pickT[:, :], start=True, stop=True)\
                  .then_inc(S("e_scatter"), 1)

            def expert_block(n, e, j_extra):
                later = not isinstance(n, int)
                pe.wait_ge(S("e_pick"), n + 1)
                if later:
                    pe.wait_ge(S("e_pickt"), n)
                for half in range(2):
                    for k in range(4):
                        for i in range(3):
                            mm = pe.matmul(E_SCR[half][:, k * BLK:(k + 1) * BLK],
                                           xtok[:, i, (4 * half + k) * P:(4 * half + k + 1) * P], pick[:, i, :],
                                           start=(i == 0), stop=(i == 2))
                    mm.then_inc(S("e_gather_full"), 1)
                pe.wait_ge(S("e_rows"), 2 * n + 2)

                def up(q, b):
                    for h in range(2):
                        hi_, lo_ = half_tile(n, q, h)
                        for k in range(4):
                            cols = slice(k * SC, (k + 1) * SC)
                            kk_ = 4 * h + k
                            pe.matmul(b[:, 0:SC], xe_hi[:, kk_, :], hi_[:, cols], start=(kk_ == 0), stop=False)
                            pe.matmul(b[:, 0:SC], xe_lo[:, kk_, :], hi_[:, cols], start=False, stop=False)
                            mm = pe.matmul(b[:, 0:SC], xe_hi[:, kk_, :], lo_[:, cols], start=False, stop=(kk_ == KC - 1))
                        mm.then_inc(S("e_used"), 1)

                def hidden_to_rows(s):
                    pe.wait_ge(S("e_g"), STRIPS * n + s + 1)
                    for j in range(2):
                        mm = pe.transpose(E_SCR[0][:, j * BLK:(j + 1) * BLK], eg[:, j * P:(j + 1) * P], ident[:, :])
                    mm.then_inc(S("e_gt_full"), 1)

                def down(s):
                    pe.wait_ge(S("e_gt"), STRIPS * n + s + 1)
                    if s == 0 and later:
                        pe.wait_ge(S("e_y"), 2 * n)
                    for j in range(2):
                        hi_, lo_ = half_tile(n, DOWN[s], j)
                        for half in range(2):
                            cols = slice(half * 512, (half + 1) * 512)
                            pe.matmul(E_Y[half][:, :], gt_hi[:, j, :], hi_[:, cols], start=(s == 0 and j == 0), stop=False)
                            pe.matmul(E_Y[half][:, :], gt_lo[:, j, :], hi_[:, cols], start=False, stop=False)
                            mm = pe.matmul(E_Y[half][:, :], gt_hi[:, j, :], lo_[:, cols],
                                           start=False, stop=(s == STRIPS - 1 and j == 1))
                        mm.then_inc(S("e_used"), 1)

                for s in range(STRIPS):
                    up(UP1[s], E_H1[s % 2])
                    if s:
                        hidden_to_rows(s - 1)
                    up(UP3[s], E_H3[s % 2])
                    if s:
                        down(s - 1)
                    if later and 1 <= s <= KC:
                        if s > 1:
                            pe.wait_ge(S("e_added"), KC * (n - 1) + s - 1)
                        scatter(n, s - 1, E_SCR[1])
                hidden_to_rows(STRIPS - 1)
                if later:
                    pe.wait_ge(S("e_added"), KC * n)
                for i, (t0, m_) in enumerate(TILES):
                    mm = pe.transpose(E_SCR[1][:, t0:t0 + m_], pickw[0:m_, i, :], ident[0:m_, 0:m_])
                mm.then_inc(S("e_pickt_full"), 1)
                down(STRIPS - 1)

            def last_rows(n):
                for k in range(KC):
                    if k >= 4:
                        pe.wait_ge(S("e_added"), KC * (n - 1) + k - 3)
                    scatter(n, k, bank[k % 4])
                pe.wait_ge(S("e_added"), KC * n)

            expert_loops(pe, expert_block, last_rows)
            layer_norm("moe")
            pe.wait_ge(*at_count("moe_ln", 1))
            for i, (t0, n) in enumerate(TILES):
                for k0 in (0, 4):
                    j = 2 * i + k0 // 4
                    b = take(("y", j), "y_done", j + 1)
                    for k in range(4):
                        mm = pe.transpose(b[0:n, k * P:(k + 1) * P], xT[:, k0 + k, t0:t0 + n], ident[:, :])
                    mm.then_inc(S("y_full"), 1)

        @block.vector
        def _(dve):
            chain = [0]

            def link(ins_):
                chain[0] += 1
                ins_.then_inc(S("dve_chain"), 1)
                dve.wait_ge(S("dve_chain"), chain[0])

            dve.wait_ge(*at_count("vec_done", 2))
            dve.wait_ge(*at_count("masks"))
            dve.wait_ge(*at_count("pr_zero"))
            l0, l1 = vec[:, V["hgrn_lb"]:V["hgrn_lb"] + HH], vec[:, V["hgrn_lb"] + HH:V["hgrn_lb"] + 2 * HH]
            link(dve.tensor_tensor(lbw[:, 6, :], l0, l1, ALU.max))
            link(dve.tensor_tensor(lbw[:, 0, :], l0, lbw[:, 6, :], ALU.subtract))
            dve.tensor_tensor(lbw[:, 1, :], l1, lbw[:, 6, :], ALU.subtract).then_inc(S("lb_in"), 1)
            dve.wait_ge(*at_count("lb_exp"))
            link(dve.tensor_tensor(lbw[:, 7, :], lbw[:, 2, :], lbw[:, 6, :], ALU.add))
            link(dve.reciprocal(lbw[:, 5, :], lbw[:, 7, :]))
            link(dve.tensor_tensor(lbw[:, 5, :], lbw[:, 5, :], lbw[:, 2, :], ALU.mult))
            dve.tensor_tensor(lbw[:, 4, :], lbw[:, 0, :], lbw[:, 1, :], ALU.subtract).then_inc(S("lb_sum"), 1)
            dve.wait_ge(*at_count("lb_ln"))
            link(dve.tensor_tensor(lbw[:, 3, :], lbw[:, 1, :], lbw[:, 7, :], ALU.subtract))
            dve.tensor_copy(PR[:, :, T_PROMPT + 1:T_PROMPT + 2].rearrange("p f a -> p (f a)"),
                            vec[:, V["shift"]:V["shift"] + RPC]).then_inc(S("shift_row"), 1)
            dve.wait_ge(*at_count("shift_row"))
            for f in range(RPC):
                dve.wait_ge(*at_count("ab_done", f + 1))
                link(dve.tensor_tensor(XS[:, f, 0:T_PROMPT], PR[:, f, 0:T_PROMPT], PR[:, f, 1:T_PROMPT + 1], ALU.subtract))
                link(dve.tensor_tensor(XS[:, f, T_PROMPT:T], PR[:, f, T_PROMPT + 1:T + 1],
                                       PR[:, f, T_PROMPT + 2:T + 2], ALU.subtract))
                dve.scalar_tensor_tensor(XS[:, f, 0:T_PROMPT], XS[:, f, 0:T_PROMPT], vcol("mu", f),
                                         PR[:, f, 1:T_PROMPT + 1], ALU.mult, ALU.add)
                dve.scalar_tensor_tensor(XS[:, f, T_PROMPT:T], XS[:, f, T_PROMPT:T], vcol("mu", f),
                                         PR[:, f, T_PROMPT + 2:T + 2], ALU.mult, ALU.add).then_inc(S("xs"), 1)
            dve.tensor_copy(last[:, 0, :], PR[:, :, T_PROMPT:T_PROMPT + 1].rearrange("p f a -> p (f a)"))\
               .then_inc(S("last_copied"), 1)
            dve.tensor_copy(last[:, 1, :], PR[:, :, T + 1:T + 2].rearrange("p f a -> p (f a)"))\
               .then_inc(S("last_copied"), 1)
            dve.wait_ge(*at_count("lora_done", RF))
            dve.wait_ge(*at_count("xs", RPC))
            dve.wait_ge(*at_count("last_copied", 2))
            link(dve.tensor_scalar(lw, lw, -DECAY_SCALE, None, ALU.mult))
            for f in range(RF):
                link(dve.tensor_tensor_scan(bT[:, f, :], reset[:, :], lw[:, f, :], 0.0, ALU.mult, ALU.add))
            dve.tensor_tensor(s1, bT, lw, ALU.subtract).then_inc(S("decay_sums"), 1)
            for f in range(RF):
                ins_ = dve.tensor_scalar(kkT[:, f, :], XS[:, 4 + f, :], vcol("rwkv_k_k", f), None, ALU.mult)
            link(ins_)
            dve.tensor_tensor(KT, kkT, kkT, ALU.mult).then_inc(S("kk_squares"), 1)
            dve.wait_ge(*at_count("lora_done", 2 * RF))
            dve.wait_ge(*at_count("kk_norm", RF))
            for f in range(RF):
                dve.tensor_scalar(KT[:, f, :], aT[:, f, :], -1.0, vcol("rwkv_k_a", f), ALU.add, ALU.mult)
            link(dve.tensor_scalar(QT, QT, 1e-12, None, ALU.max))
            link(dve.scalar_tensor_tensor(KT, KT, 1.0, XS[:, 4:8, :], ALU.add, ALU.mult))
            link(dve.reciprocal(QT, QT))
            link(dve.tensor_tensor(kkT, kkT, QT, ALU.mult))
            for f in range(RF):
                dve.scalar_tensor_tensor(oT[:, f, :], XS[:, f, :], vcol("rwkv_r_k", f), KT[:, f, :],
                                         ALU.mult, ALU.mult).then_inc(S("bonus_row"), 1)
            link(dve.tensor_tensor(QT, aT, kkT, ALU.mult))
            dve.wait_ge(*at_count("bonus_row", RF))
            dve.wait_ge(*at_count("decay_exp", 3))
            dve.tensor_tensor(PRC[:, :, 0, :], s2, kkT, ALU.mult).then_inc(S("bonus_in"), 1)
            dve.tensor_tensor(PRC[:, :, 1, :], s1, XS[:, 0:4, :], ALU.mult)
            dve.tensor_copy(dC[:, :, :], s1.rearrange("p f (c t) -> p f c t", c=NCH)[:, :, :, C - 1])
            dve.tensor_tensor(QT, QT, lw, ALU.mult)
            dve.tensor_tensor(KT, KT, lw, ALU.mult).then_inc(S("rwkv_ready"), 1)
            dve.wait_ge(*at_count("rwkv_ready"))
            for f in range(RF):
                dve.wait_ge(*at_count("bonus_full", f + 1))
                dve.tensor_tensor(BV[:, f, :], where["bonus", f][:, 0:T], XS[:, 8 + f, :], ALU.mult)\
                   .then_inc(S("bonus_done"), 1)
            link(dve.memset(H[:, :, :, :], 0.0))
            dve.wait_ge(*at_count("h0_full"))
            dve.tensor_copy(H[:, 1, :, :], where["h0", 0][:, :].rearrange("p (f n) -> p f n", f=RF))\
               .then_inc(S("h_init"), 1)
            dve.wait_ge(*at_count("h_init"))
            invf = [0]

            def inv_full():
                invf[0] += 1
                dve.wait_ge(*at_count("inv_full", invf[0]))

            for batch in BATCHES:
                first, nb = batch[0], len(batch)
                for bi, c in enumerate(batch):
                    for n, dst in enumerate((G1, G2)):
                        for par in range(2):
                            i = 6 * c + 2 * n + par
                            dve.wait_ge(*at_count("gram_full", i + 1))
                            dve.tensor_tensor(dst[0:C, bi, par * RF:(par + 1) * RF, :],
                                              where["gram", i][0:C, :].rearrange("p (f n) -> p f n", f=RF),
                                              bc(mask_pr[:, :, :].rearrange("p a t -> p (a t)"), 1, RF), ALU.mult)\
                               .then_inc(S("gram_done"), 1)
                    for par in range(2):
                        i = 6 * c + 4 + par
                        dve.wait_ge(*at_count("gram_full", i + 1))
                        dve.tensor_tensor(Tm[0:C, bi, par * RF:(par + 1) * RF, :],
                                          where["gram", i][0:C, 0:RF * C].rearrange("p (f n) -> p f n", f=RF),
                                          bc(lower[:, 0, :], 1, RF), ALU.mult).then_inc(S("gram_done"), 1)
                    dve.wait_ge(*at_count("gram_done", 6 * c + 6))
                    link(dve.tensor_tensor(Tt[0:C, bi, :, :], G2[0:C, bi, :, 0:C], bc(upper[:, 0, :], 1, RH), ALU.mult))
                    dve.scalar_tensor_tensor(Tm[0:C, bi, :, :], Tm[0:C, bi, :, :], -1.0,
                                             bc(ident[0:C, 0:C], 1, RH), ALU.mult, ALU.add)
                    dve.scalar_tensor_tensor(Tt[0:C, bi, :, :], Tt[0:C, bi, :, :], -1.0,
                                             bc(ident[0:C, 0:C], 1, RH), ALU.mult, ALU.add).then_inc(S("inv_ready"), 1)
                for lv in range(1, LEVELS):
                    for bi, c in enumerate(batch):
                        inv_full()
                        dve.tensor_tensor(Xm[0:C, bi, :, :],
                                          where["X", lv, c][0:C, :].rearrange("p (h n) -> p h n", h=RH),
                                          bc(lower[:, lv, :], 1, RH), ALU.mult).then_inc(S("inv_x"), 1)
                    for bi, c in enumerate(batch):
                        dve.wait_ge(*at_count("inv_ready", LEVELS * first + (lv - 1) * nb + bi + 1))
                        if lv < LEVELS - 1:
                            inv_full()
                            inv_full()
                            dve.tensor_tensor(Tm[0:C, bi, :, :], Tm[0:C, bi, :, :],
                                              where["Y", lv, c][0:C, :].rearrange("p (h n) -> p h n", h=RH),
                                              ALU.subtract).then_inc(S("inv_y"), 1)
                        else:
                            inv_full()
                        dve.tensor_tensor(Tt[0:C, bi, :, :], Tt[0:C, bi, :, :],
                                          where["Yt", lv, c][0:C, :].rearrange("p (h n) -> p h n", h=RH),
                                          ALU.subtract).then_inc(S("inv_ready"), 1)
                for bi, c in enumerate(batch):
                    g = 0 if c < N_PROMPT_CH else 1
                    dve.wait_ge(*at_count("seq_full", 4 * c + 1))
                    dve.tensor_copy(W1s[0:C, :], where["w1", c][0:C, :]).then_inc(S("w1_done"), 1)
                    dve.wait_ge(*at_count("seq_full", 4 * c + 2))
                    dve.tensor_scalar(Un[0:C, :], where["u", c][0:C, :], -1.0, None, ALU.mult).then_inc(S("u_done"), 1)
                    dve.wait_ge(*at_count("seq_full", 4 * c + 4))
                    for par in range(2):
                        rows = slice(64 * par, 64 * par + 64)
                        hs = H[rows, g, :, rows]
                        link(dve.tensor_tensor(hs, hs, where["dh", c][rows, :].rearrange("p (f n) -> p f n", f=RF)[:, :, rows],
                                               ALU.add))
                        mul = dve.tensor_tensor(hs, hs, dC[rows, :, c:c + 1].to_broadcast([64, RF, 64]), ALU.mult)
                    mul.then_inc(S("h_done"), 1)
                    dve.wait_ge(*at_count("h_done", c + 1))
            dve.wait_ge(*at_count("o_done", NCH))
            o3 = Osb[0:C].rearrange("p c h n -> p (c h) n")
            q3 = Osq[0:C].rearrange("p c h n -> p (c h) n")
            G40 = NCH * RH

            def wide(ap):
                return bc(ap, 2, RN)

            link(dve.tensor_reduce(stat[:, 0, :], o3, AX.X, ALU.add))
            link(dve.tensor_scalar(stat[:, 0, :], stat[:, 0, :], 1.0 / RN, None, ALU.mult))
            dve.tensor_tensor(o3, o3, wide(stat[:, 0, :]), ALU.subtract).then_inc(S("gn_centered"), 1)
            dve.wait_ge(*at_count("gn_squares"))
            dve.tensor_reduce(stat[:, 1, :], q3, AX.X, ALU.add).then_inc(S("gn_sums"), 1)
            dve.wait_ge(*at_count("gn_std"))
            link(dve.reciprocal(stat[:, 0, :], stat[:, 1, :]))
            dve.tensor_tensor(o3, o3, wide(stat[:, 0, :]), ALU.mult).then_inc(S("gn_done"), 1)
            dve.wait_ge(*at_count("ot_done", NCH))
            dve.wait_ge(*at_count("bonus_done", RF))
            dve.wait_ge(*at_count("lora_done", 3 * RF))
            for f in range(RF):
                dve.tensor_scalar(oT[:, f, :], oT[:, f, :], vcol("rwkv_gn_w", f), vcol("rwkv_gn_b", f), ALU.mult, ALU.add)\
                   .then_inc(S("gn_scaled"), 1)
            dve.wait_ge(*at_count("gn_scaled", RF))
            link(dve.tensor_tensor(oT[:, 0:RF, :], oT[:, 0:RF, :], BV, ALU.add))
            dve.tensor_tensor(oT[:, 0:RF, :], oT[:, 0:RF, :], GT, ALU.mult).then_inc(S("rwkv_out"), 1)

            def log_sigmoid(a, x, out):
                dve.tensor_scalar(out, x, 0.0, None, ALU.min).then_inc(S(a["name"] + "_min"), 1)
                dve.wait_ge(*at_count(a["name"] + "_softplus"))
                dve.wait_ge(*at_count(a["name"] + "_min"))
                link(dve.tensor_tensor(out, out, a["E"], ALU.subtract))

            def attention(a):
                n_, F, NH = a["name"], a["F"], a["heads"]
                pars = NH // F
                W = P // pars
                dve.memset(a["S"][:, 0], 0.0).then_inc(S(n_ + "_s_zero"), 1)
                dve.memset(a["S"][:, 1], 0.0).then_inc(S(n_ + "_s_zero"), 1)
                for f in range(F):
                    dve.tensor_tensor_scan(a["b"][:, f, :], reset[:, :], a["Z"][:, f, :], 0.0, ALU.mult, ALU.add)\
                       .then_inc(S(n_ + "_b"), 1)
                dve.wait_ge(*at_count(n_ + "_b", F))

                def select(lv):
                    for c in range(NCH):
                        for par in range(pars):
                            i = lv * NCH * pars + c * pars + par
                            dve.wait_ge(*at_count(n_ + "_sc_full", i + 1))
                            src = where[n_, "sc", i][0:C, 0:F * C].rearrange("p (f t) -> p f t", f=F)
                            dst = a["Sc"][0:C, c, par * F:(par + 1) * F, :]
                            if lv == 0:
                                ins_ = dve.tensor_tensor(dst, src, bc(ident[0:C, 0:C], 1, F), ALU.mult)
                            else:
                                dve.wait_ge(*at_count(n_ + "_sc", i + 1 - NCH * pars))
                                ins_ = dve.copy_predicated(dst, bc(upper[:, lv - 1, :].bitcast(I32), 1, F), src)
                            ins_.then_inc(S(n_ + "_sc"), 1)

                for lv in range(1, LEVELS + 1):
                    L = 1 << lv
                    hl = L // 2

                    def blocks(x):
                        return x.rearrange("p f t -> p (f t)").rearrange("p (n l) -> p n l", l=L)

                    zb = (a["Z"], a["KD"])[lv % 2]
                    bb, eb, z_, q_, k_ = blocks(a["b"]), blocks(a["E"]), blocks(zb), blocks(a["q"]), blocks(a["k"])
                    nb_ = F * T // L
                    if lv > 1:
                        dve.wait_ge(*at_count(n_ + "_z", lv))
                    dve.tensor_tensor(eb, bb, bb[:, :, hl - 1:hl].to_broadcast([P, nb_, L]), ALU.subtract)\
                       .then_inc(S(n_ + "_dist"), 1)
                    if lv >= 2:
                        select(lv - 2)
                    dve.wait_ge(*at_count(n_ + "_e", lv))
                    dve.tensor_tensor(z_[:, :, hl:L], eb[:, :, hl:L], q_[:, :, hl:L], ALU.mult)
                    dve.tensor_tensor(z_[:, :, 0:hl], eb[:, :, 0:hl], k_[:, :, 0:hl], ALU.mult).then_inc(S(n_ + "_z"), 1)
                select(LEVELS - 1)
                select(LEVELS)
                dve.wait_ge(*at_count(n_ + "_z", LEVELS + 1))
                b4 = a["b"].rearrange("p f t -> p (f t)").rearrange("p (n l) -> p n l", l=C)
                kd = a["KD"].rearrange("p f t -> p (f t)").rearrange("p (n l) -> p n l", l=C)
                dve.tensor_tensor(kd, b4, b4[:, :, C - 1:C].to_broadcast([P, F * NCH, C]), ALU.subtract)\
                   .then_inc(S(n_ + "_dist"), 1)
                dve.wait_ge(*at_count(n_ + "_e", LEVELS + 1))
                dve.tensor_tensor(a["Z"], a["E"], a["q"], ALU.mult)
                dve.tensor_copy(ends[:, 0:F, :], a["E"].rearrange("p f (c t) -> p f c t", c=NCH)[:, :, :, C - 1])
                dve.wait_ge(*at_count(n_ + "_e", LEVELS + 2))
                dve.tensor_tensor(a["KD"], a["KD"], a["k"], ALU.mult).then_inc(S(n_ + "_qk"), 1)
                dve.wait_ge(*at_count(n_ + "_qk"))
                dve.wait_ge(*at_count(n_ + "_state_in", 16 * pars))
                per = min(4 // pars, F)
                for c in range(NCH):
                    g = 0 if c < N_PROMPT_CH else 1
                    if c:
                        dve.wait_ge(*at_count(n_ + "_s", c))
                    for k0 in range(0, F, per):
                        i = c * (F // per) + k0 // per
                        dve.wait_ge(*at_count(n_ + "_ds_full", i + 1))
                        ps = where[n_, "ds", i]
                        for k in range(per):
                            f = k0 + k
                            for par in range(pars):
                                rows = slice(W * par, W * par + W)
                                st = a["S"][rows, g, f, par * P:(par + 1) * P]
                                up = dve.scalar_tensor_tensor(st, st, ends[rows, f, c:c + 1],
                                                              ps[rows, (k * pars + par) * P:(k * pars + par + 1) * P],
                                                              ALU.mult, ALU.add)
                    up.then_inc(S(n_ + "_s"), 1)
                dve.wait_ge(*at_count(n_ + "_rms", NH))
                link(dve.reciprocal(a["sq"], a["sq"]))
                link(dve.tensor_tensor(a["O"], a["O"], a["sq"], ALU.mult))
                dve.scalar_tensor_tensor(a["O"], a["O"], vcol("gla_norm_w" if n_ == "gla" else "hgrn_norm_w"), a["gate"],
                                         ALU.mult, ALU.mult).then_inc(S(n_ + "_out"), 1)

            def layer_norm(n_, g_, b_):
                r_, q_ = res_of(n_), sq_of(n_)
                dve.wait_ge(*at_count(n_ + "_ln_full", 1))
                dve.scalar_tensor_tensor(r_, bc(where[n_, "sum"][:, 0:T], 1, KC), -1.0 / D, r_, ALU.mult, ALU.add)\
                   .then_inc(S(n_ + "_centered"), 1)
                dve.wait_ge(*at_count(n_ + "_std"))
                dve.wait_ge(*at_count(n_ + "_centered"))
                link(dve.reciprocal(mean[:, :], mean[:, :]))
                link(dve.tensor_tensor(r_, r_, bc(mean[:, :], 1, KC), ALU.mult))
                for k in range(KC):
                    ins_ = dve.tensor_scalar(xT[:, k, :], r_[:, k, :], vcol(g_, k), vcol(b_, k), ALU.mult, ALU.add)
                ins_.then_inc(S(n_ + "_ln"), 1)

            def residual(full, taken, name):
                for j in range(KC):
                    dve.wait_ge(*at_count(full, j + 1))
                    dve.scalar_tensor_tensor(res[:, j, :], xT[:, j, :], ALPHA, where[name, j][:, 0:T],
                                             ALU.mult, ALU.add).then_inc(S(taken), 1)
                dve.wait_ge(*at_count(taken, KC))

            log_sigmoid(gla, gla["b"], gla["KD"])
            dve.tensor_scalar(gla["Z"], gla["KD"], 1.0 / GLA_TAU, None, ALU.mult).then_inc(S("gla_z"), 1)
            dve.wait_ge(*at_count("gla_z"))
            attention(gla)
            residual("out_ab_full", "ab_res", "out_ab")
            layer_norm("ab", "ln_ab_g", "ln_ab_b")
            for j in range(FC):
                dve.wait_ge(*at_count("h3_full", j + 1))
                dve.wait_ge(*at_count("h1_done", j + 1))
                dve.tensor_tensor(ff_g[:, j, :], ff_s[:, j % 4, :], where["h3", j][:, 0:T], ALU.mult)\
                   .then_inc(S("ffn_g"), 1)
            dve.wait_ge(*at_count("ab_ln"))
            residual("w2_full", "ffn_res", "w2")
            layer_norm("ffn", "ln_ffn_g", "ln_ffn_b")
            dve.wait_ge(*at_count("in_c_done", 16))
            log_sigmoid(hgrn, hf, hgrn["KD"])
            for k in range(HH):
                ins_ = dve.tensor_scalar(hgrn["Z"][:, k, :], hgrn["KD"][:, k, :], lbw[:, 4, k:k + 1], None, ALU.add)
            ins_.then_inc(S("hgrn_gap"), 1)
            dve.wait_ge(*at_count("hgrn_gap"))
            link(dve.tensor_scalar(hgrn["KD"], hgrn["Z"], 0.0, None, ALU.max))
            dve.wait_ge(*at_count("hgrn_softplus", 2))
            link(dve.tensor_tensor(hgrn["Z"], hgrn["KD"], hgrn["E"], ALU.add))
            dve.wait_ge(*at_count("hgrn_sig"))
            for k in range(HH):
                dve.tensor_scalar(hgrn["Z"][:, k, :], hgrn["Z"][:, k, :], lbw[:, 3, k:k + 1], 0.0, ALU.add, ALU.min)
                ins_ = dve.tensor_scalar(hf[:, k, :], hf[:, k, :], lbw[:, 5, k:k + 1], None, ALU.mult)
            ins_.then_inc(S("hgrn_z"), 1)
            dve.wait_ge(*at_count("hgrn_z"))
            attention(hgrn)
            residual("out_c_full", "c_res", "out_c")
            layer_norm("c", "ln_c_g", "ln_c_b")

            dve.wait_ge(*at_count("c_ln"))
            link(dve.memset(lg[:, :, :], 0.0))
            dve.memset(xtok[:, 2, :], 0.0).then_inc(S("xtok_zero"), 1)
            for k in range(KC):
                dve.tensor_scalar(acc[:, k, :], xT[:, k, :], ALPHA, None, ALU.mult)
            for i, (t0, n) in enumerate(TILES):
                dve.wait_ge(*at_count("logit_full", i + 1))
                dve.tensor_copy(lg[0:n, i, :], where["logit", i][0:n, 0:NE]).then_inc(S("logits_done"), 1)
            dve.wait_ge(*at_count("logits_done", 3))
            sel, pr_, wp = rt[:, 0], rt[:, 1], rt[:, 2]
            t3 = rt[:, 3, :, 0:1].rearrange("p i a -> p (i a)")
            t4 = rt[:, 4, :, 0:1].rearrange("p i a -> p (i a)")
            link(dve.tensor_reduce(t3, lg[:, :, :], AX.X, ALU.max))
            dve.tensor_tensor(lg[:, :, :], lg[:, :, :], rt[:, 3, :, 0:1].to_broadcast([P, 3, NE]), ALU.subtract)\
               .then_inc(S("logits_shifted"), 1)
            dve.wait_ge(*at_count("router_exp"))
            link(dve.tensor_reduce(t3, pr_, AX.X, ALU.add))
            link(dve.reciprocal(t4, t3))
            link(dve.tensor_tensor(pr_, pr_, rt[:, 4, :, 0:1].to_broadcast([P, 3, NE]), ALU.mult))
            pj = bc(pr_, 2, NE)
            pi = bc(pr_, 3, NE)
            g4 = pair[:, 0].rearrange("p i (a b) -> p i a b", a=NE)
            e4 = pair[:, 1].rearrange("p i (a b) -> p i a b", a=NE)
            dve.tensor_tensor(g4, pj, pi, ALU.is_gt)
            link(dve.tensor_tensor(e4, pj, pi, ALU.is_equal))
            link(dve.tensor_tensor(e4, e4, bc(jlt[:, :, :], 1, 3), ALU.mult))
            link(dve.tensor_tensor(g4, g4, e4, ALU.add))
            link(dve.tensor_reduce(rt[:, 5], g4, AX.X, ALU.add))
            link(dve.tensor_scalar(sel, rt[:, 5], 1.5, None, ALU.is_lt))
            link(dve.memset(rt[64:P, 0, 2, :], 0.0))
            link(dve.tensor_tensor(wp, sel, pr_, ALU.mult))
            link(dve.tensor_reduce(t3, wp, AX.X, ALU.add))
            link(dve.tensor_scalar(t3, t3, 1e-30, None, ALU.max))
            link(dve.reciprocal(t4, t3))
            link(dve.tensor_tensor(wts[:, :, :].rearrange("p e i -> p i e"), wp, rt[:, 4, :, 0:1].to_broadcast([P, 3, NE]), ALU.mult))
            dve.tensor_scalar(rt[:, 6], sel, -1.0, 1e6, ALU.add, ALU.mult).then_inc(S("chosen"), 1)
            dve.wait_ge(*at_count("chosen"))
            for i in range(3):
                dve.wait_ge(*at_count("pos_full", i + 1))
                dve.tensor_tensor(pos[:, :, i:i + 1].rearrange("p e a -> p (e a)"), where["pos", i][:, 0:NE],
                                  rt[:, 6, i, :], ALU.add).then_inc(S("pos_done"), 1)
            dve.wait_ge(*at_count("pos_full", 4))
            dve.tensor_copy(cnt[:, :], where["count", 0][:, 0:NE]).then_inc(S("pos_done"), 1)
            dve.wait_ge(*at_count("pos_done", 4))
            for r_ in range(1, MAX_BLOCKS):
                ins_ = dve.tensor_scalar(cand[:, 0, (r_ - 1) * NE:r_ * NE], cnt[:, :], BLK * r_ + 0.5, None, ALU.is_gt)
            link(ins_)
            link(dve.tensor_tensor_scan(cand[:, 1, :], ones[:, 0:NX], cand[:, 0, :], 0.0, ALU.mult, ALU.add))
            link(dve.tensor_tensor(cand[:, 1, :], cand[:, 1, :], cand[:, 0, :], ALU.mult))
            link(dve.tensor_scalar(cand[:, 1, :], cand[:, 1, :], -1.0, None, ALU.add))
            for src, dst in ((2, extra_i[:, 0, :]), (3, bases[:, :])):
                link(dve.tensor_tensor(compact[:, :, :], bc(cand[:, 1, :], 1, NX), bc(slots[:, 0:NX], 2, NX), ALU.is_equal))
                link(dve.tensor_tensor(compact[:, :, :], compact[:, :, :], bc(cand[:, src, :], 1, NX), ALU.mult))
                link(dve.tensor_reduce(cand[:, 4, :], compact[:, :, :], AX.X, ALU.add))
                link(dve.tensor_copy(dst, cand[:, 4, :]))
            link(dve.tensor_reduce(cand[:, 5, 0:1], cand[:, 0, :], AX.X, ALU.add))
            dve.tensor_copy(n_extra[:, 0:1], cand[:, 5, 0:1]).then_inc(S("extras_known"), 1)

            def weight_rest(n, i):
                dve.wait_ge(S("e_hi"), HALVES * n + i + 1)
                dve.tensor_tensor(w_lo[:, i % UNITS, :], moe_ring[:, MOE_RING - 1 - i % MOE_RING, :], w_hi[:, i % UNITS, :], ALU.subtract)\
                   .then_inc(S("e_lo"), 1)

            def add_rows(n, k, b):
                dve.wait_ge(S("e_scatter"), KC * (n - 1) + k + 1)
                dve.tensor_tensor(acc[:, k, :], acc[:, k, :], b[:, 0:T], ALU.add).then_inc(S("e_added"), 1)

            def expert_block(n, e, j_extra):
                later = not isinstance(n, int)
                if later:
                    dve.wait_ge(S("e_pickt_full"), n)
                dve.tensor_copy(wcur[:, :].unsqueeze(1), wts[:, bass.ds(e, 1), :]).then_inc(S("e_col"), 1)
                if j_extra is None:
                    dve.tensor_copy(cur[:, :].unsqueeze(1), pos[:, bass.ds(e, 1), :]).then_inc(S("e_col"), 1)
                else:
                    dve.tensor_tensor(cur[:, :].unsqueeze(1), pos[:, bass.ds(e, 1), :],
                                      bases[:, bass.ds(j_extra, 1)].unsqueeze(2).to_broadcast([P, 1, 3]), ALU.subtract)\
                       .then_inc(S("e_col"), 1)
                dve.wait_ge(S("e_col"), n * 2 + 2)
                for i in range(3):
                    ins_ = dve.tensor_scalar(pick[:, i, :], slots[:, :], cur[:, i:i + 1], None, ALU.is_equal)
                ins_.then_inc(S("e_map"), 1)
                dve.wait_ge(S("e_map"), n + 1)
                for i in range(3):
                    ins_ = dve.tensor_scalar(pickw[:, i, :], pick[:, i, :], wcur[:, i:i + 1], None, ALU.mult)
                ins_.then_inc(S("e_pick"), 1)

                def hidden(s):
                    dve.wait_ge(S("e_silu"), n * STRIPS + s + 1)
                    dve.wait_ge(S("e_used"), n * HALVES + 2 * UP3[s] + 2)
                    if s:
                        dve.wait_ge(S("e_gt_full"), n * STRIPS + s)
                    dve.tensor_tensor(eg[:, :], eh[:, s % 2, :], E_H3[s % 2][:, 0:SC], ALU.mult).then_inc(S("e_g"), 1)

                def hidden_rest(s):
                    dve.wait_ge(S("e_gt_hi"), n * STRIPS + s + 1)
                    dve.tensor_tensor(gt_lo[:, :, :], E_SCR[0][:, 0:2 * BLK].rearrange("p (j n) -> p j n", j=2),
                                      gt_hi[:, :, :], ALU.subtract).then_inc(S("e_gt"), 1)

                weight_rest(n, 0)
                weight_rest(n, 1)
                for half in range(2):
                    dve.wait_ge(S("e_rows_hi"), n * 2 + half + 1)
                    dve.tensor_tensor(xe_lo[:, 4 * half:4 * half + 4, :], E_SCR[half][:, :].rearrange("p (k n) -> p k n", k=4),
                                      xe_hi[:, 4 * half:4 * half + 4, :], ALU.subtract).then_inc(S("e_rows"), 1)
                    weight_rest(n, 2 + half)
                weight_rest(n, 4)
                weight_rest(n, 5)
                hidden(0)
                weight_rest(n, 6)
                weight_rest(n, 7)
                for s in range(1, STRIPS):
                    weight_rest(n, 6 * s + 2)
                    weight_rest(n, 6 * s + 3)
                    hidden_rest(s - 1)
                    weight_rest(n, 6 * s + 4)
                    weight_rest(n, 6 * s + 5)
                    hidden(s)
                    if s < STRIPS - 1:
                        weight_rest(n, 6 * s + 6)
                        weight_rest(n, 6 * s + 7)
                    if later and s <= KC:
                        add_rows(n, s - 1, E_SCR[1])
                hidden_rest(STRIPS - 1)

            def last_rows(n):
                for k in range(KC):
                    add_rows(n, k, bank[k % 4])
                dve.wait_ge(S("e_added"), KC * n)

            expert_loops(dve, expert_block, last_rows)
            layer_norm("moe", "ln_moe_g", "ln_moe_b")

        @block.scalar
        def _(act):
            chain = [0]

            def link(ins_):
                chain[0] += 1
                ins_.then_inc(S("act_chain"), 1)
                act.wait_ge(S("act_chain"), chain[0])

            for table, row, rows, ap in vloads:
                act.dma_start(vrow[row:row + rows, table, :], ap).then_inc(S("vectors_in"), 16)
            for t in range(2):
                act.wait_ge(*at_count("vec_full", t + 1))
                o = 0 if t == 0 else 91
                act.activation(vec[:, o:o + at[t]], where["vec", t][:, 0:at[t]], ACT.Copy).then_inc(S("vec_done"), 1)
            for k in range(KC):
                act.wait_ge(*at_count("x_full", k + 1))
                act.activation(xT[:, k, :], where["x", k][:, 0:T], ACT.Copy).then_inc(S("x_done"), 1)
            act.wait_ge(*at_count("lb_in"))
            link(act.activation(lbw[:, 2, :], lbw[:, 0, :], ACT.Exp))
            act.activation(lbw[:, 6, :], lbw[:, 1, :], ACT.Exp).then_inc(S("lb_exp"), 1)
            act.wait_ge(*at_count("lb_sum", 1))
            act.activation(lbw[:, 7, :], lbw[:, 7, :], ACT.Ln).then_inc(S("lb_ln"), 1)
            act.wait_ge(*at_count("pr_zero"))
            dests = [None] * RPC + [gq[:, 0], gq[:, 1], gk[:, 0], gk[:, 1]] + [gv[:, i] for i in range(4)] + \
                    [gog[:, i] for i in range(4)]
            for j, d in enumerate(dests):
                act.wait_ge(*at_count("ab_full", j + 1))
                b = where["ab", j]
                if d is None:
                    act.activation(PR[:, j, 1:T_PROMPT + 1], b[:, 0:T_PROMPT], ACT.Copy)
                    act.activation(PR[:, j, T_PROMPT + 2:T + 2], b[:, T_PROMPT:T], ACT.Copy).then_inc(S("ab_done"), 1)
                else:
                    fn = ACT.Silu if j >= RPC + 8 else ACT.Copy
                    act.activation(d, b[:, 0:T], fn, scale=GDK ** -0.5 if j < RPC + 2 else 1.0).then_inc(S("ab_done"), 1)
            act.wait_ge(*at_count("ab_full", len(dests) + 1))
            act.activation(gz_s[:, :], where["ab", len(dests)][0:GR, 0:T], ACT.Copy).then_inc(S("ab_done"), 1)
            act.wait_ge(*at_count("xs", RPC))
            act.activation(XS[0:64, 12, :], XS[0:64, 12, :], ACT.Tanh).then_inc(S("lora_in"), 1)
            act.activation(XS[:, 13, :], XS[:, 13, :], ACT.Sigmoid).then_inc(S("lora_in"), 1)
            act.wait_ge(*at_count("last_copied", 2))
            for n in range(3 * RF + 2):
                act.wait_ge(*at_count("lora_full", n + 1))
                f, b = n % RF, where["lora", n][:, 0:T]
                if n < RF:
                    ins_ = act.activation(lw[:, f, :], b, ACT.Sigmoid, bias=vcol("rwkv_w0", f))
                elif n < 2 * RF:
                    ins_ = act.activation(aT[:, f, :], b, ACT.Sigmoid, bias=vcol("rwkv_a0", f))
                elif n < 3 * RF:
                    ins_ = act.activation(GT[:, f, :], b, ACT.Copy)
                else:
                    ins_ = act.activation(gla_b[:, f, :], b, ACT.Identity, bias=vcol("gla_gate_b", f))
                ins_.then_inc(S("lora_done"), 1)
            for g in range(2):
                act.wait_ge(*at_count("last_full", g + 1))
                act.activation(lrow[:, g, :], where["last", g][0:RPC, 0:P], ACT.Copy).then_inc(S("last_rows"), 1)
            act.wait_ge(*at_count("decay_sums"))
            act.activation(s2, s1, ACT.Exp).then_inc(S("decay_exp"), 1)
            act.wait_ge(*at_count("decay_exp", 1))
            act.activation(s1, bT, ACT.Exp).then_inc(S("decay_exp"), 1)
            act.activation(lw, bT, ACT.Exp, scale=-1.0).then_inc(S("decay_exp"), 1)
            for f in range(RF):
                act.wait_ge(*at_count("kk_full", f + 1))
                act.activation(QT[:, f, :], where["kk", f][:, 0:T], ACT.Sqrt).then_inc(S("kk_norm"), 1)
            for batch in BATCHES:
                for bi, c in enumerate(batch):
                    for n, dst in enumerate((TV, TQ, TK)):
                        act.wait_ge(*at_count("tm_full", 3 * c + n + 1))
                        act.activation(dst[0:C, bi, :], where["tm", 3 * c + n][0:C, :], ACT.Copy).then_inc(S("tm_done"), 1)
                for bi, c in enumerate(batch):
                    act.wait_ge(*at_count("seq_full", 4 * c + 3))
                    act.activation(Osb[0:C, c].rearrange("p h n -> p (h n)"), where["o", c][0:C, :], ACT.Copy)\
                       .then_inc(S("o_done"), 1)
            for g in range(2):
                act.wait_ge(*at_count("hout_full", g + 1))
                act.activation(Hout[:, g].rearrange("p f n -> p (f n)"), where["hout", g][:, :], ACT.Copy)\
                   .then_inc(S("hout_done"), 1)
            act.wait_ge(*at_count("gn_centered"))
            o3 = Osb[0:C].rearrange("p c h n -> p (c h n)")
            act.activation(Osq[0:C].rearrange("p c h n -> p (c h n)"), o3, ACT.Square).then_inc(S("gn_squares"), 1)
            act.wait_ge(*at_count("gn_sums"))
            act.activation(stat[:, 1, :], stat[:, 1, :], ACT.Sqrt, bias=eps_gn[0:C, :], scale=1.0 / RN).then_inc(S("gn_std"), 1)
            for c in range(NCH):
                act.wait_ge(*at_count("ot_full", c + 1))
                act.activation(oT[:, 0:RF, chunk(c)], where["ot", c][:, 0:RF * C].rearrange("p (f t) -> p f t", f=RF),
                               ACT.Copy).then_inc(S("ot_done"), 1)

            def softplus_neg_abs(a, x):
                link(act.activation(a["E"], x, ACT.Abs))
                link(act.activation(a["E"], a["E"], ACT.Exp, scale=-1.0))
                act.activation(a["E"], a["E"], ACT.Ln, bias=1.0).then_inc(S(a["name"] + "_softplus"), 1)

            def attention(a):
                n_, F, NH = a["name"], a["F"], a["heads"]
                pars = NH // F
                for lv in range(1, LEVELS + 1):
                    L = 1 << lv
                    hl = L // 2
                    eb = a["E"].rearrange("p f t -> p (f t)").rearrange("p (n l) -> p n l", l=L)
                    act.wait_ge(*at_count(n_ + "_dist", lv))
                    act.activation(eb[:, :, hl:L], eb[:, :, hl:L], ACT.Exp)
                    act.activation(eb[:, :, 0:hl], eb[:, :, 0:hl], ACT.Exp, scale=-1.0).then_inc(S(n_ + "_e"), 1)
                act.wait_ge(*at_count(n_ + "_dist", LEVELS + 1))
                act.activation(a["E"], a["b"], ACT.Exp).then_inc(S(n_ + "_e"), 1)
                act.activation(a["KD"], a["KD"], ACT.Exp, scale=-1.0).then_inc(S(n_ + "_e"), 1)
                tv = 0
                for c in range(NCH):
                    for dst, cnt_ in ((a["TV"], NH), (a["TK"], F)):
                        for k0 in range(0, cnt_, 4):
                            m_ = min(4, cnt_ - k0)
                            tv += 1
                            act.wait_ge(*at_count(n_ + "_tm_full", tv))
                            act.activation(dst[0:C, k0 * P:(k0 + m_) * P], where[n_, "tm", tv - 1][0:C, 0:m_ * P], ACT.Copy)\
                               .then_inc(S(n_ + "_tm"), 1)
                    act.wait_ge(*at_count(n_ + "_o_full", c + 1))
                    act.activation(a["O"][:, :, chunk(c)],
                                   where[n_, "o", c][:, 0:NH * C].rearrange("p (h t) -> p h t", h=NH), ACT.Copy)\
                       .then_inc(S(n_ + "_o"), 1)
                act.wait_ge(*at_count(n_ + "_o", NCH))
                act.activation(a["sq"], a["O"], ACT.Square).then_inc(S(n_ + "_osq"), 1)
                for hh in range(NH):
                    act.wait_ge(*at_count(n_ + "_rms_full", hh + 1))
                    act.activation(a["sq"][:, hh, :], where[n_, "rms", hh][:, 0:T], ACT.Sqrt,
                                   bias=eps_norm[:, :], scale=1.0 / a["vdim"]).then_inc(S(n_ + "_rms"), 1)

            def layer_norm(n_):
                act.wait_ge(*at_count(n_ + "_centered"))
                act.activation(sq_of(n_), res_of(n_), ACT.Square).then_inc(S(n_ + "_sq"), 1)
                act.wait_ge(*at_count(n_ + "_ln_full", 2))
                act.activation(mean[:, :], where[n_, "sqs"][:, 0:T], ACT.Sqrt, bias=eps_norm[:, :], scale=1.0 / D)\
                   .then_inc(S(n_ + "_std"), 1)

            softplus_neg_abs(gla, gla["b"])
            attention(gla)
            layer_norm("ab")
            for j in range(FC):
                act.wait_ge(*at_count("h1_full", j + 1))
                if j >= 4:
                    act.wait_ge(*at_count("ffn_g", j - 3))
                act.activation(ff_s[:, j % 4, :], where["h1", j][:, 0:T], ACT.Silu).then_inc(S("h1_done"), 1)
            layer_norm("ffn")
            for j in range(4 * KC):
                act.wait_ge(*at_count("in_c_full", j + 1))
                dst = (hq, hf, hi, hg)[j // KC][:, j % KC, :]
                act.activation(dst, where["in_c", j][:, 0:T], ACT.Silu if j // KC in (0, 3) else ACT.Copy)\
                   .then_inc(S("in_c_done"), 1)
            softplus_neg_abs(hgrn, hf)
            act.wait_ge(*at_count("hgrn_min"))
            act.activation(hf, hf, ACT.Sigmoid, scale=-1.0).then_inc(S("hgrn_sig"), 1)
            act.wait_ge(*at_count("hgrn_gap"))
            softplus_neg_abs(hgrn, hgrn["Z"])
            attention(hgrn)
            layer_norm("c")
            act.wait_ge(*at_count("xtok_zero"))
            for j in range(6):
                act.wait_ge(*at_count("xtok_full", j + 1))
                n = TILES[j // 2][1]
                act.activation(xtok[0:n, j // 2, (j % 2) * 512:(j % 2 + 1) * 512], where["xtok", j][0:n, :], ACT.Copy)\
                   .then_inc(S("xtok_done"), 1)
            act.wait_ge(*at_count("logits_shifted"))
            act.activation(rt[:, 1], lg[:, :, :], ACT.Exp).then_inc(S("router_exp"), 1)

            def weight_rounded(n, i):
                act.wait_ge(S(f"moe_in{i % MOE_RING}"), 16 * (n * (HALVES // MOE_RING) + i // MOE_RING + 1))
                if i >= UNITS or not isinstance(n, int):
                    act.wait_ge(S("e_used"), n * HALVES + i - UNITS + 1)
                act.activation(w_hi[:, i % UNITS, :], moe_ring[:, MOE_RING - 1 - i % MOE_RING, :], ACT.Copy).then_inc(S("e_hi"), 1)

            def outputs(n):
                act.wait_ge(S("e_used"), n * HALVES)
                for half in range(2):
                    act.activation(ey[:, half * 512:(half + 1) * 512], E_Y[half][:, :], ACT.Copy).then_inc(S("e_y"), 1)

            def expert_block(n, e, j_extra):
                later = not isinstance(n, int)

                def silu(s):
                    act.wait_ge(S("e_used"), n * HALVES + 2 * UP1[s] + 2)
                    if s >= 2:
                        act.wait_ge(S("e_g"), n * STRIPS + s - 1)
                    act.activation(eh[:, s % 2, :], E_H1[s % 2][:, 0:SC], ACT.Silu).then_inc(S("e_silu"), 1)

                def hidden_rounded(s):
                    act.wait_ge(S("e_gt_full"), n * STRIPS + s + 1)
                    act.activation(gt_hi[:, :, :], E_SCR[0][:, 0:2 * BLK].rearrange("p (j n) -> p j n", j=2), ACT.Copy)\
                       .then_inc(S("e_gt_hi"), 1)

                for i in range(4):
                    weight_rounded(n, i)
                if later:
                    outputs(n)
                for half in range(2):
                    act.wait_ge(S("e_gather_full"), n * 2 + half + 1)
                    act.activation(xe_hi[:, 4 * half:4 * half + 4, :], E_SCR[half][:, :].rearrange("p (k n) -> p k n", k=4),
                                   ACT.Copy).then_inc(S("e_rows_hi"), 1)
                weight_rounded(n, 4)
                weight_rounded(n, 5)
                silu(0)
                weight_rounded(n, 6)
                weight_rounded(n, 7)
                for s in range(1, STRIPS):
                    weight_rounded(n, 6 * s + 2)
                    weight_rounded(n, 6 * s + 3)
                    silu(s)
                    hidden_rounded(s - 1)
                    weight_rounded(n, 6 * s + 4)
                    weight_rounded(n, 6 * s + 5)
                    if s < STRIPS - 1:
                        weight_rounded(n, 6 * s + 6)
                        weight_rounded(n, 6 * s + 7)
                hidden_rounded(STRIPS - 1)
                act.wait_ge(S("e_pickt_full"), n + 1)
                act.activation(pickT[:, :], E_SCR[1][:, 0:T], ACT.Copy).then_inc(S("e_pickt"), 1)

            expert_loops(act, expert_block, outputs)
            layer_norm("moe")
            for j in range(6):
                act.wait_ge(*at_count("y_full", j + 1))
                n = TILES[j // 2][1]
                act.activation(xtok[0:n, j // 2, (j % 2) * 512:(j % 2 + 1) * 512], where["y", j][0:n, :], ACT.Copy)\
                   .then_inc(S("y_done"), 1)

        @block.gpsimd
        def _(pool):
            chain = [0]

            def link(ins_):
                chain[0] += 1
                ins_.then_inc(S("pool_chain"), 1)
                pool.wait_ge(S("pool_chain"), chain[0])

            def keep(m, pattern, base, mult, op=ALU.is_ge):
                link(pool.affine_select(out=m, in_=m, compare_op=op, fill=0.0, base=base, pattern=pattern,
                                        channel_multiplier=mult))

            for m_ in (ident, ones, utri):
                link(pool.memset(m_[:, :], 1.0))
            keep(ident[:, :], [[-1, P]], 0, 1, ALU.is_equal)
            keep(utri[:, :], [[1, P]], -1, -1)
            link(pool.memset(bdones[:, :], 0.0))
            for par in range(2):
                rows = slice(64 * par, 64 * par + 64)
                link(pool.memset(bdones[rows, rows], 1.0))
            link(pool.memset(mask_pr[:, :, :], 1.0))
            keep(mask_pr[:, 0, :], [[1, C]], -1, -1)
            keep(mask_pr[:, 1, :], [[1, C]], 0, -1)
            link(pool.memset(lower[:, :, :], 1.0))
            link(pool.memset(upper[:, :, :], 1.0))
            for lv in range(LEVELS):
                L, n = 2 << lv, C >> (lv + 1)
                lo = lower[:, lv, :].rearrange("p (n l) -> p n l", l=L)
                up = upper[:, lv, :].rearrange("p (n l) -> p n l", l=L)
                keep(lo, [[-L, n], [0, L]], -(L // 2), 1)
                keep(lo, [[L, n], [0, L]], L - 1, -1)
                keep(lo, [[0, n], [-1, L]], L // 2 - 1, 0)
                keep(up, [[-L, n], [0, L]], 0, 1)
                keep(up, [[L, n], [0, L]], L // 2 - 1, -1)
                keep(up, [[0, n], [1, L]], -(L // 2), 0)
            link(pool.memset(reset[:, :], 1.0))
            link(pool.memset(reset[:, 0:T:C], 0.0))
            link(pool.memset(jlt[:, :, :], 1.0))
            keep(jlt[:, :, :], [[1, NE], [-1, NE]], -1, 0)
            link(pool.memset(eps_gn[:, :], GN_EPS))
            link(pool.memset(eps_norm[:, :], NORM_EPS))
            link(pool.iota(slots[:, :], [[1, BLK]], base=0, channel_multiplier=0, allow_small_or_imprecise_dtypes=True))
            link(pool.iota(cand[:, 2, :].rearrange("p (r e) -> p r e", e=NE), [[0, MAX_BLOCKS - 1], [1, NE]], base=0,
                           channel_multiplier=0, allow_small_or_imprecise_dtypes=True))
            link(pool.iota(cand[:, 3, :].rearrange("p (r e) -> p r e", e=NE), [[BLK, MAX_BLOCKS - 1], [0, NE]], base=BLK,
                           channel_multiplier=0, allow_small_or_imprecise_dtypes=True))
            pool.memset(mean[:, :], 1.0).then_inc(S("masks"), 1)
            link(pool.memset(wup[:, :], 0.0))
            pool.memset(aup[:, :], 0.0).then_inc(S("lora_zero"), 1)
            link(pool.memset(state_nat, 0.0))
            pool.memset(PR[:, :, 0:1], 0.0).then_inc(S("pr_zero"), 1)

        @block.sync
        def _(sp):
            xp = ins["x_prompt"][0]
            sp.dma_start(xst[:, 0, :], xp[0:P, :]).then_inc(S("x_in"), 16)
            sp.dma_start(xst[:, 1, :], xp[P:2 * P, :]).then_inc(S("x_in"), 16)
            sp.dma_start(xst[0:T_SAMPLE, 2, :], ins["x_sample"][0]).then_inc(S("x_in"), 16)

            def load_tile(i):
                src, n, _, _ = tiles[i]
                if i >= DENSE_RING:
                    _, _, name, value = tiles[i - DENSE_RING]
                    sp.wait_ge(*at_count(name, value))
                sp.dma_start(tile_of(i)[:, 0:n, :], src).then_inc(S(f"tile_in{i % DENSE_RING}"), 16)

            for i in range(DENSE_RING):
                load_tile(i)
            sp.wait_ge(*at_count("lora_zero", 1))
            sp.dma_start(gz_w[:, :, :], w_in[:, GZ0:GZ0 + GR].rearrange("(k p) n -> p k n", p=P)).then_inc(S("small_in"), 16)
            sp.dma_start(router[:, :, :], ins["moe_router"][0].rearrange("(k p) n -> p k n", p=P)).then_inc(S("small_in"), 16)
            sp.dma_start(wup[0:64, :], ins["rwkv_w_up"][0]).then_inc(S("small_in"), 16)
            sp.dma_start(aup[64:P, :], ins["rwkv_a_up"][0]).then_inc(S("small_in"), 16)
            sp.dma_start(gup[:, :], ins["rwkv_g_up"][0]).then_inc(S("small_in"), 16)
            sp.dma_start(gate_up[:, :], ins["gla_gate_up"][0]).then_inc(S("small_in"), 16)
            sp.wait_ge(*at_count("pr_zero", 1))
            for par in range(2):
                rows = slice(64 * par, 64 * par + 64)
                sp.dma_start(state_nat[rows, :, rows],
                             ins["state_rwkv"][0, 0].rearrange("(f a) v k -> a v f k", a=2)[par]).then_inc(S("rwkv_state_in"), 16)
            for i in range(DENSE_RING, OUT_T):
                load_tile(i)
            for g in range(2):
                sp.wait_ge(*at_count("last_rows", g + 1))
                sp.dma_start(outs[3 + 4 * g].rearrange("a b (r w) -> (a b r) w", w=P), lrow[:, g, :]).then_inc(S("stored"), 16)
            for i in range(OUT_T, OUT_T + 4):
                load_tile(i)
            for g in range(2):
                sp.wait_ge(*at_count("hout_done", g + 1))
                for par in range(2):
                    rows = slice(64 * par, 64 * par + 64)
                    sp.dma_start(outs[2 + 4 * g][0, 0].rearrange("(f a) v k -> a v f k", a=2)[par],
                                 Hout[rows, g, :, rows]).then_inc(S("stored"), 16)
            sp.wait_ge(*at_count("gla_s_zero", 2))
            for par in range(2):
                rows = slice(64 * par, 64 * par + 64)
                sp.dma_start(gla["S"][rows, 1, :, par * P:(par + 1) * P],
                             ins["state_gla"][0, 0].rearrange("(f a) d v -> a d f v", a=2)[par]).then_inc(S("gla_state_in"), 16)
            sp.wait_ge(*at_count("gla_s", NCH))
            for g in range(2):
                for par in range(2):
                    rows = slice(64 * par, 64 * par + 64)
                    sp.dma_start(outs[4 + 4 * g][0, 0].rearrange("(f a) d v -> a d f v", a=2)[par],
                                 gla["S"][rows, g, :, par * P:(par + 1) * P]).then_inc(S("gla_stored"), 16)
            sp.wait_ge(*at_count("gla_stored", 64))
            for i in range(OUT_T + 4, OUTC_T + 4):
                if i == OUTC_T:
                    sp.wait_ge(*at_count("hgrn_s_zero", 2))
                    sp.dma_start(hgrn["S"][:, 1, :, :], ins["state_hgrn"][0, 0].rearrange("h d v -> d h v"))\
                      .then_inc(S("hgrn_state_in"), 16)
                load_tile(i)
            sp.wait_ge(*at_count("hgrn_s", NCH))
            for g in range(2):
                sp.dma_start(outs[5 + 4 * g][0, 0].rearrange("h d v -> d h v"), hgrn["S"][:, g, :, :])\
                  .then_inc(S("hgrn_stored"), 16)
            sp.wait_ge(*at_count("hgrn_stored", 32))

            w1, w3, w2 = ins["moe_w1"][0], ins["moe_w3"][0], ins["moe_w2"][0]

            def expert_block(n, e, j_extra):
                for i in range(HALVES):
                    q, h = i // 2, i % 2
                    if isinstance(n, int) and i < MOE_RING:
                        if i == 0:
                            sp.wait_ge(*at_count("out_c_full", KC))
                        elif i * HALF == DENSE_RING * TILE:
                            sp.wait_ge(*at_count("c_ln", 1))
                    else:
                        sp.wait_ge(S("e_lo"), n * HALVES + i - MOE_RING + 1)
                    buf = moe_ring[:, MOE_RING - 1 - i % MOE_RING, :]
                    if q in DOWN:
                        row = DOWN.index(q) * SC + h * P
                        sp.dma_start(buf.rearrange("p (k n) -> p k n", k=1),
                                     w2[bass.ds(e, 1), row:row + P, :].rearrange("e p n -> p e n"))\
                          .then_inc(S(f"moe_in{i % MOE_RING}"), 16)
                    else:
                        w, s = (w1, UP1.index(q)) if q in UP1 else (w3, UP3.index(q))
                        rows = slice(h * D // 2, (h + 1) * D // 2)
                        sp.dma_start(buf.rearrange("p (k n) -> p k n", k=4),
                                     w[bass.ds(e, 1), rows, s * SC:(s + 1) * SC].rearrange("e (k p) n -> p (e k) n", p=P))\
                          .then_inc(S(f"moe_in{i % MOE_RING}"), 16)

            expert_loops(sp, expert_block, lambda n: None)
            for i in range(3):
                sp.wait_ge(*at_count("y_done", 2 * i + 2))
                dst = outs[0][0][i * P:(i + 1) * P, :] if i < 2 else outs[1][0]
                sp.dma_start(dst, xtok[0:TILES[i][1], i, :]).then_inc(S("stored"), 16)
            sp.wait_ge(*at_count("stored", 16 * (2 + 4 + 3)))


_OUTS = [(1, T_PROMPT, D), (1, T_SAMPLE, D)] + \
        2 * [(1, 1, RH, RN, RN), (1, 1, RPROJ), (1, 1, GH, GDK, GDV), (1, 1, HH, HD, HD)]


def kernel(**inputs):
    import numpy as _np
    import concourse.bacc as _bacc
    from concourse import mybir as _mybir
    from concourse.bass_utils import run_bass_kernel_spmd as _run

    nc = _bacc.Bacc("TRN2", target_bir_lowering=False, num_devices=1)
    arrays, ins, outs = {}, {}, []
    for name, value in inputs.items():
        a = _np.ascontiguousarray(value)
        arrays[f"in_{name}"] = a
        ins[name] = nc.dram_tensor(f"in_{name}", a.shape, _mybir.dt.from_np(a.dtype), kind="ExternalInput").ap()
    for i, shape in enumerate(_OUTS):
        outs.append(nc.dram_tensor(f"out_{i}", shape, _mybir.dt.float32, kind="ExternalOutput").ap())
    mixed_trunk(nc, ins, outs)
    r = _run(nc, [arrays], core_ids=[0])
    return tuple(r.results[0][f"out_{i}"] for i in range(len(_OUTS)))
```

```python
import numpy as np
from contextlib import ExitStack

import concourse.bass as bass
from concourse import mybir

F32 = mybir.dt.float32
F32R = mybir.dt.float32r
I32 = mybir.dt.int32
ALU = mybir.AluOpType
ACT = mybir.ActivationFunctionType
AX = mybir.AxisListType

P = 128
D = 1024
KC = D // P
T_PROMPT, T_SAMPLE = 256, 64
T = T_PROMPT + T_SAMPLE
C = 64
NCH = T // C
N_PROMPT_CH = T_PROMPT // C
LEVELS = 6
TILES = [(0, 128), (128, 128), (256, 64)]

RH, RN = 8, 64
RDIM = RH * RN
RF = RDIM // P
RPROJ = 3 * RDIM + 64 + 64 + 128
RPC = RPROJ // P
DECAY_SCALE = 0.6065306597126334
GN_EPS = RN * 1e-5

GH, GDK, GDV = 4, 64, 128
GK, GV, GR = GH * GDK, GH * GDV, 16
G0 = RPROJ
GZ0 = G0 + 2 * GK + GV
GO0 = GZ0 + GR
P_AB = GO0 + GV
GLA_TAU = 16.0

HH, HD = 8, 128
FF = 2816
FC = FF // P
NE = 8
ALPHA = 4.0 ** 0.25
NORM_EPS = 1e-5

SC = 256
TILE = KC * SC
DENSE_RING = 4
DENSE_UNITS = 3
HALF = TILE // 2
BLK = 128
STRIPS = FF // SC
HALVES = 6 * STRIPS
MOE_RING = 11
UNITS = 6
assert HALVES % MOE_RING == 0 and HALVES % UNITS == 0
MAX_BLOCKS = -(-T // BLK)
NX = NE * (MAX_BLOCKS - 1)


def mixed_trunk(nc, ins, outs):
    ctx = ExitStack()
    with ctx:
        def sem(name):
            return ctx.enter_context(nc.semaphore(name))

        def sb(name, shape, dt=F32):
            return ctx.enter_context(nc.sbuf_tensor(name, shape, dt))

        bank = [ctx.enter_context(nc.psum_tensor(f"bank{i}", [P, 512], F32)) for i in range(8)]

        ident = sb("ident", [P, P])
        ones = sb("ones", [P, P])
        bdones = sb("bdones", [P, P])
        utri = sb("utri", [P, P])
        mask_pr = sb("mask_pr", [C, 2, C])
        lower = sb("lower", [P, LEVELS, C])
        upper = sb("upper", [P, LEVELS, C])
        reset = sb("reset", [P, T])
        slots = sb("slots", [P, BLK])
        vec = sb("vec", [P, 160])
        gate_up = sb("gate_up", [GR, GK])
        gz_w = sb("gz_w", [P, KC, GR])
        router = sb("router", [P, KC, NE])
        xT = sb("xT", [P, KC, T])
        arena_words = 45760
        with nc.sbuf_tensor("arena", [P, arena_words], F32) as arena:
            pass
        NORM0 = KC * T
        HID0 = NORM0 + 2 * KC * T
        MIX0 = 26268
        HID_PART = FC // 2
        with ExitStack() as dense:
            def dsb(name, shape, dt=F32R):
                return dense.enter_context(nc.sbuf_tensor(name, shape, dt))

            dsb("dense_low", [P, HID0], F32)
            hid_hi = [dsb(f"hid_hi{i}", [P, HID_PART, T]) for i in range(2)]
            hid_lo = [dsb(f"hid_lo{i}", [P, HID_PART, T]) for i in range(2)]
            dsb("dense_mid", [P, MIX0 - HID0 - 2 * FC * T], F32)
            in_hi = dsb("in_hi", [P, KC, T])
            in_lo = dsb("in_lo", [P, KC, T])
            wd_hi = dsb("wd_hi", [P, DENSE_UNITS, HALF])
            wd_lo = dsb("wd_lo", [P, DENSE_UNITS, HALF])
        split_words = (2 * UNITS * HALF) + 2 * KC * BLK + 2 * 2 * BLK
        split_at = arena_words - MOE_RING * HALF - split_words
        sb("arena_low", [P, split_at])
        w_hi = sb("w_hi", [P, UNITS, HALF], F32R)
        w_lo = sb("w_lo", [P, UNITS, HALF], F32R)
        xe_hi = sb("xe_hi", [P, KC, BLK], F32R)
        xe_lo = sb("xe_lo", [P, KC, BLK], F32R)
        gt_hi = sb("gt_hi", [P, 2, BLK], F32R)
        gt_lo = sb("gt_lo", [P, 2, BLK], F32R)
        moe_ring = sb("moe_ring", [P, MOE_RING, HALF])

        def slot(i):
            o = arena_words - (i + 1) * TILE
            return arena[:, o:o + TILE]

        class Region:
            def __init__(self, start, end):
                self.at, self.end = start, end

            def take(self, n):
                o = self.at
                self.at += n
                assert self.at <= self.end, (self.at, self.end)
                return arena[:, o:o + n]

        def tok(ap, k):
            return ap.rearrange("p (k t) -> p k t", k=k)

        dense_top = arena_words - DENSE_RING * TILE

        r = Region(0, dense_top)
        pr_all = r.take(RPC * (T + 2))
        PR = pr_all.rearrange("p (f t) -> p f t", f=RPC)
        XS = tok(r.take(RPC * T), RPC)
        aT = tok(r.take(RF * T), RF)
        bT = tok(r.take(RF * T), RF)
        kkT = tok(r.take(RF * T), RF)
        PRC = r.take(RF * 2 * T).rearrange("p (f a t) -> p f a t", f=RF, a=2)
        QT = tok(r.take(RF * T), RF)
        KT = tok(r.take(RF * T), RF)
        GT = tok(r.take(RF * T), RF)
        gq_at = r.at
        gq = tok(r.take(2 * T), 2)
        gk = tok(r.take(2 * T), 2)
        gv = tok(r.take(4 * T), 4)
        gog = tok(r.take(4 * T), 4)
        gla_b = tok(r.take(2 * T), 2)
        oT = tok(r.take(8 * T), 8)
        mix0 = r.at
        assert mix0 == MIX0
        s1 = tok(pr_all[:, 0:RF * T], RF)
        s2 = tok(pr_all[:, RF * T:2 * RF * T], RF)
        lw = tok(pr_all[:, 2 * RF * T:3 * RF * T], RF)
        BV = kkT
        a0 = RPC * (T + 2) + RPC * T
        early = Region(RPC * (T + 2) + RPC * T, RPC * (T + 2) + RPC * T + 3 * RF * T)
        xst = early.take(3 * D).rearrange("p (i n) -> p i n", i=3)
        vrow = early.take(2 * P).rearrange("p (a n) -> p a n", a=2)
        prc = PRC.rearrange("p f a t -> p (f a t)")
        wup = prc[:, 0:RDIM]
        aup = prc[:, RDIM:2 * RDIM]
        gup = prc[:, 2 * RDIM:3 * RDIM]
        state_nat = oT[:, 4:8, :].rearrange("p f t -> p (f t)")[:, 0:RDIM].rearrange("p (f n) -> p f n", f=RF)
        m = Region(mix0, dense_top)
        TV = m.take(2 * RDIM).rearrange("p (b n) -> p b n", b=2)
        TQ = m.take(2 * RDIM).rearrange("p (b n) -> p b n", b=2)
        TK = m.take(2 * RDIM).rearrange("p (b n) -> p b n", b=2)
        G1 = m.take(2 * 2 * RDIM).rearrange("p (b h n) -> p b h n", b=2, h=RH)
        G2 = m.take(2 * 2 * RDIM).rearrange("p (b h n) -> p b h n", b=2, h=RH)
        Tm, Tt, Xm = (m.take(2 * RF * P).rearrange("p (b f n) -> p b f n", b=2, f=RF) for _ in range(3))
        oT_all = oT.rearrange("p f t -> p (f t)")
        At = oT_all[:, 0:2 * RF * P].rearrange("p (b f n) -> p b f n", b=2, f=RF)
        inverse = oT_all[:, 4 * T:4 * T + 2 * RDIM].rearrange("p (b h n) -> p b h n", b=2, h=RH)
        W1s = m.take(RDIM)
        Un = m.take(RDIM)
        m2 = Region(0, RPC * (T + 2))
        H = m2.take(2 * RDIM).rearrange("p (g f n) -> p g f n", g=2, f=RF)
        Hout = m2.take(2 * RDIM).rearrange("p (g f n) -> p g f n", g=2, f=RF)
        Osb = arena[:, RPC * (T + 2):RPC * (T + 2) + NCH * RDIM].rearrange("p (c h n) -> p c h n", c=NCH, h=RH)
        Osq = arena[:, mix0:mix0 + NCH * RDIM].rearrange("p (c h n) -> p c h n", c=NCH, h=RH)

        def attention_buffers(reg, F, heads, width):
            b = {}
            b["Z"] = tok(reg.take(F * T), F)
            b["KD"] = tok(reg.take(F * T), F)
            b["E"] = tok(reg.take(F * T), F)
            b["Sc"] = reg.take(NCH * heads * C).rearrange("p (c h t) -> p c h t", c=NCH, h=heads)
            rows = Region(reg.at - NCH * heads * C - F * T, reg.at - NCH * heads * C)
            b["TV"] = rows.take(heads * P)
            b["TK"] = rows.take(F * P)
            b["S"] = reg.take(2 * F * width).rearrange("p (g f n) -> p g f n", g=2, f=F)
            return b

        pr_scratch = Region(2 * 2 * RDIM, RPC * (T + 2))
        decays = Region(a0, a0 + 2 * RF * T)
        gla = {"Z": tok(pr_scratch.take(2 * T), 2),
               "Sc": pr_scratch.take(NCH * GH * C).rearrange("p (c h t) -> p c h t", c=NCH, h=GH),
               "E": XS[:, RPC - 2:RPC, :],
               "S": decays.take(2 * 2 * 2 * GDV).rearrange("p (g f n) -> p g f n", g=2, f=2),
               "TV": decays.take(GH * P), "TK": decays.take(2 * P), "KD": tok(decays.take(2 * T), 2), "TVs": None,
               "F": 2, "heads": GH, "q": gq, "k": gk, "v": gv, "b": gla_b, "O": oT[:, 4:8, :],
               "sq": tok(arena[:, gq_at:gq_at + 4 * T], 4), "gate": gog, "name": "gla", "vdim": GDV, "lag": 1}
        f_ = Region(HID0 + 2 * FC * T, MIX0)
        ff_s = tok(f_.take(4 * T), 4)
        ff_g = tok(f_.take(2 * T), 2)
        res = tok(arena[:, NORM0:NORM0 + KC * T], KC)
        sq = tok(arena[:, NORM0 + KC * T:HID0], KC)
        h_ = Region(0, MIX0)
        hq = tok(h_.take(HH * T), HH)
        hf = tok(h_.take(HH * T), HH)
        hi = tok(h_.take(HH * T), HH)
        hg = tok(h_.take(HH * T), HH)
        hb = tok(h_.take(HH * T), HH)
        hgrn = attention_buffers(h_, HH, HH, HD)
        hgrn["TVs"] = arena[:, MIX0:MIX0 + NCH * D].rearrange("p (c n) -> p c n", c=NCH)
        hgrn.update(F=HH, heads=HH, q=hq, k=hf, v=hi, b=hb, O=hq, sq=hgrn["E"], gate=hg,
                    name="hgrn", vdim=HD, lag=2)
        e_ = Region(0, split_at)
        xtok = e_.take(3 * D).rearrange("p (i n) -> p i n", i=3)
        acc = tok(e_.take(KC * T), KC)
        sq2 = tok(e_.take(KC * T), KC)
        pick = e_.take(3 * BLK).rearrange("p (i n) -> p i n", i=3)
        pickw = e_.take(3 * BLK).rearrange("p (i n) -> p i n", i=3)
        pickT = e_.take(T)
        eh = e_.take(2 * SC).rearrange("p (b n) -> p b n", b=2)
        eg = e_.take(SC)
        ey = e_.take(D)
        pair = e_.take(2 * 3 * NE * NE).rearrange("p (a i n) -> p a i n", a=2, i=3)
        compact = e_.take(NX * NX).rearrange("p (j c) -> p j c", j=NX)

        dC = sb("dC", [P, RF, NCH])
        ends = sb("ends", [P, HH, NCH])
        last = sb("last", [P, 2, RPC])
        lrow = sb("lrow", [RPC, 2, P])
        gz_s = sb("gz_s", [GR, T])
        stat = sb("stat", [C, 2, NCH * RH])
        mean = sb("mean", [P, T])
        lbw = sb("lbw", [P, 8, HH])
        eps_gn = sb("eps_gn", [P, 1])
        eps_norm = sb("eps_norm", [P, 1])
        lg = sb("lg", [P, 3, NE])
        rt = sb("rt", [P, 12, 3, NE])
        cur = sb("cur", [P, 3])
        wcur = sb("wcur", [P, 3])
        jlt = sb("jlt", [P, NE, NE])
        pos = sb("pos", [P, NE, 3])
        wts = sb("wts", [P, NE, 3])
        cnt = sb("cnt", [P, NE])
        cand = sb("cand", [P, 8, NX])
        extra_i = sb("extra_i", [P, 2, NX], I32)
        bases = sb("bases", [P, NX])
        n_extra = sb("n_extra", [P, 4], I32)

        V, vloads, at = {}, [], [0, 0]

        def vector(name, ap, table):
            rows = ap.shape[0]
            V[name] = (0 if table == 0 else 91) + at[table]
            vloads.append((table, at[table], rows, ap))
            at[table] += rows

        def rows_of(ap, w=P):
            return ap.rearrange("a (r w) -> (a r) w", w=w)

        vector("mu", rows_of(ins["rwkv_mu"]), 0)
        vector("shift", rows_of(ins["cache_rwkv_shift"].rearrange("a b n -> (a b) n")), 0)
        for n in ("rwkv_w0", "rwkv_a0", "rwkv_k_k", "rwkv_k_a"):
            vector(n, rows_of(ins[n]), 0)
        vector("rwkv_r_k", rows_of(ins["rwkv_r_k"].rearrange("a h n -> a (h n)")), 0)
        for n in ("rwkv_gn_w", "rwkv_gn_b", "gla_gate_b", "gla_norm_w",
                  "ln_ab_g", "ln_ab_b", "ln_ffn_g", "ln_ffn_b"):
            vector(n, rows_of(ins[n]), 0)
        assert at[0] == 91
        for n in ("hgrn_lb", "hgrn_norm_w", "ln_c_g", "ln_c_b", "ln_moe_g", "ln_moe_b"):
            vector(n, rows_of(ins[n]), 1)

        def vcol(name, j=0):
            return vec[:, V[name] + j:V[name] + j + 1]

        names = {}

        shared = {}
        for stage, of_gla in (("z", LEVELS + 1), ("sc", (LEVELS + 1) * NCH * 2), ("sc_full", (LEVELS + 1) * NCH * 2),
                              ("qk", 1), ("tm", 2 * NCH), ("tm_full", 2 * NCH), ("s", NCH), ("o", NCH), ("o_full", NCH),
                              ("ds_full", NCH), ("osq", 1), ("rms", GH), ("rms_full", GH), ("min", 1), ("softplus", 1), ("gated", 1),
                              ("dist", LEVELS + 1), ("e", LEVELS + 2), ("s_zero", 2), ("b", 2), ("out", GH),
                              ("state_in", 32), ("stored", 64)):
            shared["gla_" + stage] = ("attention_" + stage, 0)
            shared["hgrn_" + stage] = ("attention_" + stage, of_gla)
        for stage, each in (("res", KC), ("ln_full", 2), ("centered", KC), ("sq", KC), ("std", 1), ("scaled", KC), ("ln", KC)):
            for i, n_ in enumerate(("ab", "ffn", "c", "moe")):
                shared[n_ + "_" + stage] = ("norm_" + stage, i * each)

        count = 0
        for stage, n in (("x_full", KC), ("vec_full", 2), ("lora_full", 3 * RF), ("last_full", 2), ("kk_full", RF),
                         ("bonus_full", RF), ("h0_full", 1), ("gate_full", 2)):
            shared[stage] = ("prepared", count)
            count += n
        shared["lora_done"], shared["gate_done"] = ("low_rank_done", 0), ("low_rank_done", 3 * RF)
        shared["x_done"], shared["vec_done"] = ("first_copies", 0), ("first_copies", KC)

        def S(name):
            name = shared.get(name, (name, 0))[0]
            if name not in names:
                names[name] = sem(name)
            return names[name]

        def at_count(name, value=1):
            return S(name), shared.get(name, (name, 0))[1] + value

        tiles = []

        def strip(w, row0, rows, col):
            return w[row0 * P:(row0 + rows) * P, col:col + SC].rearrange("(k p) n -> p k n", p=P)

        w_in = ins["w_in_ab"][0]
        AB_COLS = [i * SC for i in range(RPROJ // SC)] + [G0, G0 + GK, G0 + 2 * GK, G0 + 2 * GK + SC, GO0, GO0 + SC]
        for i, col in enumerate(AB_COLS):
            tiles.append((strip(w_in, 0, KC, col), KC, "ab_full", 2 * i + 2))
        for i in range(D // SC):
            tiles.append((strip(ins["w_out_ab"][0], 0, KC, i * SC), KC, "out_ab_full", 2 * i + 2))
        for i in range(STRIPS):
            tiles.append((strip(ins["ffn_w1"][0], 0, KC, i * SC), KC, "h1_full", 2 * i + 2))
            tiles.append((strip(ins["ffn_w3"][0], 0, KC, i * SC), KC, "h3_full", 2 * i + 2))
        W2_GROUPS = [(0, 8), (8, 8), (16, 6)]
        for i in range(D // SC):
            for gi, (r0, n) in enumerate(W2_GROUPS):
                tiles.append((strip(ins["ffn_w2"][0], r0, n, i * SC), n) +
                             (("w2_full", 2 * i + 2) if gi == 2 else ("w2_part_used", 2 * i + gi + 1)))
        first_in_c = len(tiles)
        for i in [(4 + n, n - 4, n, n)[n // 4] for n in range(4 * D // SC)]:
            tiles.append((strip(ins["w_in_c"][0], 0, KC, i * SC), KC, "in_c_full", 2 * (len(tiles) - first_in_c) + 2))
        for i in range(D // SC):
            tiles.append((strip(ins["w_out_c"][0], 0, KC, i * SC), KC, "out_c_full", 2 * i + 2))
        ND = len(tiles)
        for i in range(DENSE_RING):
            shared[f"moe_in{i}"] = (f"tile_in{i}", 16 * len(range(i, ND, DENSE_RING)))
        AB_T, OUT_T = 0, len(AB_COLS)
        FFN_T = OUT_T + D // SC
        W2_T = FFN_T + 2 * STRIPS
        INC_T = W2_T + 3 * (D // SC)
        OUTC_T = INC_T + 4 * D // SC

        def tile_of(i):
            return slot(i % DENSE_RING).rearrange("p (k n) -> p k n", k=KC)

        def half_of(m_):
            words = (min(4 * (m_ % 2) + 4, tiles[m_ // 2][1]) - 4 * (m_ % 2)) * SC
            return slot(m_ // 2 % DENSE_RING)[:, (m_ % 2) * HALF:(m_ % 2) * HALF + words], words

        def bc(ap, axis, n):
            shape = list(ap.shape)
            return ap.unsqueeze(axis).to_broadcast(shape[:axis] + [n] + shape[axis:])

        def chunk(c):
            return slice(c * C, (c + 1) * C)

        BATCHES = [[0, 1], [2, 3], [4]]
        E_H1, E_H3, E_Y, E_SCR = bank[0:2], bank[2:4], bank[4:6], bank[6:8]

        UP1 = [0] + [3 * s - 1 for s in range(1, STRIPS)]
        UP3 = [1] + [3 * s for s in range(1, STRIPS)]
        DOWN = [3 * s + 4 for s in range(STRIPS - 1)] + [3 * STRIPS - 1]

        def res_of(n_):
            return acc if n_ == "moe" else res

        def sq_of(n_):
            return sq2 if n_ == "moe" else sq

        GLA_AT = {(BATCHES[0][0], 2): 0, (BATCHES[1][0], LEVELS - 2): 1, (BATCHES[1][0], LEVELS - 1): 2,
                  **{(BATCHES[2][0], lv): lv + 2 for lv in range(1, LEVELS)}}
        IN_C_FIRST = 11

        def ahead(first, per_pair, until):
            return [list(range(first + per_pair * (j // 2), first + per_pair * (j // 2 + 1))) if j % 2 == 0 and j < until
                    else [] for j in range(KC)]

        def expert_loops(eng, body, rest):
            body(0, 0, None)
            with eng.Fori(1, NE) as e:
                body(e, e, None)
            eng.wait_ge(S("extras_known"), 1)
            nx = eng.value_load(n_extra[0:1, 0:1], min_val=0, max_val=NX)
            with eng.If(nx > 0):
                with eng.Fori(0, nx) as j:
                    body(j + NE, eng.value_load(extra_i[0:1, 0, bass.ds(j, 1)], min_val=0, max_val=NE - 1), j)
            rest(nx + NE)

        block = ctx.enter_context(nc.Block())
        where = {}

        @block.tensor
        def _(pe):
            turn = [0]
            owner = [None] * 8

            def take(name, taken, value):
                k = turn[0] % 8
                turn[0] += 1
                if owner[k]:
                    pe.wait_ge(*at_count(owner[k][0], owner[k][1]))
                owner[k] = (taken, value)
                where[name] = bank[k]
                return bank[k]

            def weights(m_):
                pe.wait_ge(*at_count("dense_lo", m_ + 1))
                return wd_hi[:, m_ % DENSE_UNITS, :], wd_lo[:, m_ % DENSE_UNITS, :]

            def product(b, w_, k, j, x_hi, x_lo, start, stop):
                cols = slice(k * SC + j * P, k * SC + (j + 1) * P)
                pe.matmul(b[:, 0:T], w_[0][:, cols], x_hi, start=start, stop=False)
                pe.matmul(b[:, 0:T], w_[0][:, cols], x_lo, start=False, stop=False)
                return pe.matmul(b[:, 0:T], w_[1][:, cols], x_hi, start=False, stop=stop)

            def dense_pair(i, stage, name, j0, full, taken):
                two = [take((name, j0 + j), taken, j0 + j + 1) for j in range(2)]
                for h in range(2):
                    w_ = weights(2 * i + h)
                    for j in range(2):
                        for k in range(4 * h, 4 * h + 4):
                            if j == 0 and j0 == 0:
                                pe.wait_ge(*at_count("in_lo", KC * stage + k + 1))
                            mm = product(two[j], w_, k - 4 * h, j, in_hi[:, k, :], in_lo[:, k, :], k == 0, k == KC - 1)
                        if h == 1:
                            mm.then_inc(S(full), 1)
                    if h == 0:
                        mm.then_inc(S("dense_half"), 1)

            pe.wait_ge(*at_count("masks", 1))
            pe.wait_ge(*at_count("x_in", 48))
            for k in range(KC):
                b = take(("x", k), "x_done", k + 1)
                for i, (t0, n) in enumerate(TILES):
                    mm = pe.transpose(b[:, t0:t0 + n], xst[0:n, i, k * P:(k + 1) * P], ident[0:n, 0:n])
                mm.then_inc(S("x_full"), 1)

            dense_pair(AB_T, 0, "ab", 0, "ab_full", "ab_done")
            pe.wait_ge(*at_count("vectors_in", 16 * len(vloads)))
            for t in range(2):
                n = at[t]
                b = take(("vec", t), "vec_done", t + 1)
                pe.transpose(b[:, 0:n], vrow[0:n, t, :], ident[0:n, 0:n]).then_inc(S("vec_full"), 1)
            for i in range(1, RPC // 2 + 1):
                dense_pair(AB_T + i, 0, "ab", 2 * i, "ab_full", "ab_done")

            pe.wait_ge(*at_count("masks", 2))
            pe.wait_ge(*at_count("last_copied", 2))
            pe.wait_ge(*at_count("lora_in", 2))
            pe.wait_ge(*at_count("small_in", 16 * 6))
            for n in range(3 * RF):
                f = n % RF
                w = (wup, aup, gup)[n // RF]
                b = take(("lora", n), "lora_done", n + 1)
                pe.matmul(b[:, 0:T], w[:, f * P:(f + 1) * P], XS[:, 13 if n >= 2 * RF else 12, :],
                          start=True, stop=True).then_inc(S("lora_full"), 1)
            dense_pair(AB_T + 8, 0, "ab", 16, "ab_full", "ab_done")
            for g in range(2):
                b = take(("last", g), "last_rows", g + 1)
                pe.transpose(b[0:RPC, 0:P], last[:, g, :], ident[:, :]).then_inc(S("last_full"), 1)
            dense_pair(AB_T + 9, 0, "ab", 18, "ab_full", "ab_done")

            pe.wait_ge(*at_count("kk_squares", 1))
            for f in range(RF):
                b = take(("kk", f), "kk_norm", f + 1)
                pe.matmul(b[:, 0:T], bdones[:, :], KT[:, f, :], start=True, stop=True).then_inc(S("kk_full"), 1)
            dense_pair(AB_T + 10, 0, "ab", 20, "ab_full", "ab_done")
            pe.wait_ge(*at_count("bonus_in", 1))
            for f in range(RF):
                b = take(("bonus", f), "bonus_done", f + 1)
                pe.matmul(b[:, 0:T], bdones[:, :], oT[:, f, :], start=True, stop=True).then_inc(S("bonus_full"), 1)
            dense_pair(AB_T + 11, 0, "ab", 22, "ab_full", "ab_done")
            dense_pair(AB_T + 12, 0, "ab", 24, "ab_full", "ab_done")
            b = take(("ab", 2 * len(AB_COLS)), "ab_done", 2 * len(AB_COLS) + 1)
            for k in range(KC):
                mm = pe.matmul(b[0:GR, 0:T], gz_w[:, k, :], xT[:, k, :], start=(k == 0), stop=(k == KC - 1))
            mm.then_inc(S("ab_full"), 1)
            pe.wait_ge(*at_count("rwkv_state_in", 32))
            b = take(("h0", 0), "h_init", 1)
            for f in range(RF):
                mm = pe.transpose(b[:, f * P:(f + 1) * P], state_nat[:, f, :], ident[:, :])
            mm.then_inc(S("h0_full"), 1)
            pe.wait_ge(*at_count("ab_done", 2 * len(AB_COLS) + 1))
            for f in range(2):
                b = take(("gate", f), "gate_done", f + 1)
                pe.matmul(b[:, 0:T], gate_up[:, f * P:(f + 1) * P], gz_s[:, :], start=True, stop=True)\
                  .then_inc(S("gate_full"), 1)

            def scores(a, lv):
                n_, F, NH = a["name"], a["F"], a["heads"]
                pars = NH // F
                W = P // pars
                pe.wait_ge(*at_count(n_ + "_z", lv + 1))
                zb = (a["Z"], a["KD"])[lv % 2]
                for c in range(NCH):
                    for par in range(pars):
                        rows = slice(W * par, W * par + W)
                        i = lv * NCH * pars + c * pars + par
                        b = take((n_, "sc", i), n_ + "_sc", i + 1)
                        for f in range(F):
                            left, right = (a["k"], a["q"]) if lv == 0 else (zb, zb)
                            mm = pe.matmul(b[0:C, f * C:(f + 1) * C], left[rows, f, chunk(c)],
                                           right[rows, f, chunk(c)], start=(f == 0), stop=(f == F - 1),
                                           skip_group_check=True)
                        mm.then_inc(S(n_ + "_sc_full"), 1)

            def state_chain(a, c):
                n_, F, NH = a["name"], a["F"], a["heads"]
                pars = NH // F
                if c == 0:
                    pe.wait_ge(*at_count(n_ + "_qk", 1))
                    pe.wait_ge(*at_count(n_ + "_sc", (LEVELS + 1) * NCH * pars))
                    pe.wait_ge(*at_count(n_ + "_state_in", 16 * pars))
                tv = 2 * c if a["TVs"] is None else 2 * NCH + 2 * c
                g = 0 if c < N_PROMPT_CH else 1
                TV_ = a["TV"] if a["TVs"] is None else a["TVs"][:, c, :]
                for src, dst_n, per in (((a["v"], NH, 4),) if a["TVs"] is None else ()) + ((a["KD"], F, 4),):
                    for k0 in range(0, dst_n, per):
                        m_ = min(per, dst_n - k0)
                        b = take((n_, "tm", tv), n_ + "_tm", tv + 1)
                        tv += 1
                        for k in range(m_):
                            mm = pe.transpose(b[0:C, k * P:(k + 1) * P], src[:, k0 + k, chunk(c)], ident[:, :])
                        mm.then_inc(S(n_ + "_tm_full"), 1)
                if c:
                    pe.wait_ge(*at_count(n_ + "_s", c))
                b = take((n_, "o", c), n_ + "_o", c + 1)
                for hh in range(NH):
                    f, par = hh // pars, hh % pars
                    pe.matmul(b[:, hh * C:(hh + 1) * C], a["S"][:, g, f, par * P:(par + 1) * P],
                              a["Z"][:, f, chunk(c)], start=(hh == 0), stop=False, skip_group_check=True)
                pe.wait_ge(*at_count(n_ + "_tm", tv))
                for hh in range(NH):
                    f, par = hh // pars, hh % pars
                    mm = pe.matmul(b[:, hh * C:(hh + 1) * C], TV_[0:C, hh * P:(hh + 1) * P],
                                   a["Sc"][0:C, c, par * F + f, :], start=False, stop=(hh == NH - 1),
                                   skip_group_check=True)
                mm.then_inc(S(n_ + "_o_full"), 1)
                per = 4 // pars
                for k0 in range(0, F, per):
                    i = c * (F // min(per, F)) + k0 // per
                    b = take((n_, "ds", i), n_ + "_s", c + 1)
                    for k in range(min(per, F)):
                        f = k0 + k
                        mm = pe.matmul(b[:, k * P * pars:(k + 1) * P * pars], a["TK"][0:C, f * P:(f + 1) * P],
                                       TV_[0:C, f * P * pars:(f + 1) * P * pars],
                                       start=(k == 0), stop=(k == min(per, F) - 1), skip_group_check=True)
                    mm.then_inc(S(n_ + "_ds_full"), 1)

            def head_sums(a):
                n_, F, NH = a["name"], a["F"], a["heads"]
                pars = NH // F
                pe.wait_ge(*at_count(n_ + "_osq", 1))
                for hh in range(NH):
                    b = take((n_, "rms", hh), n_ + "_rms", hh + 1)
                    pe.matmul(b[:, 0:T], ones[:, :], a["sq"][:, hh, :], start=True, stop=True)\
                      .then_inc(S(n_ + "_rms_full"), 1)

            pe.wait_ge(*at_count("rwkv_ready", 1))
            for batch in BATCHES:
                for bi, c in enumerate(batch):
                    for n, src in enumerate((XS[:, 8:12, :], QT, KT)):
                        b = take(("tm", 3 * c + n), "tm_done", 3 * c + n + 1)
                        for f in range(RF):
                            mm = pe.transpose(b[0:C, f * P:(f + 1) * P], src[:, f, chunk(c)], ident[:, :])
                        mm.then_inc(S("tm_full"), 1)
                    for n, left in enumerate((KT, QT)):
                        for par in range(2):
                            rows = slice(64 * par, 64 * par + 64)
                            b = take(("gram", 6 * c + 2 * n + par), "gram_done", 6 * c + 2 * n + par + 1)
                            for f in range(RF):
                                mm = pe.matmul(b[0:C, f * P:(f + 1) * P], left[rows, f, chunk(c)],
                                               PRC[rows, f, :, chunk(c)], start=(f == 0), stop=(f == RF - 1),
                                               skip_group_check=True)
                            mm.then_inc(S("gram_full"), 1)
                    for par in range(2):
                        rows = slice(64 * par, 64 * par + 64)
                        b = take(("gram", 6 * c + 4 + par), "gram_done", 6 * c + 4 + par + 1)
                        for f in range(RF):
                            mm = pe.matmul(b[0:C, f * C:(f + 1) * C], PRC[rows, f, 0, chunk(c)], QT[rows, f, chunk(c)],
                                           start=(f == 0), stop=(f == RF - 1), skip_group_check=True)
                        mm.then_inc(S("gram_full"), 1)
                first, nb = batch[0], len(batch)
                for lv in range(1, LEVELS):
                    for bi, c in enumerate(batch):
                        pe.wait_ge(*at_count("inv_ready", LEVELS * first + (lv - 1) * nb + bi + 1))
                        n = 5 * first + (lv - 1) * nb + bi + 1
                        b = take(("X", lv, c), "inv_x", n)
                        for f in range(RF):
                            mm = pe.matmul(b[:, f * P:(f + 1) * P], At[:, bi, f, :], Tm[:, bi, f, :],
                                           start=(f == 0), stop=(f == RF - 1), skip_group_check=True)
                        mm.then_inc(S("inv_full"), 1)
                    for bi, c in enumerate(batch):
                        pe.wait_ge(*at_count("inv_x", 5 * first + (lv - 1) * nb + bi + 1))
                        if lv < LEVELS - 1:
                            b = take(("Y", lv, c), "inv_y", 4 * first + (lv - 1) * nb + bi + 1)
                            for f in range(RF):
                                mm = pe.matmul(b[:, f * P:(f + 1) * P], Tt[:, bi, f, :], Xm[:, bi, f, :],
                                               start=(f == 0), stop=(f == RF - 1), skip_group_check=True)
                            mm.then_inc(S("inv_full"), 1)
                        b = take(("Yt", lv, c), "inv_ready", LEVELS * first + lv * nb + bi + 1)
                        for f in range(RF):
                            mm = pe.matmul(b[:, f * P:(f + 1) * P], Xm[:, bi, f, :], Tt[:, bi, f, :],
                                           start=(f == 0), stop=(f == RF - 1), skip_group_check=True)
                        mm.then_inc(S("inv_full"), 1)
                    if (first, lv) in GLA_AT and GLA_AT[first, lv] > 0:
                        scores(gla, GLA_AT[first, lv] - 1)
                for bi, c in enumerate(batch):
                    g = 0 if c < N_PROMPT_CH else 1

                    def heads(b, left, right, last_one=False):
                        for hh in range(RH):
                            st = (hh % 2) * RF + hh // 2
                            mm = pe.matmul(b[0:C, hh * C:(hh + 1) * C], left(st), right[:, hh * C:(hh + 1) * C],
                                           start=False, stop=(last_one and hh == RH - 1), skip_group_check=True)
                        return mm

                    pe.wait_ge(*at_count("h_init", 1))
                    if c:
                        pe.wait_ge(*at_count("h_done", c))
                    pe.wait_ge(*at_count("tm_done", 3 * c + 3))
                    b = take(("w1", c), "w1_done", c + 1)
                    for f in range(RF):
                        pe.matmul(b[0:C, f * P:(f + 1) * P], PRC[:, f, 0, chunk(c)], H[:, g, f, :],
                                  start=(f == 0), stop=False, skip_group_check=True)
                    heads(b, lambda st: G1[0:C, bi, st, 0:C], TV[0:C, bi, :], True).then_inc(S("seq_full"), 1)
                    bo = take(("o", c), "o_done", c + 1)
                    for f in range(RF):
                        pe.matmul(bo[0:C, f * P:(f + 1) * P], PRC[:, f, 1, chunk(c)], H[:, g, f, :],
                                  start=(f == 0), stop=False, skip_group_check=True)
                    heads(bo, lambda st: G1[0:C, bi, st, C:2 * C], TV[0:C, bi, :])
                    pe.wait_ge(*at_count("inv_ready", LEVELS * first + (LEVELS - 1) * nb + bi + 1))
                    pe.wait_ge(*at_count("w1_done", c + 1))
                    b = take(("u", c), "u_done", c + 1)
                    for hh in range(RH):
                        st = (hh % 2) * RF + hh // 2
                        mm = pe.matmul(b[0:C, hh * C:(hh + 1) * C], inverse[0:C, bi, st, :], W1s[0:C, hh * C:(hh + 1) * C],
                                       start=(hh == 0), stop=(hh == RH - 1), skip_group_check=True)
                    mm.then_inc(S("seq_full"), 1)
                    pe.wait_ge(*at_count("u_done", c + 1))
                    heads(bo, lambda st: G2[0:C, bi, st, C:2 * C], Un[0:C, :], True).then_inc(S("seq_full"), 1)
                    b = take(("dh", c), "h_done", c + 1)
                    for f in range(RF):
                        cols = slice(f * P, (f + 1) * P)
                        pe.matmul(b[:, cols], TK[0:C, bi, cols], TV[0:C, bi, cols],
                                  start=(f == 0), stop=False, skip_group_check=True)
                        mm = pe.matmul(b[:, cols], TQ[0:C, bi, cols], Un[0:C, cols],
                                       start=False, stop=(f == RF - 1), skip_group_check=True)
                    mm.then_inc(S("seq_full"), 1)
            pe.wait_ge(*at_count("h_done", NCH))
            for g in range(2):
                b = take(("hout", g), "hout_done", g + 1)
                for f in range(RF):
                    mm = pe.transpose(b[:, f * P:(f + 1) * P], H[:, g, f, :], ident[:, :])
                mm.then_inc(S("hout_full"), 1)
            for c in range(3):
                state_chain(gla, c)
            pe.wait_ge(*at_count("gn_done", 1))
            for c in range(NCH):
                b = take(("ot", c), "ot_done", c + 1)
                for f in range(RF):
                    mm = pe.transpose(b[:, f * C:(f + 1) * C],
                                      Osb[0:C, c, 2 * f:2 * f + 2, :].rearrange("p h n -> p (h n)"), ident[0:C, 0:C])
                mm.then_inc(S("ot_full"), 1)
            for c in range(3, NCH):
                state_chain(gla, c)
            head_sums(gla)

            def layer_norm(n_):
                b = take((n_, "sum"), n_ + "_centered", KC)
                for k in range(KC):
                    if n_ != "moe":
                        pe.wait_ge(*at_count(n_ + "_res", k + 1))
                    mm = pe.matmul(b[:, 0:T], ones[:, :], res_of(n_)[:, k, :], start=(k == 0), stop=(k == KC - 1))
                mm.then_inc(S(n_ + "_ln_full"), 1)
                b = take((n_, "sqs"), n_ + "_std", 1)
                for k in range(KC):
                    pe.wait_ge(*at_count(n_ + "_sq", k + 1))
                    mm = pe.matmul(b[:, 0:T], ones[:, :], sq_of(n_)[:, k, :], start=(k == 0), stop=(k == KC - 1))
                mm.then_inc(S(n_ + "_ln_full"), 1)

            for i in range(D // SC):
                dense_pair(OUT_T + i, 1, "out_ab", 2 * i, "out_ab_full", "ab_res")
            layer_norm("ab")
            for i in range(STRIPS):
                dense_pair(FFN_T + 2 * i, 2, "h1", 2 * i, "h1_full", "h1_done")
                dense_pair(FFN_T + 2 * i + 1, 2, "h3", 2 * i, "h3_full", "ffn_g")
            for i in range(D // SC):
                two = [take(("w2", 2 * i + j), "ffn_res", 2 * i + j + 1) for j in range(2)]
                for gi, (r0, n) in enumerate(W2_GROUPS):
                    for h in range(2):
                        w_ = weights(2 * (W2_T + 3 * i + gi) + h)
                        for j in range(2):
                            for k in range(r0 + 4 * h, r0 + min(4 * h + 4, n)):
                                if i == 0 and j == 0:
                                    pe.wait_ge(*at_count("hid_lo", k + 1))
                                part, kk_ = k // HID_PART, k % HID_PART
                                mm = product(two[j], w_, k - r0 - 4 * h, j, hid_hi[part][:, kk_, :], hid_lo[part][:, kk_, :],
                                             k == 0, k == FC - 1)
                            if h == 1 and gi == len(W2_GROUPS) - 1:
                                mm.then_inc(S("w2_full"), 1)
                        if h == 0:
                            mm.then_inc(S("dense_half"), 1)
                        elif gi < len(W2_GROUPS) - 1:
                            mm.then_inc(S("w2_part_used"), 1)
            layer_norm("ffn")
            def in_c(i):
                dense_pair(INC_T + i, 3, "in_c", 2 * i, "in_c_full", "in_c_done")

            for i in range(IN_C_FIRST):
                in_c(i)

            def v_rows(chunks):
                for c in chunks:
                    for half in range(2):
                        b = take(("hgrn", "tm", 2 * c + half), "hgrn_tm", 2 * c + half + 1)
                        for k in range(4):
                            mm = pe.transpose(b[0:C, k * P:(k + 1) * P], hi[:, 4 * half + k, chunk(c)], ident[:, :])
                        mm.then_inc(S("hgrn_tm_full"), 1)

            def between_levels(lv):
                if IN_C_FIRST + lv < OUTC_T - INC_T:
                    in_c(IN_C_FIRST + lv)
                elif lv < LEVELS:
                    pe.wait_ge(*at_count("in_c_done", 3 * KC))
                    v_rows((0, 1))
                else:
                    v_rows(range(2, NCH))
                    pe.wait_ge(*at_count("in_c_done", 4 * KC))

            for lv in range(LEVELS + 1):
                scores(hgrn, lv)
                between_levels(lv)
            for c in range(NCH):
                state_chain(hgrn, c)
            head_sums(hgrn)
            for i in range(D // SC):
                dense_pair(OUTC_T + i, 4, "out_c", 2 * i, "out_c_full", "c_res")
            layer_norm("c")

            pe.wait_ge(*at_count("c_ln", KC))
            for i, (t0, n) in enumerate(TILES):
                for k0 in (0, 4):
                    j = 2 * i + k0 // 4
                    b = take(("xtok", j), "xtok_done", j + 1)
                    for k in range(4):
                        mm = pe.transpose(b[0:n, k * P:(k + 1) * P], xT[:, k0 + k, t0:t0 + n], ident[:, :])
                    mm.then_inc(S("xtok_full"), 1)
            for i, (t0, n) in enumerate(TILES):
                b = take(("logit", i), "logits_done", i + 1)
                for k in range(KC):
                    mm = pe.matmul(b[0:n, 0:NE], xT[:, k, t0:t0 + n], router[:, k, :],
                                   start=(k == 0), stop=(k == KC - 1))
                mm.then_inc(S("logit_full"), 1)
            pe.wait_ge(*at_count("chosen", 1))
            for i in range(3):
                b = take(("pos", i), "pos_done", i + 1)
                for j in range(i):
                    pe.matmul(b[:, 0:NE], ones[:, :], rt[:, 0, j, :], start=(j == 0), stop=False)
                pe.matmul(b[:, 0:NE], utri[:, :], rt[:, 0, i, :], start=(i == 0), stop=True).then_inc(S("pos_full"), 1)
            b = take(("count", 0), "pos_done", 4)
            for j in range(3):
                mm = pe.matmul(b[:, 0:NE], ones[:, :], rt[:, 0, j, :], start=(j == 0), stop=(j == 2))
            mm.then_inc(S("pos_full"), 1)
            pe.wait_ge(*at_count("xtok_done", 6))
            pe.wait_ge(*at_count("pos_done", 4))
            pe.wait_ge(*at_count("logits_done", 3))
            pe.wait_ge(*at_count("c_std", 1))
            pe.wait_ge(*at_count("hgrn_rms", HH))
            pe.wait_ge(*at_count("c_res", KC))

            def half_tile(n, q, h):
                pe.wait_ge(S("e_lo"), HALVES * n + 2 * q + h + 1)
                u = (2 * q + h) % UNITS
                return w_hi[:, u, :], w_lo[:, u, :]

            def scatter(n, k, b):
                if k == 0:
                    pe.wait_ge(S("e_y"), 2 * n)
                    pe.wait_ge(S("e_pickt"), n)
                pe.matmul(b[:, 0:T], ey[:, k * P:(k + 1) * P], pickT[:, :], start=True, stop=True)\
                  .then_inc(S("e_scatter"), 1)

            def expert_block(n, e, j_extra):
                later = not isinstance(n, int)
                pe.wait_ge(S("e_pick"), n + 1)
                if later:
                    pe.wait_ge(S("e_pickt"), n)
                for half in range(2):
                    for k in range(4):
                        for i in range(3):
                            mm = pe.matmul(E_SCR[half][:, k * BLK:(k + 1) * BLK],
                                           xtok[:, i, (4 * half + k) * P:(4 * half + k + 1) * P], pick[:, i, :],
                                           start=(i == 0), stop=(i == 2))
                    mm.then_inc(S("e_gather_full"), 1)
                pe.wait_ge(S("e_rows"), 2 * n + 2)

                def up(q, b):
                    for h in range(2):
                        hi_, lo_ = half_tile(n, q, h)
                        for k in range(4):
                            cols = slice(k * SC, (k + 1) * SC)
                            kk_ = 4 * h + k
                            pe.matmul(b[:, 0:SC], xe_hi[:, kk_, :], hi_[:, cols], start=(kk_ == 0), stop=False)
                            pe.matmul(b[:, 0:SC], xe_lo[:, kk_, :], hi_[:, cols], start=False, stop=False)
                            mm = pe.matmul(b[:, 0:SC], xe_hi[:, kk_, :], lo_[:, cols], start=False, stop=(kk_ == KC - 1))
                        mm.then_inc(S("e_used"), 1)

                def hidden_to_rows(s):
                    pe.wait_ge(S("e_g"), STRIPS * n + s + 1)
                    for j in range(2):
                        mm = pe.transpose(E_SCR[0][:, j * BLK:(j + 1) * BLK], eg[:, j * P:(j + 1) * P], ident[:, :])
                    mm.then_inc(S("e_gt_full"), 1)

                def down(s):
                    pe.wait_ge(S("e_gt"), STRIPS * n + s + 1)
                    if s == 0 and later:
                        pe.wait_ge(S("e_y"), 2 * n)
                    for j in range(2):
                        hi_, lo_ = half_tile(n, DOWN[s], j)
                        for half in range(2):
                            cols = slice(half * 512, (half + 1) * 512)
                            pe.matmul(E_Y[half][:, :], gt_hi[:, j, :], hi_[:, cols], start=(s == 0 and j == 0), stop=False)
                            pe.matmul(E_Y[half][:, :], gt_lo[:, j, :], hi_[:, cols], start=False, stop=False)
                            mm = pe.matmul(E_Y[half][:, :], gt_hi[:, j, :], lo_[:, cols],
                                           start=False, stop=(s == STRIPS - 1 and j == 1))
                        mm.then_inc(S("e_used"), 1)

                for s in range(STRIPS):
                    up(UP1[s], E_H1[s % 2])
                    if s:
                        hidden_to_rows(s - 1)
                    up(UP3[s], E_H3[s % 2])
                    if s:
                        down(s - 1)
                    if later and 1 <= s <= KC:
                        if s > 1:
                            pe.wait_ge(S("e_added"), KC * (n - 1) + s - 1)
                        scatter(n, s - 1, E_SCR[1])
                hidden_to_rows(STRIPS - 1)
                if later:
                    pe.wait_ge(S("e_added"), KC * n)
                for i, (t0, m_) in enumerate(TILES):
                    mm = pe.transpose(E_SCR[1][:, t0:t0 + m_], pickw[0:m_, i, :], ident[0:m_, 0:m_])
                mm.then_inc(S("e_pickt_full"), 1)
                down(STRIPS - 1)

            def last_rows(n):
                for k in range(KC):
                    if k >= 4:
                        pe.wait_ge(S("e_added"), KC * (n - 1) + k - 3)
                    scatter(n, k, bank[k % 4])
                pe.wait_ge(S("e_added"), KC * n)

            expert_loops(pe, expert_block, last_rows)
            layer_norm("moe")
            pe.wait_ge(*at_count("moe_ln", KC))
            for i, (t0, n) in enumerate(TILES):
                for k0 in (0, 4):
                    j = 2 * i + k0 // 4
                    b = take(("y", j), "y_done", j + 1)
                    for k in range(4):
                        mm = pe.transpose(b[0:n, k * P:(k + 1) * P], xT[:, k0 + k, t0:t0 + n], ident[:, :])
                    mm.then_inc(S("y_full"), 1)

        @block.vector
        def _(dve):
            chain = [0]

            def link(ins_):
                chain[0] += 1
                ins_.then_inc(S("dve_chain"), 1)
                dve.wait_ge(S("dve_chain"), chain[0])

            def dense_rest(i):
                for m_ in (2 * i, 2 * i + 1):
                    dve.wait_ge(*at_count("dense_hi", m_ + 1))
                    src, words = half_of(m_)
                    dve.tensor_tensor(wd_lo[:, m_ % DENSE_UNITS, 0:words], src, wd_hi[:, m_ % DENSE_UNITS, 0:words],
                                      ALU.subtract).then_inc(S("dense_lo"), 1)

            def input_rest(stage, x):
                for k in range(KC):
                    if stage == 0:
                        dve.wait_ge(*at_count("x_done", k + 1))
                    dve.wait_ge(*at_count("in_hi", KC * stage + k + 1))
                    dve.tensor_tensor(in_lo[:, k, :], x[:, k, :], in_hi[:, k, :], ALU.subtract).then_inc(S("in_lo"), 1)

            dense_rest(AB_T)
            input_rest(0, xT)
            dense_rest(AB_T + 1)
            dve.wait_ge(*at_count("vec_done", 2))
            dve.wait_ge(*at_count("pr_zero"))
            l0, l1 = vec[:, V["hgrn_lb"]:V["hgrn_lb"] + HH], vec[:, V["hgrn_lb"] + HH:V["hgrn_lb"] + 2 * HH]
            link(dve.tensor_tensor(lbw[:, 6, :], l0, l1, ALU.max))
            link(dve.tensor_tensor(lbw[:, 0, :], l0, lbw[:, 6, :], ALU.subtract))
            dve.tensor_tensor(lbw[:, 1, :], l1, lbw[:, 6, :], ALU.subtract).then_inc(S("lb_in"), 1)
            dve.wait_ge(*at_count("lb_exp"))
            link(dve.tensor_tensor(lbw[:, 7, :], lbw[:, 2, :], lbw[:, 6, :], ALU.add))
            link(dve.reciprocal(lbw[:, 5, :], lbw[:, 7, :]))
            link(dve.tensor_tensor(lbw[:, 5, :], lbw[:, 5, :], lbw[:, 2, :], ALU.mult))
            dve.tensor_tensor(lbw[:, 4, :], lbw[:, 0, :], lbw[:, 1, :], ALU.subtract).then_inc(S("lb_sum"), 1)
            dve.wait_ge(*at_count("lb_ln"))
            link(dve.tensor_tensor(lbw[:, 3, :], lbw[:, 1, :], lbw[:, 7, :], ALU.subtract))
            dve.tensor_copy(PR[:, :, T_PROMPT + 1:T_PROMPT + 2].rearrange("p f a -> p (f a)"),
                            vec[:, V["shift"]:V["shift"] + RPC]).then_inc(S("shift_row"), 1)
            dve.wait_ge(*at_count("shift_row"))
            for f in range(RPC):
                if f % 2 == 0 and f:
                    dense_rest(AB_T + f // 2 + 1)
                dve.wait_ge(*at_count("ab_done", f + 1))
                link(dve.tensor_tensor(XS[:, f, 0:T_PROMPT], PR[:, f, 0:T_PROMPT], PR[:, f, 1:T_PROMPT + 1], ALU.subtract))
                link(dve.tensor_tensor(XS[:, f, T_PROMPT:T], PR[:, f, T_PROMPT + 1:T + 1],
                                       PR[:, f, T_PROMPT + 2:T + 2], ALU.subtract))
                dve.scalar_tensor_tensor(XS[:, f, 0:T_PROMPT], XS[:, f, 0:T_PROMPT], vcol("mu", f),
                                         PR[:, f, 1:T_PROMPT + 1], ALU.mult, ALU.add)
                dve.scalar_tensor_tensor(XS[:, f, T_PROMPT:T], XS[:, f, T_PROMPT:T], vcol("mu", f),
                                         PR[:, f, T_PROMPT + 2:T + 2], ALU.mult, ALU.add).then_inc(S("xs"), 1)
            dve.tensor_copy(last[:, 0, :], PR[:, :, T_PROMPT:T_PROMPT + 1].rearrange("p f a -> p (f a)"))\
               .then_inc(S("last_copied"), 1)
            dve.tensor_copy(last[:, 1, :], PR[:, :, T + 1:T + 2].rearrange("p f a -> p (f a)"))\
               .then_inc(S("last_copied"), 1)
            dense_rest(AB_T + 8)
            dve.wait_ge(*at_count("lora_done", RF))
            dve.wait_ge(*at_count("xs", RPC))
            dve.wait_ge(*at_count("last_copied", 2))
            link(dve.tensor_scalar(lw, lw, -DECAY_SCALE, None, ALU.mult))
            dve.wait_ge(*at_count("masks", 2))
            for f in range(RF):
                link(dve.tensor_tensor_scan(bT[:, f, :], reset[:, :], lw[:, f, :], 0.0, ALU.mult, ALU.add))
            dve.tensor_tensor(s1, bT, lw, ALU.subtract).then_inc(S("decay_sums"), 1)
            for f in range(RF):
                ins_ = dve.tensor_scalar(kkT[:, f, :], XS[:, 4 + f, :], vcol("rwkv_k_k", f), None, ALU.mult)
            link(ins_)
            dve.tensor_tensor(KT, kkT, kkT, ALU.mult).then_inc(S("kk_squares"), 1)
            dense_rest(AB_T + 9)
            dense_rest(AB_T + 10)
            dve.wait_ge(*at_count("lora_done", 2 * RF))
            for f in range(RF):
                dve.wait_ge(*at_count("kk_full", f + 1))
                dve.tensor_scalar(QT[:, f, :], where["kk", f][:, 0:T], 1e-24, None, ALU.max).then_inc(S("kk_norm"), 1)
            for f in range(RF):
                ins_ = dve.tensor_scalar(KT[:, f, :], aT[:, f, :], -1.0, vcol("rwkv_k_a", f), ALU.add, ALU.mult)
            link(ins_)
            link(dve.scalar_tensor_tensor(KT, KT, 1.0, XS[:, 4:8, :], ALU.add, ALU.mult))
            for f in range(RF):
                dve.scalar_tensor_tensor(oT[:, f, :], XS[:, f, :], vcol("rwkv_r_k", f), KT[:, f, :],
                                         ALU.mult, ALU.mult).then_inc(S("bonus_row"), 1)
            dve.wait_ge(*at_count("decay_exp", 4))
            link(dve.tensor_tensor(kkT, kkT, QT, ALU.mult))
            link(dve.tensor_tensor(QT, aT, kkT, ALU.mult))
            dve.wait_ge(*at_count("bonus_row", RF))
            dve.wait_ge(*at_count("decay_exp", 3))
            dve.tensor_tensor(PRC[:, :, 0, :], s2, kkT, ALU.mult).then_inc(S("bonus_in"), 1)
            dve.tensor_tensor(PRC[:, :, 1, :], s1, XS[:, 0:4, :], ALU.mult)
            dve.tensor_copy(dC[:, :, :], s1.rearrange("p f (c t) -> p f c t", c=NCH)[:, :, :, C - 1])
            dve.tensor_tensor(QT, QT, lw, ALU.mult)
            dve.tensor_tensor(KT, KT, lw, ALU.mult).then_inc(S("rwkv_ready"), 1)
            dense_rest(AB_T + 11)
            dense_rest(AB_T + 12)
            dve.wait_ge(*at_count("rwkv_ready"))
            for f in range(RF):
                dve.wait_ge(*at_count("bonus_full", f + 1))
                dve.tensor_tensor(BV[:, f, :], where["bonus", f][:, 0:T], XS[:, 8 + f, :], ALU.mult)\
                   .then_inc(S("bonus_done"), 1)
            link(dve.memset(H[:, :, :, :], 0.0))
            dve.wait_ge(*at_count("h0_full"))
            dve.tensor_copy(H[:, 1, :, :], where["h0", 0][:, :].rearrange("p (f n) -> p f n", f=RF))\
               .then_inc(S("h_init"), 1)
            dve.wait_ge(*at_count("h_init"))
            dve.wait_ge(*at_count("zero_blocks", 4))
            dve.wait_ge(*at_count("masks", 3))
            invf = [0]

            def inv_full():
                invf[0] += 1
                dve.wait_ge(*at_count("inv_full", invf[0]))

            def log_sigmoid(a, x, out, tile=None):
                dve.tensor_scalar(out, x, 0.0, None, ALU.min).then_inc(S(a["name"] + "_min"), 1)
                if tile is not None:
                    dense_rest(tile)
                dve.wait_ge(*at_count(a["name"] + "_softplus"))
                dve.wait_ge(*at_count(a["name"] + "_min"))
                link(dve.tensor_tensor(out, out, a["E"], ALU.subtract))

            def attention_start(a):
                n_, F, NH = a["name"], a["F"], a["heads"]
                pars = NH // F
                dve.memset(a["S"][:, 0], 0.0).then_inc(S(n_ + "_s_zero"), 1)
                dve.memset(a["S"][:, 1], 0.0).then_inc(S(n_ + "_s_zero"), 1)
                for f in range(F):
                    dve.tensor_tensor_scan(a["b"][:, f, :], reset[:, :], a["Z"][:, f, :], 0.0, ALU.mult, ALU.add)\
                       .then_inc(S(n_ + "_b"), 1)
                dve.wait_ge(*at_count(n_ + "_b", F))

            def select(a, lv):
                n_, F, NH = a["name"], a["F"], a["heads"]
                pars = NH // F
                for c in range(NCH):
                    for par in range(pars):
                        i = lv * NCH * pars + c * pars + par
                        dve.wait_ge(*at_count(n_ + "_sc_full", i + 1))
                        src = where[n_, "sc", i][0:C, 0:F * C].rearrange("p (f t) -> p f t", f=F)
                        dst = a["Sc"][0:C, c, par * F:(par + 1) * F, :]
                        if lv == 0:
                            ins_ = dve.tensor_tensor(dst, src, bc(ident[0:C, 0:C], 1, F), ALU.mult)
                        else:
                            dve.wait_ge(*at_count(n_ + "_sc", i + 1 - NCH * pars))
                            ins_ = dve.copy_predicated(dst, bc(upper[0:C, lv - 1, :].bitcast(I32), 1, F), src)
                        ins_.then_inc(S(n_ + "_sc"), 1)

            def level(a, lv):
                n_, F, NH = a["name"], a["F"], a["heads"]
                pars = NH // F
                L = 1 << lv
                hl = L // 2

                def blocks(x):
                    return x.rearrange("p f t -> p (f t)").rearrange("p (n l) -> p n l", l=L)

                zb = (a["Z"], a["KD"])[lv % 2]
                bb, eb, z_, q_, k_ = blocks(a["b"]), blocks(a["E"]), blocks(zb), blocks(a["q"]), blocks(a["k"])
                nb_ = F * T // L
                if lv > 1:
                    dve.wait_ge(*at_count(n_ + "_z", lv))
                dve.tensor_tensor(eb, bb, bb[:, :, hl - 1:hl].to_broadcast([P, nb_, L]), ALU.subtract)\
                   .then_inc(S(n_ + "_dist"), 1)
                if lv >= a["lag"]:
                    select(a, lv - a["lag"])
                dve.wait_ge(*at_count(n_ + "_e", lv))
                dve.tensor_tensor(z_[:, :, hl:L], eb[:, :, hl:L], q_[:, :, hl:L], ALU.mult)
                dve.tensor_tensor(z_[:, :, 0:hl], eb[:, :, 0:hl], k_[:, :, 0:hl], ALU.mult).then_inc(S(n_ + "_z"), 1)

            def chain_operands(a):
                n_, F, NH = a["name"], a["F"], a["heads"]
                pars = NH // F
                for lv in range(LEVELS + 1 - a["lag"], LEVELS + 1):
                    select(a, lv)
                dve.wait_ge(*at_count(n_ + "_z", LEVELS + 1))
                b4 = a["b"].rearrange("p f t -> p (f t)").rearrange("p (n l) -> p n l", l=C)
                kd = a["KD"].rearrange("p f t -> p (f t)").rearrange("p (n l) -> p n l", l=C)
                dve.tensor_tensor(kd, b4, b4[:, :, C - 1:C].to_broadcast([P, F * NCH, C]), ALU.subtract)\
                   .then_inc(S(n_ + "_dist"), 1)
                dve.wait_ge(*at_count(n_ + "_e", LEVELS + 1))
                dve.tensor_tensor(a["Z"], a["E"], a["q"], ALU.mult)
                dve.tensor_copy(ends[:, 0:F, :], a["E"].rearrange("p f (c t) -> p f c t", c=NCH)[:, :, :, C - 1])
                dve.wait_ge(*at_count(n_ + "_e", LEVELS + 2))
                dve.tensor_tensor(a["KD"], a["KD"], a["k"], ALU.mult).then_inc(S(n_ + "_qk"), 1)
                dve.wait_ge(*at_count(n_ + "_qk"))
                dve.wait_ge(*at_count(n_ + "_state_in", 16 * pars))

            def state_chain(a, c):
                n_, F, NH = a["name"], a["F"], a["heads"]
                pars = NH // F
                W = P // pars
                per = min(4 // pars, F)
                g = 0 if c < N_PROMPT_CH else 1
                if c:
                    dve.wait_ge(*at_count(n_ + "_s", c))
                for k0 in range(0, F, per):
                    i = c * (F // per) + k0 // per
                    dve.wait_ge(*at_count(n_ + "_ds_full", i + 1))
                    ps = where[n_, "ds", i]
                    for k in range(per):
                        f = k0 + k
                        for par in range(pars):
                            rows = slice(W * par, W * par + W)
                            st = a["S"][rows, g, f, par * P:(par + 1) * P]
                            up = dve.scalar_tensor_tensor(st, st, ends[rows, f, c:c + 1],
                                                          ps[rows, (k * pars + par) * P:(k * pars + par + 1) * P],
                                                          ALU.mult, ALU.add)
                up.then_inc(S(n_ + "_s"), 1)

            def attention_end(a):
                n_, F, NH = a["name"], a["F"], a["heads"]
                pars = NH // F
                dve.wait_ge(*at_count(n_ + "_o", NCH))
                dve.scalar_tensor_tensor(a["gate"], a["O"], vcol("gla_norm_w" if n_ == "gla" else "hgrn_norm_w"), a["gate"],
                                         ALU.mult, ALU.mult).then_inc(S(n_ + "_gated"), 1)
                dve.wait_ge(*at_count(n_ + "_gated"))
                dve.wait_ge(*at_count(n_ + "_osq"))
                for hh in range(NH):
                    dve.wait_ge(*at_count(n_ + "_rms", hh + 1))
                    link(dve.reciprocal(a["sq"][:, hh, :], a["sq"][:, hh, :]))
                    dve.tensor_tensor(a["O"][:, hh, :], a["gate"][:, hh, :], a["sq"][:, hh, :], ALU.mult)\
                       .then_inc(S(n_ + "_out"), 1)

            def gla_step(n):
                if n == 0:
                    log_sigmoid(gla, gla["b"], gla["KD"])
                    dve.tensor_scalar(gla["Z"], gla["KD"], 1.0 / GLA_TAU, None, ALU.mult).then_inc(S("gla_z"), 1)
                    dve.wait_ge(*at_count("gla_z"))
                    attention_start(gla)
                elif n <= LEVELS:
                    level(gla, n)
                else:
                    chain_operands(gla)

            for batch in BATCHES:
                first, nb = batch[0], len(batch)
                for bi, c in enumerate(batch):
                    for n, dst in enumerate((G1, G2)):
                        for par in range(2):
                            i = 6 * c + 2 * n + par
                            dve.wait_ge(*at_count("gram_full", i + 1))
                            src = where["gram", i][0:C, :].rearrange("p (f a t) -> p f a t", f=RF, a=2)
                            out = dst[0:C, bi, par * RF:(par + 1) * RF, :].rearrange("p f (a t) -> p f a t", a=2)
                            if n == 1:
                                rows = slice(64 * par, 64 * par + 64)
                                dve.tensor_tensor(At[rows, bi, :, rows], src[:, :, 0, :], bc(mask_pr[:, 0, :], 1, RF), ALU.mult)
                                dve.tensor_tensor(out[:, :, 1, :], src[:, :, 1, :], bc(mask_pr[:, 1, :], 1, RF), ALU.mult)\
                                   .then_inc(S("gram_done"), 1)
                            else:
                                dve.tensor_tensor(out, src, bc(mask_pr[:, :, :], 1, RF), ALU.mult).then_inc(S("gram_done"), 1)
                    for par in range(2):
                        rows = slice(64 * par, 64 * par + 64)
                        i = 6 * c + 4 + par
                        dve.wait_ge(*at_count("gram_full", i + 1))
                        dve.tensor_tensor(Tm[rows, bi, :, rows],
                                          where["gram", i][0:C, 0:RF * C].rearrange("p (f n) -> p f n", f=RF),
                                          bc(lower[0:C, 0, :], 1, RF), ALU.mult).then_inc(S("gram_done"), 1)
                    dve.wait_ge(*at_count("gram_done", 6 * c + 6))
                    for par in range(2):
                        rows = slice(64 * par, 64 * par + 64)
                        ins_ = dve.tensor_tensor(Tt[rows, bi, :, rows], At[rows, bi, :, rows], bc(upper[rows, 0, :], 1, RF),
                                                 ALU.mult)
                    link(ins_)
                    for par in range(2):
                        rows = slice(64 * par, 64 * par + 64)
                        for t_ in (Tm, Tt):
                            ins_ = dve.scalar_tensor_tensor(t_[rows, bi, :, rows], t_[rows, bi, :, rows], -1.0,
                                                            bc(ident[rows, rows], 1, RF), ALU.mult, ALU.add)
                    ins_.then_inc(S("inv_ready"), 1)

                def blocks_of(ap, par):
                    rows = slice(64 * par, 64 * par + 64)
                    return ap[rows, :].rearrange("p (f n) -> p f n", f=RF)[:, :, rows]

                for lv in range(1, LEVELS):
                    for bi, c in enumerate(batch):
                        inv_full()
                        for par in range(2):
                            rows = slice(64 * par, 64 * par + 64)
                            ins_ = dve.tensor_tensor(Xm[rows, bi, :, rows], blocks_of(where["X", lv, c], par),
                                                     bc(lower[rows, lv, :], 1, RF), ALU.mult)
                        ins_.then_inc(S("inv_x"), 1)
                    for bi, c in enumerate(batch):
                        dve.wait_ge(*at_count("inv_ready", LEVELS * first + (lv - 1) * nb + bi + 1))
                        if lv < LEVELS - 1:
                            inv_full()
                            inv_full()
                            for par in range(2):
                                rows = slice(64 * par, 64 * par + 64)
                                ins_ = dve.tensor_tensor(Tm[rows, bi, :, rows], Tm[rows, bi, :, rows],
                                                         blocks_of(where["Y", lv, c], par), ALU.subtract)
                            ins_.then_inc(S("inv_y"), 1)
                        else:
                            inv_full()
                        for par in range(2):
                            rows = slice(64 * par, 64 * par + 64)
                            dst = Tt[rows, bi, :, rows] if lv < LEVELS - 1 else inverse[0:C, bi, par * RF:(par + 1) * RF, :]
                            ins_ = dve.tensor_tensor(dst, Tt[rows, bi, :, rows], blocks_of(where["Yt", lv, c], par),
                                                     ALU.subtract)
                        ins_.then_inc(S("inv_ready"), 1)
                    if (first, lv) in GLA_AT:
                        gla_step(GLA_AT[first, lv])
                for bi, c in enumerate(batch):
                    g = 0 if c < N_PROMPT_CH else 1
                    dve.wait_ge(*at_count("seq_full", 4 * c + 1))
                    dve.tensor_copy(W1s[0:C, :], where["w1", c][0:C, :]).then_inc(S("w1_done"), 1)
                    dve.wait_ge(*at_count("seq_full", 4 * c + 2))
                    dve.tensor_scalar(Un[0:C, :], where["u", c][0:C, :], -1.0, None, ALU.mult).then_inc(S("u_done"), 1)
                    dve.wait_ge(*at_count("seq_full", 4 * c + 4))
                    for par in range(2):
                        rows = slice(64 * par, 64 * par + 64)
                        hs = H[rows, g, :, rows]
                        link(dve.tensor_tensor(hs, hs, where["dh", c][rows, :].rearrange("p (f n) -> p f n", f=RF)[:, :, rows],
                                               ALU.add))
                        mul = dve.tensor_tensor(hs, hs, dC[rows, :, c:c + 1].to_broadcast([64, RF, 64]), ALU.mult)
                    mul.then_inc(S("h_done"), 1)
                    dve.wait_ge(*at_count("h_done", c + 1))
            dve.wait_ge(*at_count("o_done", NCH))
            o3 = Osb[0:C].rearrange("p c h n -> p (c h) n")
            q3 = Osq[0:C].rearrange("p c h n -> p (c h) n")
            G40 = NCH * RH

            def wide(ap):
                return bc(ap, 2, RN)

            link(dve.tensor_reduce(stat[:, 0, :], o3, AX.X, ALU.add))
            link(dve.tensor_scalar(stat[:, 0, :], stat[:, 0, :], 1.0 / RN, None, ALU.mult))
            dve.tensor_tensor(o3, o3, wide(stat[:, 0, :]), ALU.subtract).then_inc(S("gn_centered"), 1)
            state_chain(gla, 0)
            dve.wait_ge(*at_count("gn_squares"))
            dve.tensor_reduce(stat[:, 1, :], q3, AX.X, ALU.add).then_inc(S("gn_sums"), 1)
            state_chain(gla, 1)
            dve.wait_ge(*at_count("gn_std"))
            link(dve.reciprocal(stat[:, 0, :], stat[:, 1, :]))
            dve.tensor_tensor(o3, o3, wide(stat[:, 0, :]), ALU.mult).then_inc(S("gn_done"), 1)
            state_chain(gla, 2)
            dve.wait_ge(*at_count("ot_done", NCH))
            dve.wait_ge(*at_count("bonus_done", RF))
            dve.wait_ge(*at_count("lora_done", 3 * RF))
            for f in range(RF):
                dve.tensor_scalar(oT[:, f, :], oT[:, f, :], vcol("rwkv_gn_w", f), vcol("rwkv_gn_b", f), ALU.mult, ALU.add)\
                   .then_inc(S("gn_scaled"), 1)
            dve.wait_ge(*at_count("gn_scaled", RF))
            link(dve.tensor_tensor(oT[:, 0:RF, :], oT[:, 0:RF, :], BV, ALU.add))
            dve.tensor_tensor(oT[:, 0:RF, :], oT[:, 0:RF, :], GT, ALU.mult).then_inc(S("rwkv_out"), 1)

            def layer_norm(n_, g_):
                r_, q_ = res_of(n_), sq_of(n_)
                dve.wait_ge(*at_count(n_ + "_ln_full", 1))
                for k in range(KC):
                    dve.scalar_tensor_tensor(r_[:, k, :], where[n_, "sum"][:, 0:T], -1.0 / D, r_[:, k, :], ALU.mult, ALU.add)\
                       .then_inc(S(n_ + "_centered"), 1)
                dve.wait_ge(*at_count(n_ + "_std"))
                dve.wait_ge(*at_count(n_ + "_centered", KC))
                link(dve.reciprocal(mean[:, :], mean[:, :]))
                for k in range(KC):
                    dve.scalar_tensor_tensor(r_[:, k, :], r_[:, k, :], vcol(g_, k), mean[:, :], ALU.mult, ALU.mult)\
                       .then_inc(S(n_ + "_scaled"), 1)

            def residual(full, taken, name, next_tiles):
                for j in range(KC):
                    for i in next_tiles[j]:
                        dense_rest(i)
                    dve.wait_ge(*at_count(full, j + 1))
                    dve.scalar_tensor_tensor(res[:, j, :], xT[:, j, :], ALPHA, where[name, j][:, 0:T],
                                             ALU.mult, ALU.add).then_inc(S(taken), 1)
                dve.wait_ge(*at_count(taken, KC))

            state_chain(gla, 3)
            state_chain(gla, 4)
            attention_end(gla)
            dense_rest(OUT_T)
            input_rest(1, oT)
            residual("out_ab_full", "ab_res", "out_ab", ahead(OUT_T + 1, 1, KC))
            layer_norm("ab", "ln_ab_g")
            input_rest(2, xT)
            for j in range(FC):
                if j % 2 == 0:
                    dense_rest(FFN_T + j + 1)
                    dense_rest(FFN_T + j + 2)
                dve.wait_ge(*at_count("h3_full", j + 1))
                dve.wait_ge(*at_count("h1_done", j + 1))
                g_ = ff_g[:, j % 2, :]
                if j >= 2:
                    dve.wait_ge(*at_count("hid_lo", j - 1))
                hi_, lo_ = hid_hi[j // HID_PART][:, j % HID_PART, :], hid_lo[j // HID_PART][:, j % HID_PART, :]
                dve.tensor_tensor(g_, ff_s[:, j % 4, :], where["h3", j][:, 0:T], ALU.mult).then_inc(S("ffn_g"), 1)
                dve.wait_ge(*at_count("ffn_g", j + 1))
                link(dve.tensor_copy(hi_, g_))
                dve.tensor_tensor(lo_, g_, hi_, ALU.subtract).then_inc(S("hid_lo"), 1)
            residual("w2_full", "ffn_res", "w2", ahead(W2_T + 1, 3, KC))
            layer_norm("ffn", "ln_ffn_g")
            input_rest(3, xT)
            for i in range(INC_T + 1, INC_T + 5):
                dense_rest(i)
            dve.wait_ge(*at_count("in_c_done", 8))
            log_sigmoid(hgrn, hf, hgrn["KD"], INC_T + 5)
            for k in range(HH):
                ins_ = dve.tensor_scalar(hgrn["Z"][:, k, :], hgrn["KD"][:, k, :], lbw[:, 4, k:k + 1], None, ALU.add)
            ins_.then_inc(S("hgrn_gap"), 1)
            dense_rest(INC_T + 6)
            dve.wait_ge(*at_count("hgrn_gap"))
            link(dve.tensor_scalar(hgrn["KD"], hgrn["Z"], 0.0, None, ALU.max))
            dense_rest(INC_T + 7)
            dve.wait_ge(*at_count("hgrn_softplus", 2))
            link(dve.tensor_tensor(hgrn["Z"], hgrn["KD"], hgrn["E"], ALU.add))
            dve.wait_ge(*at_count("hgrn_sig"))
            dve.wait_ge(*at_count("in_c_done", 16))
            for k in range(HH):
                dve.tensor_scalar(hgrn["Z"][:, k, :], hgrn["Z"][:, k, :], lbw[:, 3, k:k + 1], 0.0, ALU.add, ALU.min)
                ins_ = dve.tensor_scalar(hf[:, k, :], hf[:, k, :], lbw[:, 5, k:k + 1], None, ALU.mult)
            ins_.then_inc(S("hgrn_z"), 1)
            for i in range(INC_T + 8, INC_T + 12):
                dense_rest(i)
            dve.wait_ge(*at_count("hgrn_z"))
            attention_start(hgrn)
            for lv in range(1, LEVELS + 1):
                level(hgrn, lv)
                if IN_C_FIRST + lv <= 4 * KC // 2:
                    dense_rest(INC_T + IN_C_FIRST + lv)
            chain_operands(hgrn)
            for c in range(NCH):
                state_chain(hgrn, c)
            attention_end(hgrn)
            input_rest(4, hq)
            residual("out_c_full", "c_res", "out_c", ahead(OUTC_T + 1, 1, KC - 2))
            layer_norm("c", "ln_c_g")

            dve.wait_ge(*at_count("c_ln", KC))
            link(dve.memset(lg[:, :, :], 0.0))
            dve.memset(xtok[:, 2, :], 0.0).then_inc(S("xtok_zero"), 1)
            for i, (t0, n) in enumerate(TILES):
                dve.wait_ge(*at_count("logit_full", i + 1))
                dve.tensor_copy(lg[0:n, i, :], where["logit", i][0:n, 0:NE]).then_inc(S("logits_done"), 1)
            dve.wait_ge(*at_count("logits_done", 3))
            sel, pr_, wp = rt[:, 0], rt[:, 1], rt[:, 2]
            t3 = rt[:, 3, :, 0:1].rearrange("p i a -> p (i a)")
            t4 = rt[:, 4, :, 0:1].rearrange("p i a -> p (i a)")
            link(dve.tensor_reduce(t3, lg[:, :, :], AX.X, ALU.max))
            dve.tensor_tensor(lg[:, :, :], lg[:, :, :], rt[:, 3, :, 0:1].to_broadcast([P, 3, NE]), ALU.subtract)\
               .then_inc(S("logits_shifted"), 1)
            dve.wait_ge(*at_count("router_exp"))
            link(dve.tensor_reduce(t3, pr_, AX.X, ALU.add))
            link(dve.reciprocal(t4, t3))
            link(dve.tensor_tensor(pr_, pr_, rt[:, 4, :, 0:1].to_broadcast([P, 3, NE]), ALU.mult))
            pj = bc(pr_, 2, NE)
            pi = bc(pr_, 3, NE)
            g4 = pair[:, 0].rearrange("p i (a b) -> p i a b", a=NE)
            e4 = pair[:, 1].rearrange("p i (a b) -> p i a b", a=NE)
            dve.tensor_tensor(g4, pj, pi, ALU.is_gt)
            link(dve.tensor_tensor(e4, pj, pi, ALU.is_equal))
            link(dve.tensor_tensor(e4, e4, bc(jlt[:, :, :], 1, 3), ALU.mult))
            link(dve.tensor_tensor(g4, g4, e4, ALU.add))
            link(dve.tensor_reduce(rt[:, 5], g4, AX.X, ALU.add))
            link(dve.tensor_scalar(sel, rt[:, 5], 1.5, None, ALU.is_lt))
            link(dve.memset(rt[64:P, 0, 2, :], 0.0))
            link(dve.tensor_tensor(wp, sel, pr_, ALU.mult))
            link(dve.tensor_reduce(t3, wp, AX.X, ALU.add))
            link(dve.tensor_scalar(t3, t3, 1e-30, None, ALU.max))
            link(dve.reciprocal(t4, t3))
            link(dve.tensor_tensor(wts[:, :, :].rearrange("p e i -> p i e"), wp, rt[:, 4, :, 0:1].to_broadcast([P, 3, NE]), ALU.mult))
            dve.tensor_scalar(rt[:, 6], sel, -1.0, 1e6, ALU.add, ALU.mult).then_inc(S("chosen"), 1)
            dve.wait_ge(*at_count("chosen"))
            for i in range(3):
                dve.wait_ge(*at_count("pos_full", i + 1))
                dve.tensor_tensor(pos[:, :, i:i + 1].rearrange("p e a -> p (e a)"), where["pos", i][:, 0:NE],
                                  rt[:, 6, i, :], ALU.add).then_inc(S("pos_done"), 1)
            dve.wait_ge(*at_count("pos_full", 4))
            dve.tensor_copy(cnt[:, :], where["count", 0][:, 0:NE]).then_inc(S("pos_done"), 1)
            dve.wait_ge(*at_count("pos_done", 4))
            def residual_and_extras():
                for k in range(KC):
                    dve.tensor_scalar(acc[:, k, :], xT[:, k, :], ALPHA, None, ALU.mult).then_inc(S("acc_ready"), 1)
                for r_ in range(1, MAX_BLOCKS):
                    ins_ = dve.tensor_scalar(cand[:, 0, (r_ - 1) * NE:r_ * NE], cnt[:, :], BLK * r_ + 0.5, None, ALU.is_gt)
                link(ins_)
                link(dve.tensor_tensor_scan(cand[:, 1, :], ones[:, 0:NX], cand[:, 0, :], 0.0, ALU.mult, ALU.add))
                link(dve.tensor_tensor(cand[:, 1, :], cand[:, 1, :], cand[:, 0, :], ALU.mult))
                link(dve.tensor_scalar(cand[:, 1, :], cand[:, 1, :], -1.0, None, ALU.add))
                for src, dst in ((2, extra_i[:, 0, :]), (3, bases[:, :])):
                    link(dve.tensor_tensor(compact[:, :, :], bc(cand[:, 1, :], 1, NX), bc(slots[:, 0:NX], 2, NX), ALU.is_equal))
                    link(dve.tensor_tensor(compact[:, :, :], compact[:, :, :], bc(cand[:, src, :], 1, NX), ALU.mult))
                    link(dve.tensor_reduce(cand[:, 4, :], compact[:, :, :], AX.X, ALU.add))
                    link(dve.tensor_copy(dst, cand[:, 4, :]))
                link(dve.tensor_reduce(cand[:, 5, 0:1], cand[:, 0, :], AX.X, ALU.add))
                dve.tensor_copy(n_extra[:, 0:1], cand[:, 5, 0:1]).then_inc(S("extras_known"), 1)

            def weight_rest(n, i):
                dve.wait_ge(S("e_hi"), HALVES * n + i + 1)
                dve.tensor_tensor(w_lo[:, i % UNITS, :], moe_ring[:, MOE_RING - 1 - i % MOE_RING, :], w_hi[:, i % UNITS, :], ALU.subtract)\
                   .then_inc(S("e_lo"), 1)

            def add_rows(n, k, b):
                dve.wait_ge(S("e_scatter"), KC * (n - 1) + k + 1)
                dve.tensor_tensor(acc[:, k, :], acc[:, k, :], b[:, 0:T], ALU.add).then_inc(S("e_added"), 1)

            def expert_block(n, e, j_extra):
                later = not isinstance(n, int)
                if later:
                    dve.wait_ge(S("e_pickt_full"), n)
                dve.tensor_copy(wcur[:, :].unsqueeze(1), wts[:, bass.ds(e, 1), :]).then_inc(S("e_col"), 1)
                if j_extra is None:
                    dve.tensor_copy(cur[:, :].unsqueeze(1), pos[:, bass.ds(e, 1), :]).then_inc(S("e_col"), 1)
                else:
                    dve.tensor_tensor(cur[:, :].unsqueeze(1), pos[:, bass.ds(e, 1), :],
                                      bases[:, bass.ds(j_extra, 1)].unsqueeze(2).to_broadcast([P, 1, 3]), ALU.subtract)\
                       .then_inc(S("e_col"), 1)
                dve.wait_ge(S("e_col"), n * 2 + 2)
                for i in range(3):
                    ins_ = dve.tensor_scalar(pick[:, i, :], slots[:, :], cur[:, i:i + 1], None, ALU.is_equal)
                ins_.then_inc(S("e_map"), 1)
                dve.wait_ge(S("e_map"), n + 1)
                for i in range(3):
                    ins_ = dve.tensor_scalar(pickw[:, i, :], pick[:, i, :], wcur[:, i:i + 1], None, ALU.mult)
                ins_.then_inc(S("e_pick"), 1)

                def hidden(s):
                    dve.wait_ge(S("e_silu"), n * STRIPS + s + 1)
                    dve.wait_ge(S("e_used"), n * HALVES + 2 * UP3[s] + 2)
                    if s:
                        dve.wait_ge(S("e_gt_full"), n * STRIPS + s)
                    dve.tensor_tensor(eg[:, :], eh[:, s % 2, :], E_H3[s % 2][:, 0:SC], ALU.mult).then_inc(S("e_g"), 1)

                def hidden_rest(s):
                    dve.wait_ge(S("e_gt_hi"), n * STRIPS + s + 1)
                    dve.tensor_tensor(gt_lo[:, :, :], E_SCR[0][:, 0:2 * BLK].rearrange("p (j n) -> p j n", j=2),
                                      gt_hi[:, :, :], ALU.subtract).then_inc(S("e_gt"), 1)

                weight_rest(n, 0)
                weight_rest(n, 1)
                for half in range(2):
                    dve.wait_ge(S("e_rows_hi"), n * 2 + half + 1)
                    dve.tensor_tensor(xe_lo[:, 4 * half:4 * half + 4, :], E_SCR[half][:, :].rearrange("p (k n) -> p k n", k=4),
                                      xe_hi[:, 4 * half:4 * half + 4, :], ALU.subtract).then_inc(S("e_rows"), 1)
                    weight_rest(n, 2 + half)
                weight_rest(n, 4)
                weight_rest(n, 5)
                hidden(0)
                weight_rest(n, 6)
                weight_rest(n, 7)
                for s in range(1, STRIPS):
                    weight_rest(n, 6 * s + 2)
                    weight_rest(n, 6 * s + 3)
                    hidden_rest(s - 1)
                    weight_rest(n, 6 * s + 4)
                    weight_rest(n, 6 * s + 5)
                    hidden(s)
                    if s < STRIPS - 1:
                        weight_rest(n, 6 * s + 6)
                        weight_rest(n, 6 * s + 7)
                    if not later and s == 1:
                        residual_and_extras()
                    if later and s <= KC:
                        add_rows(n, s - 1, E_SCR[1])
                hidden_rest(STRIPS - 1)

            def last_rows(n):
                for k in range(KC):
                    add_rows(n, k, bank[k % 4])
                dve.wait_ge(S("e_added"), KC * n)

            expert_loops(dve, expert_block, last_rows)
            layer_norm("moe", "ln_moe_g")

        @block.scalar
        def _(act):
            chain = [0]

            def link(ins_):
                chain[0] += 1
                ins_.then_inc(S("act_chain"), 1)
                act.wait_ge(S("act_chain"), chain[0])

            def dense_rounded(i):
                act.wait_ge(*at_count(f"tile_in{i % DENSE_RING}", 16 * (i // DENSE_RING + 1)))
                for m_ in (2 * i, 2 * i + 1):
                    before = m_ - DENSE_UNITS
                    if before >= 0 and before % 2 == 0:
                        act.wait_ge(*at_count("dense_half", before // 2 + 1))
                    elif before >= 0:
                        act.wait_ge(*at_count(tiles[before // 2][2], tiles[before // 2][3]))
                    src, words = half_of(m_)
                    act.activation(wd_hi[:, m_ % DENSE_UNITS, 0:words], src, ACT.Copy).then_inc(S("dense_hi"), 1)

            def input_rounded(x, ready):
                for k in range(KC):
                    act.wait_ge(*ready(k))
                    act.activation(in_hi[:, k, :], x[:, k, :], ACT.Copy).then_inc(S("in_hi"), 1)

            dense_rounded(AB_T)
            for k in range(KC):
                act.wait_ge(*at_count("x_full", k + 1))
                act.activation(in_hi[:, k, :], where["x", k][:, 0:T], ACT.Copy).then_inc(S("in_hi"), 1)
                act.activation(xT[:, k, :], where["x", k][:, 0:T], ACT.Copy).then_inc(S("x_done"), 1)
            dense_rounded(AB_T + 1)
            for t in range(2):
                act.wait_ge(*at_count("vec_full", t + 1))
                o = 0 if t == 0 else 91
                act.activation(vec[:, o:o + at[t]], where["vec", t][:, 0:at[t]], ACT.Copy).then_inc(S("vec_done"), 1)
            act.wait_ge(*at_count("lb_in"))
            link(act.activation(lbw[:, 2, :], lbw[:, 0, :], ACT.Exp))
            act.activation(lbw[:, 6, :], lbw[:, 1, :], ACT.Exp).then_inc(S("lb_exp"), 1)
            act.wait_ge(*at_count("lb_sum", 1))
            act.activation(lbw[:, 7, :], lbw[:, 7, :], ACT.Ln).then_inc(S("lb_ln"), 1)
            act.wait_ge(*at_count("pr_zero"))
            dests = [None] * RPC + [gq[:, 0], gq[:, 1], gk[:, 0], gk[:, 1]] + [gv[:, i] for i in range(4)] + \
                    [gog[:, i] for i in range(4)]

            def projected(i):
                for j in (2 * i, 2 * i + 1):
                    act.wait_ge(*at_count("ab_full", j + 1))
                    b = where["ab", j]
                    if dests[j] is None:
                        act.activation(PR[:, j, 1:T_PROMPT + 1], b[:, 0:T_PROMPT], ACT.Copy)
                        act.activation(PR[:, j, T_PROMPT + 2:T + 2], b[:, T_PROMPT:T], ACT.Copy).then_inc(S("ab_done"), 1)
                    else:
                        fn = ACT.Silu if j >= RPC + 8 else ACT.Copy
                        act.activation(dests[j], b[:, 0:T], fn, scale=GDK ** -0.5 if j < RPC + 2 else 1.0)\
                           .then_inc(S("ab_done"), 1)

            for i in range(RPC // 2 + 1):
                if i:
                    dense_rounded(AB_T + i + 1)
                projected(i)
            act.wait_ge(*at_count("xs", RPC))
            act.wait_ge(*at_count("last_copied", 2))
            act.activation(XS[0:64, 12, :], XS[0:64, 12, :], ACT.Tanh).then_inc(S("lora_in"), 1)
            act.activation(XS[:, 13, :], XS[:, 13, :], ACT.Sigmoid).then_inc(S("lora_in"), 1)
            for n in range(3 * RF):
                act.wait_ge(*at_count("lora_full", n + 1))
                f, b = n % RF, where["lora", n][:, 0:T]
                if n < RF:
                    ins_ = act.activation(lw[:, f, :], b, ACT.Sigmoid, bias=vcol("rwkv_w0", f))
                elif n < 2 * RF:
                    ins_ = act.activation(aT[:, f, :], b, ACT.Sigmoid, bias=vcol("rwkv_a0", f))
                else:
                    ins_ = act.activation(GT[:, f, :], b, ACT.Copy)
                ins_.then_inc(S("lora_done"), 1)
            dense_rounded(AB_T + 9)
            act.wait_ge(*at_count("decay_sums"))
            act.activation(s2, s1, ACT.Exp).then_inc(S("decay_exp"), 1)
            act.wait_ge(*at_count("decay_exp", 1))
            act.activation(s1, bT, ACT.Exp).then_inc(S("decay_exp"), 1)
            act.activation(lw, bT, ACT.Exp, scale=-1.0).then_inc(S("decay_exp"), 1)
            projected(8)
            dense_rounded(AB_T + 10)
            act.wait_ge(*at_count("kk_norm", RF))
            link(act.activation(QT, QT, ACT.Ln))
            act.activation(QT, QT, ACT.Exp, scale=-0.5).then_inc(S("decay_exp"), 1)
            for g in range(2):
                act.wait_ge(*at_count("last_full", g + 1))
                act.activation(lrow[:, g, :], where["last", g][0:RPC, 0:P], ACT.Copy).then_inc(S("last_rows"), 1)
            projected(9)
            dense_rounded(AB_T + 11)
            projected(10)
            dense_rounded(AB_T + 12)
            projected(11)
            projected(12)
            act.wait_ge(*at_count("ab_full", len(dests) + 1))
            act.activation(gz_s[:, :], where["ab", len(dests)][0:GR, 0:T], ACT.Copy).then_inc(S("ab_done"), 1)
            for f in range(2):
                act.wait_ge(*at_count("gate_full", f + 1))
                act.activation(gla_b[:, f, :], where["gate", f][:, 0:T], ACT.Identity, bias=vcol("gla_gate_b", f))\
                   .then_inc(S("gate_done"), 1)
            def in_c(i):
                for j in (2 * i, 2 * i + 1):
                    act.wait_ge(*at_count("in_c_full", j + 1))
                    dst = (hf, hq, hi, hg)[j // KC][:, j % KC, :]
                    act.activation(dst, where["in_c", j][:, 0:T], ACT.Silu if j // KC in (1, 3) else ACT.Copy)\
                       .then_inc(S("in_c_done"), 1)

            def softplus_neg_abs(a, x, tile=None):
                link(act.activation(a["E"], x, ACT.Abs))
                if tile is not None:
                    dense_rounded(INC_T + tile + 1)
                link(act.activation(a["E"], a["E"], ACT.Exp, scale=-1.0))
                if tile is not None:
                    in_c(tile)
                act.activation(a["E"], a["E"], ACT.Ln, bias=1.0).then_inc(S(a["name"] + "_softplus"), 1)

            def level(a, lv):
                n_ = a["name"]
                L = 1 << lv
                hl = L // 2
                eb = a["E"].rearrange("p f t -> p (f t)").rearrange("p (n l) -> p n l", l=L)
                act.wait_ge(*at_count(n_ + "_dist", lv))
                act.activation(eb[:, :, hl:L], eb[:, :, hl:L], ACT.Exp)
                act.activation(eb[:, :, 0:hl], eb[:, :, 0:hl], ACT.Exp, scale=-1.0).then_inc(S(n_ + "_e"), 1)

            def chain_operands(a):
                n_ = a["name"]
                act.wait_ge(*at_count(n_ + "_dist", LEVELS + 1))
                act.activation(a["E"], a["b"], ACT.Exp).then_inc(S(n_ + "_e"), 1)
                act.activation(a["KD"], a["KD"], ACT.Exp, scale=-1.0).then_inc(S(n_ + "_e"), 1)

            def state_chain(a, c):
                n_, F, NH = a["name"], a["F"], a["heads"]
                pars = NH // F
                tv = 2 * c if a["TVs"] is None else 2 * NCH + 2 * c
                for dst, cnt_ in (((a["TV"], NH),) if a["TVs"] is None else ()) + ((a["TK"], F),):
                    for k0 in range(0, cnt_, 4):
                        m_ = min(4, cnt_ - k0)
                        tv += 1
                        act.wait_ge(*at_count(n_ + "_tm_full", tv))
                        act.activation(dst[0:C, k0 * P:(k0 + m_) * P], where[n_, "tm", tv - 1][0:C, 0:m_ * P], ACT.Copy)\
                           .then_inc(S(n_ + "_tm"), 1)
                act.wait_ge(*at_count(n_ + "_o_full", c + 1))
                act.activation(a["O"][:, :, chunk(c)],
                               where[n_, "o", c][:, 0:NH * C].rearrange("p (h t) -> p h t", h=NH), ACT.Copy)\
                   .then_inc(S(n_ + "_o"), 1)

            def attention_end(a):
                n_, F, NH = a["name"], a["F"], a["heads"]
                pars = NH // F
                act.wait_ge(*at_count(n_ + "_o", NCH))
                act.wait_ge(*at_count(n_ + "_ds_full", NCH * F * pars // 4))
                act.activation(a["sq"], a["O"], ACT.Square).then_inc(S(n_ + "_osq"), 1)
                for hh in range(NH):
                    act.wait_ge(*at_count(n_ + "_rms_full", hh + 1))
                    act.activation(a["sq"][:, hh, :], where[n_, "rms", hh][:, 0:T], ACT.Sqrt,
                                   bias=eps_norm[:, :], scale=1.0 / a["vdim"]).then_inc(S(n_ + "_rms"), 1)

            for batch in BATCHES:
                for bi, c in enumerate(batch):
                    for n, dst in enumerate((TV, TQ, TK)):
                        act.wait_ge(*at_count("tm_full", 3 * c + n + 1))
                        act.activation(dst[0:C, bi, :], where["tm", 3 * c + n][0:C, :], ACT.Copy).then_inc(S("tm_done"), 1)
                for (batch_first, _), n in GLA_AT.items():
                    if batch_first != batch[0]:
                        continue
                    if n == 0:
                        softplus_neg_abs(gla, gla["b"])
                    elif n <= LEVELS:
                        level(gla, n)
                    else:
                        chain_operands(gla)
                for bi, c in enumerate(batch):
                    act.wait_ge(*at_count("seq_full", 4 * c + 3))
                    act.activation(Osb[0:C, c].rearrange("p h n -> p (h n)"), where["o", c][0:C, :], ACT.Copy)\
                       .then_inc(S("o_done"), 1)
            for g in range(2):
                act.wait_ge(*at_count("hout_full", g + 1))
                act.activation(Hout[:, g].rearrange("p f n -> p (f n)"), where["hout", g][:, :], ACT.Copy)\
                   .then_inc(S("hout_done"), 1)
            act.wait_ge(*at_count("gn_centered"))
            o3 = Osb[0:C].rearrange("p c h n -> p (c h n)")
            act.activation(Osq[0:C].rearrange("p c h n -> p (c h n)"), o3, ACT.Square).then_inc(S("gn_squares"), 1)
            state_chain(gla, 0)
            act.wait_ge(*at_count("gn_sums"))
            act.activation(stat[:, 1, :], stat[:, 1, :], ACT.Sqrt, bias=eps_gn[0:C, :], scale=1.0 / RN).then_inc(S("gn_std"), 1)
            state_chain(gla, 1)
            state_chain(gla, 2)
            for c in range(NCH):
                act.wait_ge(*at_count("ot_full", c + 1))
                act.activation(oT[:, 0:RF, chunk(c)], where["ot", c][:, 0:RF * C].rearrange("p (f t) -> p f t", f=RF),
                               ACT.Copy).then_inc(S("ot_done"), 1)

            def layer_norm(n_, stage=None):
                for k in range(KC):
                    act.wait_ge(*at_count(n_ + "_centered", k + 1))
                    act.activation(sq_of(n_)[:, k, :], res_of(n_)[:, k, :], ACT.Square).then_inc(S(n_ + "_sq"), 1)
                act.wait_ge(*at_count(n_ + "_ln_full", 2))
                act.activation(mean[:, :], where[n_, "sqs"][:, 0:T], ACT.Sqrt, bias=eps_norm[:, :], scale=1.0 / D)\
                   .then_inc(S(n_ + "_std"), 1)
                for k in range(KC):
                    act.wait_ge(*at_count(n_ + "_scaled", k + 1))
                    r_ = res_of(n_)[:, k, :]
                    act.activation(xT[:, k, :], r_, ACT.Identity, bias=vcol(f"ln_{n_}_b", k)).then_inc(S(n_ + "_ln"), 1)
                    if stage is not None:
                        act.activation(in_hi[:, k, :], r_, ACT.Identity, bias=vcol(f"ln_{n_}_b", k)).then_inc(S("in_hi"), 1)

            for c in range(3, NCH):
                state_chain(gla, c)
            attention_end(gla)
            act.wait_ge(*at_count("rwkv_out"))
            dense_rounded(OUT_T)
            input_rounded(oT, lambda k: at_count("rwkv_out") if k < RF else at_count("gla_out", k - RF + 1))
            for i in range(OUT_T + 1, FFN_T + 1):
                dense_rounded(i)
            layer_norm("ab", 2)
            for j in range(FC):
                dense_rounded(FFN_T + j + 1)
                if j % 2 == 0:
                    for jj in (j, j + 1):
                        act.wait_ge(*at_count("h1_full", jj + 1))
                        if jj >= 4:
                            act.wait_ge(*at_count("ffn_g", jj - 3))
                        act.activation(ff_s[:, jj % 4, :], where["h1", jj][:, 0:T], ACT.Silu).then_inc(S("h1_done"), 1)
            for i in range(W2_T + 1, INC_T + 1):
                dense_rounded(i)
            layer_norm("ffn", 3)

            for i in range(4):
                dense_rounded(INC_T + i + 1)
                in_c(i)
            act.wait_ge(*at_count("in_c_done", 8))
            softplus_neg_abs(hgrn, hf, 4)
            act.wait_ge(*at_count("hgrn_min"))
            act.activation(hf, hf, ACT.Sigmoid, scale=-1.0).then_inc(S("hgrn_sig"), 1)
            dense_rounded(INC_T + 6)
            in_c(5)
            act.wait_ge(*at_count("hgrn_gap"))
            softplus_neg_abs(hgrn, hgrn["Z"], 6)
            for i in range(7, 10):
                dense_rounded(INC_T + i + 1)
                in_c(i)
            dense_rounded(INC_T + 11)

            def rest_of_in_c(lv):
                if IN_C_FIRST + lv - 2 < 4 * KC // 2:
                    in_c(IN_C_FIRST + lv - 2)
                if IN_C_FIRST + lv <= 4 * KC // 2:
                    dense_rounded(INC_T + IN_C_FIRST + lv)
                if lv == LEVELS:
                    for i in range(2 * NCH):
                        act.wait_ge(*at_count("hgrn_tm_full", i + 1))
                        act.activation(hgrn["TVs"][0:C, i // 2, (i % 2) * 512:(i % 2 + 1) * 512],
                                       where["hgrn", "tm", i][0:C, :], ACT.Copy).then_inc(S("hgrn_tm"), 1)

            for lv in range(1, LEVELS + 1):
                level(hgrn, lv)
                rest_of_in_c(lv)
            chain_operands(hgrn)
            for c in range(NCH):
                state_chain(hgrn, c)
            attention_end(hgrn)
            input_rounded(hq, lambda k: at_count("hgrn_out", k + 1))
            for i in range(OUTC_T + 1, ND):
                dense_rounded(i)
            layer_norm("c")
            act.wait_ge(*at_count("xtok_zero"))
            for j in range(6):
                act.wait_ge(*at_count("xtok_full", j + 1))
                n = TILES[j // 2][1]
                act.activation(xtok[0:n, j // 2, (j % 2) * 512:(j % 2 + 1) * 512], where["xtok", j][0:n, :], ACT.Copy)\
                   .then_inc(S("xtok_done"), 1)
            act.wait_ge(*at_count("logits_shifted"))
            act.activation(rt[:, 1], lg[:, :, :], ACT.Exp).then_inc(S("router_exp"), 1)

            def weight_rounded(n, i):
                act.wait_ge(*at_count(f"moe_in{i % MOE_RING}", 16 * (n * (HALVES // MOE_RING) + i // MOE_RING + 1)))
                if i >= UNITS or not isinstance(n, int):
                    act.wait_ge(S("e_used"), n * HALVES + i - UNITS + 1)
                act.activation(w_hi[:, i % UNITS, :], moe_ring[:, MOE_RING - 1 - i % MOE_RING, :], ACT.Copy).then_inc(S("e_hi"), 1)

            def outputs(n):
                act.wait_ge(S("e_used"), n * HALVES)
                for half in range(2):
                    act.activation(ey[:, half * 512:(half + 1) * 512], E_Y[half][:, :], ACT.Copy).then_inc(S("e_y"), 1)

            def expert_block(n, e, j_extra):
                later = not isinstance(n, int)

                def silu(s):
                    act.wait_ge(S("e_used"), n * HALVES + 2 * UP1[s] + 2)
                    if s >= 2:
                        act.wait_ge(S("e_g"), n * STRIPS + s - 1)
                    act.activation(eh[:, s % 2, :], E_H1[s % 2][:, 0:SC], ACT.Silu).then_inc(S("e_silu"), 1)

                def hidden_rounded(s):
                    act.wait_ge(S("e_gt_full"), n * STRIPS + s + 1)
                    act.activation(gt_hi[:, :, :], E_SCR[0][:, 0:2 * BLK].rearrange("p (j n) -> p j n", j=2), ACT.Copy)\
                       .then_inc(S("e_gt_hi"), 1)

                for i in range(4):
                    weight_rounded(n, i)
                if later:
                    outputs(n)
                for half in range(2):
                    act.wait_ge(S("e_gather_full"), n * 2 + half + 1)
                    act.activation(xe_hi[:, 4 * half:4 * half + 4, :], E_SCR[half][:, :].rearrange("p (k n) -> p k n", k=4),
                                   ACT.Copy).then_inc(S("e_rows_hi"), 1)
                weight_rounded(n, 4)
                weight_rounded(n, 5)
                silu(0)
                weight_rounded(n, 6)
                weight_rounded(n, 7)
                for s in range(1, STRIPS):
                    weight_rounded(n, 6 * s + 2)
                    weight_rounded(n, 6 * s + 3)
                    silu(s)
                    hidden_rounded(s - 1)
                    weight_rounded(n, 6 * s + 4)
                    weight_rounded(n, 6 * s + 5)
                    if s < STRIPS - 1:
                        weight_rounded(n, 6 * s + 6)
                        weight_rounded(n, 6 * s + 7)
                hidden_rounded(STRIPS - 1)
                act.wait_ge(S("e_pickt_full"), n + 1)
                act.activation(pickT[:, :], E_SCR[1][:, 0:T], ACT.Copy).then_inc(S("e_pickt"), 1)

            expert_loops(act, expert_block, outputs)
            layer_norm("moe")
            for j in range(6):
                act.wait_ge(*at_count("y_full", j + 1))
                n = TILES[j // 2][1]
                act.activation(xtok[0:n, j // 2, (j % 2) * 512:(j % 2 + 1) * 512], where["y", j][0:n, :], ACT.Copy)\
                   .then_inc(S("y_done"), 1)

        @block.gpsimd
        def _(pool):
            chain = [0]

            def link(ins_):
                chain[0] += 1
                ins_.then_inc(S("pool_chain"), 1)
                pool.wait_ge(S("pool_chain"), chain[0])

            def keep(m, pattern, base, mult, op=ALU.is_ge):
                link(pool.affine_select(out=m, in_=m, compare_op=op, fill=0.0, base=base, pattern=pattern,
                                        channel_multiplier=mult))

            link(pool.memset(ident[:, :], 1.0))
            pool.affine_select(out=ident[:, :], in_=ident[:, :], compare_op=ALU.is_equal, fill=0.0, base=0,
                               pattern=[[-1, P]], channel_multiplier=1).then_inc(S("masks"), 1)
            link(pool.memset(wup[:, :], 0.0))
            pool.memset(aup[:, :], 0.0).then_inc(S("lora_zero"), 1)
            link(pool.memset(state_nat, 0.0))
            pool.memset(PR[:, :, 0:1], 0.0).then_inc(S("pr_zero"), 1)
            for m_ in (ones, utri):
                link(pool.memset(m_[:, :], 1.0))
            keep(utri[:, :], [[1, P]], -1, -1)
            link(pool.memset(bdones[:, :], 0.0))
            for par in range(2):
                rows = slice(64 * par, 64 * par + 64)
                link(pool.memset(bdones[rows, rows], 1.0))
            link(pool.memset(mask_pr[:, :, :], 1.0))
            keep(mask_pr[:, 0, :], [[1, C]], -1, -1)
            keep(mask_pr[:, 1, :], [[1, C]], 0, -1)
            link(pool.memset(reset[:, :], 1.0))
            link(pool.memset(reset[:, 0:T:C], 0.0))
            link(pool.memset(jlt[:, :, :], 1.0))
            keep(jlt[:, :, :], [[1, NE], [-1, NE]], -1, 0)
            link(pool.memset(eps_gn[:, :], GN_EPS))
            link(pool.memset(eps_norm[:, :], NORM_EPS))
            link(pool.iota(slots[:, :], [[1, BLK]], base=0, channel_multiplier=0, allow_small_or_imprecise_dtypes=True))
            link(pool.iota(cand[:, 2, :].rearrange("p (r e) -> p r e", e=NE), [[0, MAX_BLOCKS - 1], [1, NE]], base=0,
                           channel_multiplier=0, allow_small_or_imprecise_dtypes=True))
            link(pool.iota(cand[:, 3, :].rearrange("p (r e) -> p r e", e=NE), [[BLK, MAX_BLOCKS - 1], [0, NE]], base=BLK,
                           channel_multiplier=0, allow_small_or_imprecise_dtypes=True))
            pool.memset(mean[:, :], 1.0).then_inc(S("masks"), 1)
            link(pool.memset(lower[:, :, :], 1.0))
            link(pool.memset(upper[:, :, :], 1.0))
            for par in range(2):
                rows = slice(64 * par, 64 * par + 64)
                for lv in range(LEVELS):
                    L, n = 2 << lv, C >> (lv + 1)
                    lo = lower[rows, lv, :].rearrange("p (n l) -> p n l", l=L)
                    up = upper[rows, lv, :].rearrange("p (n l) -> p n l", l=L)
                    keep(lo, [[-L, n], [0, L]], -(L // 2), 1)
                    keep(lo, [[L, n], [0, L]], L - 1, -1)
                    keep(lo, [[0, n], [-1, L]], L // 2 - 1, 0)
                    keep(up, [[-L, n], [0, L]], 0, 1)
                    keep(up, [[L, n], [0, L]], L // 2 - 1, -1)
                    keep(up, [[0, n], [1, L]], -(L // 2), 0)
            pool.wait_ge(S("pool_chain"), chain[0])
            pool.memset(cand[:, 4, :], 0.0).then_inc(S("masks"), 1)
            pool.wait_ge(*at_count("ab_full", 2 * len(AB_COLS)))
            pool.wait_ge(*at_count("bonus_full", RF))
            for m_ in (Tm, Tt, Xm, At):
                pool.memset(m_[:, :, :, :], 0.0).then_inc(S("zero_blocks"), 1)

        @block.sync
        def _(sp):
            xp = ins["x_prompt"][0]
            sp.dma_start(xst[:, 0, :], xp[0:P, :]).then_inc(S("x_in"), 16)
            sp.dma_start(xst[:, 1, :], xp[P:2 * P, :]).then_inc(S("x_in"), 16)
            sp.dma_start(xst[0:T_SAMPLE, 2, :], ins["x_sample"][0]).then_inc(S("x_in"), 16)

            def load_tile(i):
                src, n, _, _ = tiles[i]
                if i >= DENSE_RING:
                    sp.wait_ge(*at_count("dense_lo", 2 * (i - DENSE_RING) + 2))
                sp.dma_start(tile_of(i)[:, 0:n, :], src).then_inc(S(f"tile_in{i % DENSE_RING}"), 16)

            for i in range(DENSE_RING):
                load_tile(i)
            for table, row, rows, ap in vloads:
                sp.dma_start(vrow[row:row + rows, table, :], ap).then_inc(S("vectors_in"), 16)
            sp.wait_ge(*at_count("lora_zero", 1))
            sp.dma_start(gz_w[:, :, :], w_in[:, GZ0:GZ0 + GR].rearrange("(k p) n -> p k n", p=P)).then_inc(S("small_in"), 16)
            sp.dma_start(router[:, :, :], ins["moe_router"][0].rearrange("(k p) n -> p k n", p=P)).then_inc(S("small_in"), 16)
            sp.dma_start(wup[0:64, :], ins["rwkv_w_up"][0]).then_inc(S("small_in"), 16)
            sp.dma_start(aup[64:P, :], ins["rwkv_a_up"][0]).then_inc(S("small_in"), 16)
            sp.dma_start(gup[:, :], ins["rwkv_g_up"][0]).then_inc(S("small_in"), 16)
            sp.dma_start(gate_up[:, :], ins["gla_gate_up"][0]).then_inc(S("small_in"), 16)
            sp.wait_ge(*at_count("pr_zero", 1))
            for par in range(2):
                rows = slice(64 * par, 64 * par + 64)
                sp.dma_start(state_nat[rows, :, rows],
                             ins["state_rwkv"][0, 0].rearrange("(f a) v k -> a v f k", a=2)[par]).then_inc(S("rwkv_state_in"), 16)
            for i in range(DENSE_RING, OUT_T):
                load_tile(i)
            for g in range(2):
                sp.wait_ge(*at_count("last_rows", g + 1))
                sp.dma_start(outs[3 + 4 * g].rearrange("a b (r w) -> (a b r) w", w=P), lrow[:, g, :]).then_inc(S("stored"), 16)
            for i in range(OUT_T, OUT_T + 4):
                load_tile(i)
            sp.wait_ge(*at_count("gla_s_zero", 2))
            for par in range(2):
                rows = slice(64 * par, 64 * par + 64)
                sp.dma_start(gla["S"][rows, 1, :, par * P:(par + 1) * P],
                             ins["state_gla"][0, 0].rearrange("(f a) d v -> a d f v", a=2)[par]).then_inc(S("gla_state_in"), 16)
            for g in range(2):
                sp.wait_ge(*at_count("hout_done", g + 1))
                for par in range(2):
                    rows = slice(64 * par, 64 * par + 64)
                    sp.dma_start(outs[2 + 4 * g][0, 0].rearrange("(f a) v k -> a v f k", a=2)[par],
                                 Hout[rows, g, :, rows]).then_inc(S("stored"), 16)
            sp.wait_ge(*at_count("gla_s", NCH))
            for g in range(2):
                for par in range(2):
                    rows = slice(64 * par, 64 * par + 64)
                    sp.dma_start(outs[4 + 4 * g][0, 0].rearrange("(f a) d v -> a d f v", a=2)[par],
                                 gla["S"][rows, g, :, par * P:(par + 1) * P]).then_inc(S("gla_stored"), 16)
            sp.wait_ge(*at_count("gla_stored", 64))
            for i in range(OUT_T + 4, OUTC_T + 4):
                load_tile(i)
            sp.wait_ge(*at_count("hgrn_s_zero", 2))
            sp.dma_start(hgrn["S"][:, 1, :, :], ins["state_hgrn"][0, 0].rearrange("h d v -> d h v"))\
              .then_inc(S("hgrn_state_in"), 16)
            sp.wait_ge(*at_count("hgrn_s", NCH))
            for g in range(2):
                sp.dma_start(outs[5 + 4 * g][0, 0].rearrange("h d v -> d h v"), hgrn["S"][:, g, :, :])\
                  .then_inc(S("hgrn_stored"), 16)
            sp.wait_ge(*at_count("hgrn_stored", 32))

            w1, w3, w2 = ins["moe_w1"][0], ins["moe_w3"][0], ins["moe_w2"][0]

            def expert_block(n, e, j_extra):
                for i in range(HALVES):
                    q, h = i // 2, i % 2
                    if isinstance(n, int) and i < MOE_RING:
                        if i == 0:
                            sp.wait_ge(*at_count("dense_lo", 2 * ND))
                        elif i * HALF == DENSE_RING * TILE:
                            sp.wait_ge(*at_count("c_ln", KC))
                    else:
                        sp.wait_ge(S("e_lo"), n * HALVES + i - MOE_RING + 1)
                    buf = moe_ring[:, MOE_RING - 1 - i % MOE_RING, :]
                    if q in DOWN:
                        row = DOWN.index(q) * SC + h * P
                        sp.dma_start(buf.rearrange("p (k n) -> p k n", k=1),
                                     w2[bass.ds(e, 1), row:row + P, :].rearrange("e p n -> p e n"))\
                          .then_inc(S(f"moe_in{i % MOE_RING}"), 16)
                    else:
                        w, s = (w1, UP1.index(q)) if q in UP1 else (w3, UP3.index(q))
                        rows = slice(h * D // 2, (h + 1) * D // 2)
                        sp.dma_start(buf.rearrange("p (k n) -> p k n", k=4),
                                     w[bass.ds(e, 1), rows, s * SC:(s + 1) * SC].rearrange("e (k p) n -> p (e k) n", p=P))\
                          .then_inc(S(f"moe_in{i % MOE_RING}"), 16)

            expert_loops(sp, expert_block, lambda n: None)
            for i in range(3):
                sp.wait_ge(*at_count("y_done", 2 * i + 2))
                dst = outs[0][0][i * P:(i + 1) * P, :] if i < 2 else outs[1][0]
                sp.dma_start(dst, xtok[0:TILES[i][1], i, :]).then_inc(S("stored"), 16)
            sp.wait_ge(*at_count("stored", 16 * (2 + 4 + 3)))


_OUTS = [(1, T_PROMPT, D), (1, T_SAMPLE, D)] + \
        2 * [(1, 1, RH, RN, RN), (1, 1, RPROJ), (1, 1, GH, GDK, GDV), (1, 1, HH, HD, HD)]


def kernel(**inputs):
    import numpy as _np
    import concourse.bacc as _bacc
    from concourse import mybir as _mybir
    from concourse.bass_utils import run_bass_kernel_spmd as _run

    nc = _bacc.Bacc("TRN2", target_bir_lowering=False, num_devices=1)
    arrays, ins, outs = {}, {}, []
    for name, value in inputs.items():
        a = _np.ascontiguousarray(value)
        arrays[f"in_{name}"] = a
        ins[name] = nc.dram_tensor(f"in_{name}", a.shape, _mybir.dt.from_np(a.dtype), kind="ExternalInput").ap()
    for i, shape in enumerate(_OUTS):
        outs.append(nc.dram_tensor(f"out_{i}", shape, _mybir.dt.float32, kind="ExternalOutput").ap())
    mixed_trunk(nc, ins, outs)
    r = _run(nc, [arrays], core_ids=[0])
    return tuple(r.results[0][f"out_{i}"] for i in range(len(_OUTS)))
```
